# Optimizing a Trainium2 kernel written in Bass

```python
import math
import jax, jax.numpy as jnp
from jax import lax
import numpy as np

D_MODEL = 1024
BATCH = 1
SEQ = 256
DEPTH = 1
DEC_BATCH = 8
DEC_SEQ = 4
PAST_LEN = 1024
PAGE_SIZE = 128

SSD_HEADS = 16
SSD_HEAD_DIM = 64
SSD_WIDTH = SSD_HEADS * SSD_HEAD_DIM
SSD_GROUPS = 2
SSD_STATE = 128
SSD_CHUNK = 128
CONV_WIDTH = 4
CONV_CH = SSD_WIDTH + 2 * SSD_GROUPS * SSD_STATE
ATT_HEADS = 8
ATT_HEAD_DIM = 64
ATT_WIDTH = ATT_HEADS * ATT_HEAD_DIM
MOBA_BLOCK = 256
MOBA_TOPK = 3
MOBA_QBLOCK = 32
REL_BUCKETS = 32
REL_MAX_DIST = 128
MIX_WIDTH = SSD_WIDTH + ATT_WIDTH
SPLIT_IDX = [SSD_WIDTH, SSD_WIDTH + CONV_CH, SSD_WIDTH + CONV_CH + SSD_HEADS,
             SSD_WIDTH + CONV_CH + SSD_HEADS + ATT_WIDTH,
             SSD_WIDTH + CONV_CH + SSD_HEADS + 2 * ATT_WIDTH]
IN_PROJ = SSD_WIDTH + CONV_CH + SSD_HEADS + 3 * ATT_WIDTH
MEM_LEN = 256
CA_HEADS = 4
CA_HEAD_DIM = 128
CA_WIDTH = CA_HEADS * CA_HEAD_DIM
FF = 4 * D_MODEL
EPS = 1e-5

kernel_name = 'hymba_ssd_moba_memory_decoder_step'

def rmsnorm(x, w):
    xf = x.astype(jnp.float32)
    y = xf * lax.rsqrt(jnp.mean(xf * xf, axis=-1, keepdims=True) + EPS)
    return (y * w.astype(jnp.float32)).astype(x.dtype)

def causal_conv(xbc, conv_state, w, b):
    L = xbc.shape[1]
    xpad = jnp.concatenate([conv_state.astype(xbc.dtype), xbc], axis=1)
    y = b
    for k in range(CONV_WIDTH):
        y = y + xpad[:, k:k + L] * w[k]
    return jax.nn.silu(y), xpad[:, L:]

def ssd_scan(x, dt, a, bm, cm, s0):
    Bsz, L, H, P = x.shape
    N = bm.shape[-1]
    Q = SSD_CHUNK if L % SSD_CHUNK == 0 else L
    nc = L // Q
    xc = x.reshape(Bsz, nc, Q, H, P)
    dtc = dt.reshape(Bsz, nc, Q, H)
    bc = bm.reshape(Bsz, nc, Q, H, N)
    cc = cm.reshape(Bsz, nc, Q, H, N)
    acum = jnp.cumsum(dtc * a, axis=2)
    causal = jnp.tril(jnp.ones((Q, Q), bool))[None, None, :, :, None]
    seg = acum[:, :, :, None, :] - acum[:, :, None, :, :]
    lmat = jnp.where(causal, jnp.exp(jnp.where(causal, seg, 0.0)), 0.0)
    scores = jnp.einsum('bcihn,bcjhn->bcijh', cc, bc) * lmat
    y_diag = jnp.einsum('bcijh,bcjh,bcjhp->bcihp', scores, dtc, xc)
    decay_end = jnp.exp(acum[:, :, -1:, :] - acum)
    chunk_states = jnp.einsum('bcjhn,bcjh,bcjhp->bchpn', bc, decay_end * dtc, xc)
    chunk_decay = jnp.exp(acum[:, :, -1, :])

    def step(s, inp):
        dec, st = inp
        return dec[:, :, None, None] * s + st, s

    s_final, s_in = lax.scan(step, s0, (jnp.moveaxis(chunk_decay, 1, 0), jnp.moveaxis(chunk_states, 1, 0)))
    s_in = jnp.moveaxis(s_in, 0, 1)
    y_off = jnp.einsum('bcihn,bchpn,bcih->bcihp', cc, s_in, jnp.exp(acum))
    return (y_diag + y_off).reshape(Bsz, L, H, P), s_final

def ssd_branch(z, xbc, dt_raw, conv_state, ssm_state, conv_w, conv_b, dt_bias, a_log, d_skip, norm_w):
    Bsz, L = z.shape[:2]
    gn = SSD_GROUPS * SSD_STATE
    xbc_c, new_conv = causal_conv(xbc, conv_state, conv_w, conv_b)
    xs = xbc_c[..., :SSD_WIDTH].reshape(Bsz, L, SSD_HEADS, SSD_HEAD_DIM).astype(jnp.float32)
    rep = SSD_HEADS // SSD_GROUPS
    bm = jnp.repeat(xbc_c[..., SSD_WIDTH:SSD_WIDTH + gn].reshape(Bsz, L, SSD_GROUPS, SSD_STATE), rep, axis=2)
    cm = jnp.repeat(xbc_c[..., SSD_WIDTH + gn:].reshape(Bsz, L, SSD_GROUPS, SSD_STATE), rep, axis=2)
    dt = jax.nn.softplus(dt_raw.astype(jnp.float32) + dt_bias.astype(jnp.float32))
    a = -jnp.exp(a_log.astype(jnp.float32))
    y, new_ssm = ssd_scan(xs, dt, a, bm.astype(jnp.float32), cm.astype(jnp.float32), ssm_state.astype(jnp.float32))
    y = y + xs * d_skip.astype(jnp.float32)[:, None]
    y = y.reshape(Bsz, L, SSD_WIDTH) * jax.nn.silu(z.astype(jnp.float32))
    y = rmsnorm(y, norm_w)
    return y.astype(z.dtype), new_conv, new_ssm.astype(ssm_state.dtype)

def t5_bucket(rel):
    n = jnp.maximum(rel, 0)
    max_exact = REL_BUCKETS // 2
    nf = jnp.maximum(n, 1).astype(jnp.float32)
    large = max_exact + (jnp.log(nf / max_exact) / math.log(REL_MAX_DIST / max_exact)
                         * (REL_BUCKETS - max_exact)).astype(jnp.int32)
    large = jnp.minimum(large, REL_BUCKETS - 1)
    return jnp.where(n < max_exact, n, large)

def moba_attention(q, k_all, v_all, q_start, rel_bias):
    Bsz, L, H, D = q.shape
    T = k_all.shape[1]
    nb = -(-T // MOBA_BLOCK)
    pad = nb * MOBA_BLOCK - T

    def blocks(t):
        t = jnp.pad(t, ((0, 0), (0, pad), (0, 0), (0, 0)))
        return t.reshape(Bsz, nb, MOBA_BLOCK, H, D).transpose(0, 3, 1, 2, 4)

    kb, vb = blocks(k_all), blocks(v_all)
    kmean = jnp.mean(kb.astype(jnp.float32), axis=3)
    n_top = min(MOBA_TOPK, nb)
    QB = MOBA_QBLOCK if L % MOBA_QBLOCK == 0 else L
    nq = L // QB
    scale = ATT_HEAD_DIM ** -0.5
    b_idx = jnp.arange(Bsz)[:, None, None, None]
    h_idx = jnp.arange(H)[None, :, None, None]
    offs = jnp.arange(MOBA_BLOCK)
    is_own = (jnp.arange(n_top + 1) == n_top)[:, None]

    def attend_block(args):
        qb, pos = args
        own = pos // MOBA_BLOCK
        gate = jnp.einsum('bhqd,bhnd->bhqn', qb.astype(jnp.float32), kmean)
        fully_past = jnp.arange(nb)[None, :] < own[:, None]
        gate = jnp.where(fully_past, gate, -jnp.inf)
        _, top = lax.top_k(gate, n_top)
        own_b = jnp.broadcast_to(own[None, None, :, None], top.shape[:3] + (1,))
        sel = jnp.concatenate([top, own_b], axis=-1)
        k_sel = kb[b_idx, h_idx, sel]
        v_sel = vb[b_idx, h_idx, sel]
        key_pos = sel[..., None] * MOBA_BLOCK + offs
        p5 = pos[None, None, :, None, None]
        allowed = jnp.where(is_own, key_pos <= p5, (sel < own[:, None])[..., None])
        bias = rel_bias[t5_bucket(p5 - key_pos), h_idx[..., None]]
        logits = jnp.einsum('bhqd,bhqskd->bhqsk', qb, k_sel).astype(jnp.float32) * scale + bias.astype(jnp.float32)
        logits = jnp.where(allowed, logits, -jnp.inf)
        probs = jax.nn.softmax(logits.reshape(logits.shape[:3] + (-1,)), axis=-1).reshape(logits.shape)
        return jnp.einsum('bhqsk,bhqskd->bhqd', probs.astype(v_sel.dtype), v_sel)

    qh = jnp.moveaxis(q.transpose(0, 2, 1, 3).reshape(Bsz, H, nq, QB, D), 2, 0)
    pos = (q_start + jnp.arange(L)).reshape(nq, QB)
    out = lax.map(attend_block, (qh, pos))
    return jnp.moveaxis(out, 0, 2).reshape(Bsz, H, L, D).transpose(0, 2, 1, 3).reshape(Bsz, L, H * D)

def memory_kv(mem, norm_w, w_kv):
    Bsz = mem.shape[0]
    kv = rmsnorm(mem, norm_w) @ w_kv
    k, v = jnp.split(kv, 2, axis=-1)
    return (k.reshape(Bsz, MEM_LEN, CA_HEADS, CA_HEAD_DIM), v.reshape(Bsz, MEM_LEN, CA_HEADS, CA_HEAD_DIM))

def cross_attend(hn, mk, mv, w_q, w_o):
    Bsz, L, _ = hn.shape
    q = (hn @ w_q).reshape(Bsz, L, CA_HEADS, CA_HEAD_DIM)
    logits = jnp.einsum('blhd,bmhd->bhlm', q, mk.astype(q.dtype)).astype(jnp.float32) * CA_HEAD_DIM ** -0.5
    p = jax.nn.softmax(logits, axis=-1)
    o = jnp.einsum('bhlm,bmhd->blhd', p.astype(q.dtype), mv.astype(q.dtype)).reshape(Bsz, L, CA_WIDTH)
    return o @ w_o

def trunk_layer(h, l, q_start, conv_state, ssm_state, k_past, v_past, mem_k, mem_v, p):
    Bsz, L, _ = h.shape
    hn = rmsnorm(h, p['norm_mix'][l])
    proj = hn @ p['w_in'][l]
    z, xbc, dt_raw, q, k, v = jnp.split(proj, SPLIT_IDX, axis=-1)
    y_ssd, new_conv, new_ssm = ssd_branch(z, xbc, dt_raw, conv_state, ssm_state, p['conv_w'][l], p['conv_b'][l],
                                          p['dt_bias'][l], p['a_log'][l], p['d_skip'][l], p['ssd_norm'][l])
    q = q.reshape(Bsz, L, ATT_HEADS, ATT_HEAD_DIM)
    k = k.reshape(Bsz, L, ATT_HEADS, ATT_HEAD_DIM)
    v = v.reshape(Bsz, L, ATT_HEADS, ATT_HEAD_DIM)
    if k_past is None:
        k_all, v_all = k, v
    else:
        k_all = jnp.concatenate([k_past.astype(k.dtype), k], axis=1)
        v_all = jnp.concatenate([v_past.astype(v.dtype), v], axis=1)
    y_att = moba_attention(q, k_all, v_all, q_start, p['rel_bias'])
    h = h + jnp.concatenate([y_ssd, y_att], axis=-1) @ p['w_out'][l]
    h = h + cross_attend(rmsnorm(h, p['norm_ca'][l]), mem_k, mem_v, p['w_ca_q'][l], p['w_ca_o'][l])
    hn = rmsnorm(h, p['norm_mlp'][l])
    h = h + jnp.square(jax.nn.relu(hn @ p['w_up'][l])) @ p['w_down'][l]
    return h, new_conv, new_ssm, k, v

def gather_pages(pool, page_table):
    g = pool[page_table]
    return g.reshape(g.shape[0], -1, g.shape[3], g.shape[4])

def setup_inputs(seed: int = 0) -> dict:
    key = jax.random.key(seed)
    ks = jax.random.split(key, 32)
    f32 = jnp.float32
    n_pages = PAST_LEN // PAGE_SIZE
    n_phys = (5 * DEC_BATCH * n_pages) // 4

    def nrm(k, shape, scale=1.0):
        return jax.random.normal(k, shape, f32) * scale

    def gain(k, shape):
        return 1.0 + 0.02 * jax.random.normal(k, shape, f32)

    page_table = jax.random.permutation(ks[0], n_phys)[:DEC_BATCH * n_pages].reshape(DEC_BATCH, n_pages).astype(jnp.int32)
    dt0 = jnp.exp(jax.random.uniform(ks[1], (DEPTH, SSD_HEADS), f32, math.log(1e-3), math.log(1e-1)))
    dt_bias = dt0 + jnp.log(-jnp.expm1(-dt0))
    a_log = jnp.log(jax.random.uniform(ks[2], (DEPTH, SSD_HEADS), f32, 1.0, 16.0))
    return {
        'x_prompt': nrm(ks[3], (BATCH, SEQ, D_MODEL)),
        'x_sample': nrm(ks[4], (DEC_BATCH, DEC_SEQ, D_MODEL)),
        'cache_k': nrm(ks[5], (DEPTH, n_phys, PAGE_SIZE, ATT_HEADS, ATT_HEAD_DIM)),
        'cache_v': nrm(ks[6], (DEPTH, n_phys, PAGE_SIZE, ATT_HEADS, ATT_HEAD_DIM)),
        'cache_mem_k': nrm(ks[7], (DEPTH, DEC_BATCH, MEM_LEN, CA_HEADS, CA_HEAD_DIM)),
        'cache_mem_v': nrm(ks[8], (DEPTH, DEC_BATCH, MEM_LEN, CA_HEADS, CA_HEAD_DIM)),
        'state_conv': nrm(ks[9], (DEPTH, DEC_BATCH, CONV_WIDTH - 1, CONV_CH)),
        'state_ssm': nrm(ks[10], (DEPTH, DEC_BATCH, SSD_HEADS, SSD_HEAD_DIM, SSD_STATE), 0.1),
        'page_table': page_table,
        'mem_prompt': nrm(ks[11], (BATCH, MEM_LEN, D_MODEL)),
        'norm_mix': gain(ks[12], (DEPTH, D_MODEL)),
        'w_in': nrm(ks[13], (DEPTH, D_MODEL, IN_PROJ), D_MODEL ** -0.5),
        'conv_w': nrm(ks[14], (DEPTH, CONV_WIDTH, CONV_CH), CONV_WIDTH ** -0.5),
        'conv_b': nrm(ks[15], (DEPTH, CONV_CH), 0.02),
        'dt_bias': dt_bias,
        'a_log': a_log,
        'd_skip': gain(ks[16], (DEPTH, SSD_HEADS)),
        'ssd_norm': gain(ks[17], (DEPTH, SSD_WIDTH)),
        'rel_bias': nrm(ks[18], (REL_BUCKETS, ATT_HEADS), 0.5),
        'w_out': nrm(ks[19], (DEPTH, MIX_WIDTH, D_MODEL), MIX_WIDTH ** -0.5),
        'norm_ca': gain(ks[20], (DEPTH, D_MODEL)),
        'norm_mem': gain(ks[21], (DEPTH, D_MODEL)),
        'w_ca_q': nrm(ks[22], (DEPTH, D_MODEL, CA_WIDTH), D_MODEL ** -0.5),
        'w_ca_kv': nrm(ks[23], (DEPTH, D_MODEL, 2 * CA_WIDTH), D_MODEL ** -0.5),
        'w_ca_o': nrm(ks[24], (DEPTH, CA_WIDTH, D_MODEL), CA_WIDTH ** -0.5),
        'norm_mlp': gain(ks[25], (DEPTH, D_MODEL)),
        'w_up': nrm(ks[26], (DEPTH, D_MODEL, FF), D_MODEL ** -0.5),
        'w_down': nrm(ks[27], (DEPTH, FF, D_MODEL), FF ** -0.5),
        'norm_final': gain(ks[28], (D_MODEL,)),
    }

def reference(x_prompt, x_sample, cache_k, cache_v, cache_mem_k, cache_mem_v, state_conv, state_ssm,
              page_table, mem_prompt, norm_mix, w_in, conv_w, conv_b, dt_bias, a_log, d_skip, ssd_norm,
              rel_bias, w_out, norm_ca, norm_mem, w_ca_q, w_ca_kv, w_ca_o, norm_mlp, w_up, w_down, norm_final):
    p = {'norm_mix': norm_mix, 'w_in': w_in, 'conv_w': conv_w, 'conv_b': conv_b, 'dt_bias': dt_bias,
         'a_log': a_log, 'd_skip': d_skip, 'ssd_norm': ssd_norm, 'rel_bias': rel_bias, 'w_out': w_out,
         'norm_ca': norm_ca, 'w_ca_q': w_ca_q, 'w_ca_o': w_ca_o, 'norm_mlp': norm_mlp,
         'w_up': w_up, 'w_down': w_down}
    past_len = page_table.shape[1] * cache_k.shape[2]

    pb = x_prompt.shape[0]
    zero_conv = jnp.zeros((pb, CONV_WIDTH - 1, CONV_CH), x_prompt.dtype)
    zero_ssm = jnp.zeros((pb, SSD_HEADS, SSD_HEAD_DIM, SSD_STATE), jnp.float32)
    h = x_prompt
    pk, pv, pmk, pmv, pconv, pssm = [], [], [], [], [], []
    for l in range(DEPTH):
        mk, mv = memory_kv(mem_prompt, norm_mem[l], w_ca_kv[l])
        h, c, s, k, v = trunk_layer(h, l, 0, zero_conv, zero_ssm, None, None, mk, mv, p)
        pk.append(k); pv.append(v); pmk.append(mk); pmv.append(mv); pconv.append(c); pssm.append(s)
    y_prompt = rmsnorm(h, norm_final)

    g = x_sample
    sk, sv, sconv, sssm = [], [], [], []
    for l in range(DEPTH):
        k_past = gather_pages(cache_k[l], page_table)
        v_past = gather_pages(cache_v[l], page_table)
        g, c, s, k, v = trunk_layer(g, l, past_len, state_conv[l], state_ssm[l], k_past, v_past,
                                    cache_mem_k[l], cache_mem_v[l], p)
        sk.append(k); sv.append(v); sconv.append(c); sssm.append(s)
    y_sample = rmsnorm(g, norm_final)

    return (y_prompt, y_sample, jnp.stack(pk), jnp.stack(pv), jnp.stack(pmk), jnp.stack(pmv),
            jnp.stack(pconv), jnp.stack(pssm), jnp.stack(sk), jnp.stack(sv), jnp.stack(sconv), jnp.stack(sssm))


_drawn_inputs = setup_inputs


def setup_inputs(seed=0):
    import zlib

    import numpy as np

    out = dict(_drawn_inputs(seed))
    spreads = {}
    factors = {'d_skip': 5.543,
     'ssd_norm': 4.15,
     'norm_ca': 8.0,
     'norm_mem': 2.743,
     'norm_mlp': 3.544,
     'norm_final': 7.446,
     'cache_k': 4.754,
     'cache_v': 3.799}
    for name, (base, spread) in spreads.items():
        noise = np.random.default_rng([zlib.crc32(name.encode()), seed]).standard_normal(out[name].shape)
        drawn = base * np.exp(spread * noise) if base else spread * noise
        out[name] = __import__('jax').numpy.asarray(drawn.astype(out[name].dtype))
    for name, factor in factors.items():
        out[name] = (out[name] * factor).astype(out[name].dtype)
    return out
```

```python
import math
from contextlib import ExitStack

import numpy as np

import concourse.bass as bass
from concourse import mybir

F32 = mybir.dt.float32
I32 = mybir.dt.int32
ALU = mybir.AluOpType
ACT = mybir.ActivationFunctionType
AX = mybir.AxisListType
ds = bass.ds

P = 128
D = 1024
DT = D // P
NP_ = 256
NB, NI = 8, 4
NS = NB * NI
T = NP_ + NS
H, DH = 8, 64
PAIRS = H // 2
SH, SP_, SN = 16, 64, 128
CW = 4
XT = 12
CROSS = 4
MEM = 256
FT = 32
PAST = 1024
PAGE = 128
NPAGE = PAST // PAGE
BUCKETS, MAXD = 32, 128
EPS = 1e-5
NEG = -1e30
SLOTS = 4
G = 2
GB = NB // G
XPAD = CW - 1 + NP_ + NB * (CW - 1 + NI)
XS = CW - 1 + NP_
IN_Z, IN_X, IN_DT, IN_Q, IN_K, IN_V = 0, 1024, 2560, 2576, 3088, 3600
TOKS = [(0, 128), (128, 128), (256, 32)]
TURN_BANKS = [2, 3, 6]

VEC, at = {}, 0
for _name, _rows in (("norm_mix", 8), ("norm_ca", 8), ("norm_mem", 8), ("norm_mlp", 8), ("ssd_norm", 8),
                     ("conv_b", 12), ("conv_w", 48)):
    VEC[_name] = at
    at += _rows
VROWS = at


def bucket(n):
    half = BUCKETS // 2
    if n < half:
        return n
    return min(BUCKETS - 1, half + int(math.log(n / half) / math.log(MAXD / half) * (BUCKETS - half)))


def constants():
    f = np.float32
    k, j = np.arange(P)[:, None], np.arange(P)[None, :]
    c = {"ident": np.eye(P, dtype=f), "later": (k > j).astype(f), "upto": (k <= j).astype(f)}
    ks, js = np.arange(NS)[:, None], np.arange(NS)[None, :]
    same = ks // NI == js // NI
    c["later_s"] = (same & (ks > js)).astype(f)
    c["upto_s"] = (same & (ks <= js)).astype(f)
    c["batch_of"] = (ks // NI == np.arange(NB)[None, :]).astype(f)
    oh = np.zeros((NI, BUCKETS, PAST + NS), f)
    for i in range(NI):
        for key in range(PAST):
            oh[i, bucket(PAST + i - key), key] = 1
        for tok in range(NS):
            if i >= tok % NI:
                oh[i, bucket(i - tok % NI), PAST + tok] = 1
    c["onehot_s"] = oh.reshape(P, PAST + NS)
    c["step_of"] = (np.arange(P)[:, None] // BUCKETS == np.arange(NI)[None, :]).astype(f)
    oh = np.zeros((BUCKETS, 512), f)
    m = np.zeros((H, 512), f)
    for r in range(512):
        if r >= 255:
            oh[bucket(r - 255), r] = 1
        else:
            m[:, r] = NEG
    c["onehot_p"], c["mask_p"] = oh, m
    row = np.arange(P)
    b4, i = row // 32, row % NI
    own = np.full((P, G, NS), NEG, f)
    for g in range(G):
        for tok in range(NS):
            own[(g * GB + b4 == tok // NI) & (tok % NI <= i), g, tok] = 0
    c["mask_own"] = own.reshape(P, G * NS)
    c["place"] = np.tile(np.arange(1, 5, dtype=f)[None], (P, 1))
    h = np.arange(SH)[:, None]
    c["head_rows"] = (h % 2 == np.arange(P)[None, :] // 64).astype(f)
    c["pair_of"] = (h // 2 == np.arange(DT)[None, :]).astype(f)
    return c


def make_plan():
    seq = []

    def pair(kind, n, chunks):
        seq.append(("pair", kind, n, chunks))

    def unit(*a):
        seq.append(("unit",) + a)

    pair("qk", 0, 1)
    seq.append(("ss", 0))
    for n in range(1, 4):
        pair("qk", n, 1)
    unit("K", 0, 0)
    for n in range(2):
        pair("v", n, 1)
    unit("K", 0, 1)
    seq.append(("kvtok",))
    pair("z", 0, 1), pair("z", 1, 1)
    unit("K", 0, 2)
    pair("z", 2, 1), pair("z", 3, 1)
    unit("K", 0, 3)
    seq.append(("own", 0))
    pair("x", 0, 1), pair("x", 1, 1)
    unit("K", 1, 0)
    pair("x", 2, 1)
    unit("K", 1, 1)
    seq.append(("probs", 0))
    pair("x", 3, 1)
    unit("K", 1, 2)
    pair("x", 4, 1)
    unit("K", 1, 3)
    seq.append(("own", 1))
    pair("x", 5, 1)
    seq.append(("dt",))
    unit("V", 0, 0)
    seq.append(("ss", 1))
    pair("m", 0, 1)
    unit("V", 0, 1)
    pair("m", 1, 1)
    unit("V", 0, 2)
    unit("V", 0, 3)
    seq.append(("pvend", 0))
    pair("m", 2, 1)
    seq.append(("probs", 1))
    unit("V", 1, 0)
    pair("m", 3, 1)
    unit("V", 1, 1)
    seq.append(("mtok",))
    unit("V", 1, 2)
    unit("V", 1, 3)
    seq.append(("pvend", 1))
    seq.append(("ssd",))
    seq.append(("prompt_self",))
    seq.append(("ss", 2))
    for n in range(4):
        pair("out", n, 2)
    pair("caq", 0, 1)
    seq.append(("ss", 3))
    pair("caq", 1, 1)
    unit("MK", 0)
    unit("MK", 1)
    seq.append(("prompt_cross",))
    for g in range(2):
        seq.append(("probs", 2 + g))
        unit("MV", g)
        seq.append(("pvend", 2 + g))
    for n in range(4):
        pair("cao", n, 1)
    seq.append(("ss", 4))
    return seq


SEQ = make_plan()
BLOCK, TILE, UNIT, TURN = {}, {}, {}, {}
USED = {}
for s in SEQ:
    if s[0] == "pair":
        for c in range(s[3]):
            if c < s[3] - 1:
                USED[s[1:3] + (c,)] = len(USED)
            BLOCK[s[1:3] + (c,)] = len(BLOCK)
        for h in range(2):
            TILE[s[1:3] + (h,)] = len(TILE)
    elif s[0] == "dt":
        TILE["dt"] = len(TILE)
    elif s[0] == "unit" and s[1] in ("K", "V"):
        UNIT[s[1:]] = len(UNIT)
    elif s[0] == "ssd":
        for h in range(2):
            UNIT[("ST", h)] = len(UNIT)
    elif s[0] == "unit":
        UNIT[s[1:]] = len(UNIT)
N_BLOCKS, N_TILES, N_USED = len(BLOCK), len(TILE), len(USED)


def turn(key):
    TURN[key] = len(TURN)


def plan_turns():
    turn("vec")
    for c in range(DT):
        turn(("x", c))
    for c in range(DT):
        turn(("mem", c))
    turn("conv")
    for s in SEQ:
        if s[0] == "unit" and s[1] in ("K", "MK"):
            for c in range(4):
                turn((s[1:], c, 0)), turn((s[1:], c, 1))
        elif s[0] == "ss":
            turn(("ss", s[1]))
        elif s[0] == "kvtok":
            for g in range(3):
                turn(("ktok", g)), turn(("vtok", g))
        elif s[0] == "mtok":
            for g in range(2):
                turn(("mktok", g)), turn(("mvtok", g))
        elif s[0] == "own":
            turn(("own", s[1]))
        elif s[0] == "probs":
            turn(("probs", s[1], 0))
            if s[1] < 2:
                turn(("probs", s[1], 1)), turn(("probs", s[1], 2))
        elif s[0] == "pvend":
            turn(("ohead", s[1]))
        elif s[0] == "ssd":
            for i in range(3):
                turn(("cvout", i))
            for q in range(3):
                turn(("dt", q))
                turn(("xtok", q, 0)), turn(("xtok", q, 1)), turn(("btok", q))
                if q < 2:
                    for hg in range(4):
                        turn(("y", q, hg))
                    turn(("st", q, 0)), turn(("st", q, 1))
                else:
                    for bi in range(GB):
                        for bh in range(G):
                            for g in range(2):
                                turn(("ss", bi, bh, g))
                    turn(("yd", 0)), turn(("yd", 1))
                    turn("ys")
            turn(("sf", 0)), turn(("sf", 1))
        elif s[0] in ("prompt_self", "prompt_cross"):
            for h in range(H if s[0] == "prompt_self" else CROSS):
                turn((s[0], h))
    for g in range(3):
        for h in range(2):
            turn(("fin", g, h))


plan_turns()
STEP = {}
for s in SEQ:
    if s[0] == "unit" and s[1] in ("K", "MK"):
        for c in range(4):
            STEP[(s[1:], c)] = len(STEP)
UP0, DOWN0 = N_TILES, N_TILES + FT
BLOCKS, UNITS = list(BLOCK), list(UNIT)
KV_DMAS = [8 if u[0] in ("K", "V") else GB for u in UNITS]
V_ORDER = {u: i for i, u in enumerate([u for u in UNITS if u[0] in ("V", "MV")])}
K_TILES = {"qk": 8, "v": 8, "z": 8, "x": 8, "m": 8, "out": 6, "caq": 8, "cao": 4}


def build(nc, I, O, scratch):
    ctx = ExitStack()
    with ctx:
        def sb(name, shape, dt=F32):
            return ctx.enter_context(nc.sbuf_tensor(name, shape, dt))

        def sem(name):
            return ctx.enter_context(nc.semaphore(name))

        ps = ctx.enter_context(nc.psum_tensor("ps", [P, 8, 512], F32))

        ident = sb("ident", [P, P])
        later, upto, ones = sb("later", [P, P]), sb("upto", [P, P]), sb("ones", [P, P])
        later_s, upto_s = sb("later_s", [NS, NS]), sb("upto_s", [NS, NS])
        batch_of, step_of = sb("batch_of", [NS, NB]), sb("step_of", [P, NI])
        place, mask_own = sb("place", [P, 4]), sb("mask_own", [P, G * NS])
        head_rows, pair_of = sb("head_rows", [SH, P]), sb("pair_of", [SH, DT])
        vec_rows, vec = sb("vec_rows", [VROWS, P]), sb("vec", [P, VROWS])
        hcol = sb("hcol", [SH, 4])
        pages = sb("pages", [1, NB * NPAGE], I32)
        rb4 = sb("rb4", [P, H])
        small = sb("small", [P, 96])
        eps_t = sb("eps_t", [P, 1])

        wring = sb("wring", [P, SLOTS, 2048])
        wdt = sb("wdt", [P, DT, SH])
        big = sb("big", [P, 2 * 4096 + DT * T])
        kvring = big[:, 0:8192].rearrange("p (s b c n) -> p s b c n", s=2, b=GB, c=2)
        z = big[:, 8192:8192 + DT * T].rearrange("p (c t) -> p c t", c=DT)
        ff = big[:, 0:FT * T]

        hT, hw = sb("hT", [P, DT * T]), sb("hw", [P, DT, T])
        h3 = hT[:, :].rearrange("p (c t) -> p c t", c=DT)
        xc = sb("xc", [P, XT, T])
        qz = sb("qz", [P, 2, PAIRS, NP_])
        kT = sb("kT", [P, PAIRS, T])
        vtok = sb("vtok", [P, 3, 512])
        attT = sb("attT", [P, 4, T])
        mkv = sb("mkv", [P, 2048])
        memkT = mkv[:, 0:1024].rearrange("p (c t) -> p c t", c=4)
        memvtok = mkv[:, 1024:2048].rearrange("p (c t) -> p c t", c=2)
        qs = sb("qs", [P, 4, NB, 32])
        sq, acc, rstd = sb("sq", [P, 2, T]), sb("acc", [P, 2, T]), sb("rstd", [P, T])
        rmem = sb("rmem", [P, NP_])
        vv = sb("vv", [P, T])
        T_FREE = 13200
        tmp = sb("tmp", [P, T_FREE])

        at = [0]

        def part(n):
            a = tmp[:, at[0]:at[0] + n]
            at[0] += n
            assert at[0] <= T_FREE, at[0]
            return a

        xpad = part(XT * XPAD).rearrange("p (c t) -> p c t", c=XT)
        ssd_at = at[0]
        memw = part(DT * NP_).rearrange("p (c t) -> p c t", c=DT)
        vT = part(PAIRS * T).rearrange("p (c t) -> p c t", c=PAIRS)
        KT_ = part(2 * 1024).rearrange("p (s b t) -> p s b t", s=2, b=GB)
        logit = part(PAST + NS)
        biasS = part(PAST + NS)
        PT = part(9 * P).rearrange("p (c t) -> p c t", c=9)
        osb = part(512)
        ctmp = part(XPAD)
        stage = xc[:, :, :].rearrange("p c t -> p (c t)")[:, 0:1024].rearrange("p (s t) -> p s t", s=2)
        mstage = hw[:, :, :].rearrange("p c t -> p (c t)")[:, 6 * T:6 * T + 512]
        xin = xc[:, :, :].rearrange("p c t -> p (c t)")[:, 0:3072].rearrange("p (g n) -> p g n", g=3)
        memin = big[:, 8192:8192 + 2048].rearrange("p (g n) -> p g n", g=2)
        cvin = mkv[0:NB * 3, 0:1536]
        at[0] = ssd_at
        xtok, xwt = part(1024), part(1024)
        btok = part(256)
        rhs4 = part(1024).rearrange("p (s t) -> p s t", s=2)
        E4 = part(1024).rearrange("p (s t) -> p s t", s=2)
        M4 = part(1024).rearrange("p (s t) -> p s t", s=2)
        CS = part(1024).rearrange("p (s t) -> p s t", s=2)
        ybuf = part(2 * 256).rearrange("p (s t) -> p s t", s=2)
        st01 = part(2048)
        st0, st1 = st01[:, 0:1024], st01[:, 1024:2048]
        Gm = part(256)
        ohT = sb("ohT", [P, 512])
        ebuf = ohT[:, :]
        bbd = tmp[:, 0:2048].rearrange("p (g b n) -> p g b n", g=2, b=NB)
        cz = tmp[:, 2048:2560].rearrange("p (g b n) -> p g b n", g=2, b=NB)
        dts = hw[0:SH, 0:6, :]
        sums = sb("sums", [SH, NB + 1])
        psums = sb("psums", [SH, DT, NB + 1])
        dec = sb("dec", [P, DT, NB + 1])
        dtok = sb("dtok", [P, 32])
        ex = sb("ex", [P, 48])
        at[0] = 0
        biasP = part(2 * H * 256).rearrange("p (q h k) -> p q h k", q=2, h=H)
        PL = part(2 * 512).rearrange("p (s q k) -> p s q k", s=2, q=2)
        PTp = part(2 * 512).rearrange("p (s m q) -> p s m q", s=2, m=2)
        mx = sb("mx", [P, 2, 8])
        at[0] = 4096 + 2048
        logit_x = part(512).rearrange("p (g t) -> p g t", g=2)
        fnorm = part(1024)
        ytok = tmp[:, 0:2048].rearrange("p (s t) -> p s t", s=2)
        yout = tmp[:, 2048:4096].rearrange("p (s t) -> p s t", s=2)
        xKT = part(2 * 1024).rearrange("p (s b t) -> p s b t", s=2, b=GB)
        xPT = part(2 * P).rearrange("p (c t) -> p c t", c=2)
        xosb = part(512)
        rb_tab = sb("rb_tab", [BUCKETS, H])

        oh_s = big[:, 0:PAST + NS]
        oh_p = wring[0:BUCKETS, 3, 0:512]
        mask_p = wring[0:H, 3, 512:1024]
        rb_row = wring[0:H, 3, 1024:1536]
        rbx = wring[:, 3, 1536:1664]

        cg = ebuf[:, 0:XT * 27].rearrange("p (c r) -> p c r", c=XT)
        cvo = st01[0:27, 0:XT * P]
        ysb, yo = CS[0:NS, :, :].rearrange("p s t -> p (s t)"), st01[0:NS, 0:1024]
        ssT = [rhs4[:, 1, :], E4[:, 1, :], M4[:, 1, :], ebuf]
        sfo = M4[:, :, :].rearrange("p s t -> p (s t)")
        own_raw = sb("own_raw", [P, NS])

        def sm(s, a, b):
            return small[:, 24 * s + a:24 * s + b]

        x_in, ident_in, vec_in, const_in = sem("x_in"), sem("ident_in"), sem("vec_in"), sem("const_in")
        mem_in, cv_in, tab_in, pages_in = sem("mem_in"), sem("cv_in"), sem("tab_in"), sem("pages_in")
        dtw_in, bias_in, fnorm_in = sem("dtw_in"), sem("bias_in"), sem("fnorm_in")
        landed = [sem(f"landed{i}") for i in range(SLOTS)]
        kv_in = [sem(f"kv_in{i}") for i in range(2)]
        dense_ps, dense_out = sem("dense_ps"), sem("dense_out")
        chunk_used = sem("chunk_used")
        turn_ps, turn_act, turn_dve = sem("turn_ps"), sem("turn_act"), sem("turn_dve")
        sq_done, acc_done, root_done, rstd_done = sem("sq_done"), sem("acc_done"), sem("root_done"), sem("rstd_done")
        hw_done, memw_done, zeros_made, qs_clear = sem("hw_done"), sem("memw_done"), sem("zeros_made"), sem("qs_clear")
        rbx_made, tab_ps, tab_made, rb_out = sem("rbx_made"), sem("tab_ps"), sem("tab_made"), sem("rb_out")
        conv_done, silu_done = sem("conv_done"), sem("silu_done")
        kt_used, scores_used = sem("kt_used"), sem("scores_used")
        bounds_made, row_exp = sem("bounds_made"), sem("row_exp")
        v_used, pv_ps, pv_out, heads_out = sem("v_used"), sem("pv_ps"), sem("pv_out"), sem("heads_out")
        dve_step, act_step, pool_step = sem("dve_step"), sem("act_step"), sem("pool_step")
        phase, stores, cv_out, st_out, y0_out = sem("phase"), sem("stores"), sem("cv_out"), sem("st_out"), sem("y0_out")
        kst_out = [sem(f"kst_out{i}") for i in range(5)]
        dt_abs, dt_exp, dt_done, alog_exp = sem("dt_abs"), sem("dt_exp"), sem("dt_done"), sem("alog_exp")
        cg_made, dec_ps, dec_exp = sem("cg_made"), sem("dec_ps"), sem("dec_exp")
        sums_ps, sums_exp, g_ps, gm_made, xw_made = sem("sums_ps"), sem("sums_exp"), sem("g_ps"), sem("gm_made"), sem("xw_made")
        rhs_made, seg_ps, seg_exp, mix_made = sem("rhs_made"), sem("seg_ps"), sem("seg_exp"), sem("mix_made")
        acb_ps, acb_exp, cs_made = sem("acb_ps"), sem("acb_exp"), sem("cs_made")
        y_used, state_made, xw_clear, cz_made = sem("y_used"), sem("state_made"), sem("xw_clear"), sem("cz_made")
        bbd_made, yoff_ps, ys_made, up_ps, up_done = sem("bbd_made"), sem("yoff_ps"), sem("ys_made"), sem("up_ps"), sem("up_done")
        z_ready, z_normed, ssT_used = sem("z_ready"), sem("z_normed"), sem("ssT_used")
        p_scores, p_bound, p_exp, p_probs = sem("p_scores"), sem("p_bound"), sem("p_exp"), sem("p_probs")
        p_pv, p_out = sem("p_pv"), sem("p_out")
        ff_done, fin_root, fin_out = sem("ff_done"), sem("fin_root"), sem("fin_out")

        def bank(key):
            return TURN_BANKS[TURN[key] % len(TURN_BANKS)]

        def turned(e, key):
            u = TURN[key]
            e.wait_ge(turn_dve if u % 2 else turn_act, u // 2 + 1)

        def bank_free(e, key):
            u = TURN[key] - len(TURN_BANKS)
            if u >= 0:
                e.wait_ge(turn_dve if u % 2 else turn_act, u // 2 + 1)

        def in_ps(e, key):
            e.wait_ge(turn_ps, TURN[key] + 1)

        def kv_ready(e, unit):
            n = UNIT[unit]
            e.wait_ge(kv_in[n % 2], sum(KV_DMAS[m] * 16 for m in range(n % 2, n + 1, 2)))

        def block_ready(e, key):
            g = BLOCK[key]
            e.wait_ge(landed[g % SLOTS], 16 * (g // SLOTS + 1))

        def tile_done(e, key):
            e.wait_ge(dense_out, TILE[key] + 1)

        def meet(e, n):
            e.drain().then_inc(phase, 1)
            e.wait_ge(phase, 4 * n)

        w_in, w_kv = I["w_in"], I["w_ca_kv"]

        def block_source(kind, n, c):
            w, col = {"qk": (w_in, IN_Q), "v": (w_in, IN_V), "z": (w_in, IN_Z), "x": (w_in, IN_X),
                      "m": (w_kv, 0), "out": (I["w_out"], 0), "caq": (I["w_ca_q"], 0),
                      "cao": (I["w_ca_o"], 0)}[kind]
            k = K_TILES[kind]
            return w[c * k * P:(c + 1) * k * P, col + 256 * n:col + 256 * (n + 1)].rearrange("(k p) n -> p k n", p=P)

        block = ctx.enter_context(nc.Block())

        @block.sync
        def _(sp):
            def load_block(key):
                g = BLOCK[key]
                if g >= SLOTS:
                    old = BLOCKS[g - SLOTS]
                    if old in USED:
                        sp.wait_ge(chunk_used, USED[old] + 1)
                    else:
                        sp.wait_ge(dense_ps, TILE[old[:2] + (1,)] + 1)
                k = K_TILES[key[0]]
                sp.dma_start(wring[:, g % SLOTS, 0:k * 256].rearrange("p (k n) -> p k n", k=k),
                             block_source(*key)).then_inc(landed[g % SLOTS], 16)

            def slot_free(n):
                if n < 2:
                    return
                old = UNITS[n - 2]
                if old[0] in ("K", "MK"):
                    sp.wait_ge(turn_ps, TURN[(old, 3, 1)] + 1)
                elif old[0] in ("V", "MV"):
                    sp.wait_ge(v_used, V_ORDER[old] + 1)
                else:
                    sp.wait_ge(st_out, 128)

            def load_unit(u):
                n = UNIT[u]
                slot_free(n)
                dst = kvring[:, n % 2]
                if u[0] in ("K", "V"):
                    cache = I["cache_k"] if u[0] == "K" else I["cache_v"]
                    first = (u[1] * 4 + u[2]) * 8
                    with sp.Fori(0, 8) as i:
                        page = sp.value_load(pages[0:1, ds(i + first, 1)], min_val=0, max_val=cache.shape[0] - 1)
                        sp.dma_start(big[:, ds(i * 512 + (n % 2) * 4096, 512)],
                                     cache[ds(page, 1)].rearrange("o p n -> p (o n)")).then_inc(kv_in[n % 2], 16)
                elif u[0] in ("MK", "MV"):
                    cache = I["cache_mem_k"] if u[0] == "MK" else I["cache_mem_v"]
                    for b in range(GB):
                        sp.dma_start(dst[:, b], cache[u[1] * GB + b].rearrange("(c p) n -> p c n", p=P))\
                            .then_inc(kv_in[n % 2], 16)
                else:
                    for b in range(GB):
                        sp.dma_start(dst[:, b].rearrange("p a (c n) -> p (a c) n", n=SN),
                                     I["state_ssm"][u[1] * GB + b].rearrange("(c p) n -> p c n", p=P))\
                            .then_inc(kv_in[n % 2], 16)

            sp.dma_start(xin[:, 0:2, :], I["x_prompt"].rearrange("(g p) n -> p g n", p=P)).then_inc(x_in, 16)
            sp.dma_start(xin[0:NS, 2, :], I["x_sample"]).then_inc(x_in, 16)
            sp.dma_start(ident[:, :], I["ident"]).then_inc(ident_in, 16)
            for name in ("norm_mix", "norm_ca", "norm_mem", "norm_mlp", "ssd_norm", "conv_b", "conv_w"):
                rows = I[name].rearrange("(r n) -> r n", n=P)
                sp.dma_start(vec_rows[VEC[name]:VEC[name] + rows.shape[0], :], rows).then_inc(vec_in, 16)
            load_block(BLOCKS[0])
            sp.dma_start(rb4[:, :], bass.AP(I["rel_bias"].tensor, 0, [[0, NI], [H, BUCKETS], [1, H]])).then_inc(tab_in, 16)
            sp.dma_start(rb_tab[:, :], I["rel_bias"]).then_inc(tab_in, 16)
            sp.dma_start(step_of[:, :], I["step_of"]).then_inc(tab_in, 16)
            sp.dma_start(oh_s, I["onehot_s"]).then_inc(tab_in, 16)
            sp.dma_start(oh_p, I["onehot_p"]).then_inc(tab_in, 16)
            sp.dma_start(mask_p, I["mask_p"]).then_inc(tab_in, 16)
            sp.dma_start(memin, I["mem_prompt"].rearrange("(g p) n -> p g n", p=P)).then_inc(mem_in, 16)
            sp.dma_start(cvin, I["state_conv"]).then_inc(cv_in, 16)
            load_block(BLOCKS[1])
            load_block(BLOCKS[2])
            sp.dma_start(pages[0:1, :].rearrange("o (k b w) -> o k b w", k=8, b=GB)[:, 0:4],
                         I["page_table"][0:GB].rearrange("b (k w) -> k b w", w=2).unsqueeze(0)).then_inc(pages_in, 16)
            sp.dma_start(pages[0:1, :].rearrange("o (k b w) -> o k b w", k=8, b=GB)[:, 4:8],
                         I["page_table"][GB:NB].rearrange("b (k w) -> k b w", w=2).unsqueeze(0)).then_inc(pages_in, 16)
            for dst, name in ((later, "later"), (upto, "upto"), (later_s, "later_s"), (upto_s, "upto_s"),
                              (batch_of, "batch_of"), (place, "place"), (mask_own, "mask_own"),
                              (head_rows, "head_rows"), (pair_of, "pair_of")):
                sp.dma_start(dst[:, :], I[name]).then_inc(const_in, 16)
            for i, name in enumerate(("dt_bias", "a_log", "d_skip")):
                sp.dma_start(hcol[:, i:i + 1], I[name].rearrange("(h o) -> h o", o=1)).then_inc(const_in, 16)
            sp.dma_start(wdt[:, :, :], w_in[:, IN_DT:IN_DT + SH].rearrange("(k p) n -> p k n", p=P)).then_inc(dtw_in, 16)
            sp.wait_ge(tab_made, 3)
            sp.dma_start(scratch, rb_row).then_inc(rb_out, 16)
            sp.wait_ge(pages_in, 32)
            sp.wait_ge(rb_out, 16)
            done = 3
            for s in SEQ:
                if s[0] == "pair":
                    for c in range(s[3]):
                        if BLOCK[s[1:3] + (c,)] >= done:
                            load_block(s[1:3] + (c,))
                elif s[0] == "unit":
                    load_unit(s[1:])
                elif s[0] == "ssd":
                    load_unit(("ST", 0))
                    load_unit(("ST", 1))
                elif s[0] == "prompt_self":
                    sp.wait_ge(phase, 8)
                    for q in range(2):
                        sp.dma_start(biasP[:, q], bass.AP(scratch.tensor, q * P, [[1, P], [512, H], [1, 256]]))\
                            .then_inc(bias_in, 16)
            up, down = I["w_up"], I["w_down"]
            first = N_BLOCKS % SLOTS

            def load_up(i, j):
                s = (first + j) % SLOTS
                sp.dma_start(wring[:, s, :].rearrange("p (k n) -> p k n", k=DT),
                             up[:, ds(i * 1024 + 256 * j, 256)].rearrange("(k p) n -> p k n", p=P)).then_inc(landed[s], 16)

            def load_down(i, j):
                s = (first + j) % SLOTS
                sp.dma_start(wring[:, s, :].rearrange("p (k n) -> p k n", k=DT),
                             down[1024 * j:1024 * (j + 1), ds(i * 256, 256)].rearrange("(k p) n -> p k n", p=P))\
                    .then_inc(landed[s], 16)

            for j in range(SLOTS):
                old = BLOCKS[N_BLOCKS - SLOTS + j]
                sp.wait_ge(dense_ps, TILE[old[:2] + (1,)] + 1)
                load_up(0, j)
            with sp.Fori(1, 4) as i:
                for j in range(SLOTS):
                    sp.wait_ge(dense_ps, i * 8 + (UP0 - 8 + 2 * j + 2))
                    load_up(i, j)
            for j in range(SLOTS):
                sp.wait_ge(dense_ps, UP0 + 24 + 2 * j + 2)
                load_down(0, j)
            sp.dma_start(fnorm, I["norm_final"].rearrange("(o n) -> o n", o=1).broadcast_to([P, D])).then_inc(fnorm_in, 16)
            with sp.Fori(1, 4) as i:
                for j in range(SLOTS):
                    if j < SLOTS - 1:
                        sp.wait_ge(chunk_used, i * 3 + (N_USED - 3 + j + 1))
                    else:
                        sp.wait_ge(dense_ps, i * 2 + DOWN0)
                    load_down(i, j)

        @block.gpsimd
        def _(pool):
            n_step = [0]

            def step(ins):
                n_step[0] += 1
                ins.then_inc(pool_step, 1)
                pool.wait_ge(pool_step, n_step[0])

            n_stores = [0]

            def store(dst, src, signal=stores):
                if signal is stores:
                    n_stores[0] += 16
                pool.dma_start(dst, src).then_inc(signal, 16)

            def add_squares(k, n):
                for c in range(DT):
                    m = 8 * k + c
                    pool.wait_ge(sq_done, m + 1)
                    a = acc[:, k % 2, 0:n]
                    if c == 0:
                        if k >= 2:
                            in_ps(pool, ("ss", k - 2))
                        pool.tensor_copy(a, sq[:, m % 2, 0:n]).then_inc(acc_done, 1)
                    else:
                        pool.wait_ge(acc_done, m)
                        pool.tensor_tensor(a, a, sq[:, m % 2, 0:n], ALU.add).then_inc(acc_done, 1)

            pool.memset(ones[:, :], 1.0).then_inc(zeros_made, 1)
            pool.memset(eps_t[:, :], EPS).then_inc(zeros_made, 1)
            pool.memset(xpad[:, :, 0:CW - 1], 0.0).then_inc(zeros_made, 1)
            pool.memset(qz[:, :, :, :], 0.0).then_inc(zeros_made, 1)
            pool.memset(qs[:, :, :, :], 0.0).then_inc(zeros_made, 1)
            add_squares(0, T)
            add_squares(1, NP_)
            for s in SEQ:
                if s[0] == "kvtok" or s[0] == "mtok":
                    outs = ((("ktok", "vtok"), ("prompt_k", "prompt_v"), vtok) if s[0] == "kvtok" else
                            (("mktok", "mvtok"), ("prompt_mem_k", "prompt_mem_v"), memvtok))
                    for g in range(3 if s[0] == "kvtok" else 2):
                        off, n = TOKS[g]
                        kd, vd = (O[x][off:off + n] if g < 2 else O["sample" + x[6:]] for x in outs[1])
                        turned(pool, (outs[0][0], g))
                        store(kd, stage[0:n, g % 2] if s[0] == "kvtok" else mstage,
                              kst_out[g if s[0] == "kvtok" else 3 + g])
                        turned(pool, (outs[0][1], g))
                        store(vd, outs[2][0:n, g, :])
                elif s[0] == "own" and s[1] == 1:
                    turned(pool, ("own", 1))
                    pool.memset(qs[:, :, :, :], 0.0).then_inc(qs_clear, 1)
                elif s[0] == "pvend":
                    k = s[1]
                    turned(pool, ("ohead", k))
                    lo = NP_ + 16 * (k % 2)
                    for h in range(H if k < 2 else CROSS):
                        r = slice(64 * (h % 2), 64 * (h % 2) + 64) if k < 2 else slice(0, P)
                        c = h // 2 if k < 2 else h
                        src = ohT[r, c * P:(c + 1) * P].rearrange("p (b h i) -> p b h i", b=GB, h=8)[:, :, h, :]
                        dst = attT[r, c, lo:lo + 16].rearrange("p (b i) -> p b i", b=GB)
                        copy = pool.tensor_copy(dst, src)
                        if h < (H if k < 2 else CROSS) - 1:
                            step(copy)
                    copy.then_inc(heads_out, 1)
                    pool.wait_ge(heads_out, k + 1)
                elif s[0] == "ssd":
                    pool.wait_ge(stores, n_stores[0])
                    for done in kst_out:
                        pool.wait_ge(done, 16)
                    meet(pool, 1)
                    pool.tensor_copy(cg[:, :, 0:3], xpad[:, :, NP_:NP_ + 3])
                    pool.tensor_copy(cg[:, :, 3:27].rearrange("p c (b r) -> p c b r", b=NB)[:, 0:6],
                                     xpad[:, 0:6, XS:XPAD].rearrange("p c (b r) -> p c b r", b=NB)[:, :, :, NI:NI + 3])
                    pool.tensor_copy(cg[:, :, 3:27].rearrange("p c (b r) -> p c b r", b=NB)[:, 6:12],
                                     xpad[:, 6:12, XS:XPAD].rearrange("p c (b r) -> p c b r", b=NB)[:, :, :, NI:NI + 3])\
                        .then_inc(cg_made, 1)
                    pool.wait_ge(cg_made, 1)
                    step(pool.memset(tmp[:, 0:2560], 0.0))
                    pool.wait_ge(silu_done, 1)
                    for g in range(2):
                        for b in range(NB):
                            last = pool.tensor_copy(cz[:, g, b, NI * b:NI * b + NI],
                                                    xc[:, 10 + g, NP_ + NI * b:NP_ + NI * b + NI])
                    last.then_inc(cz_made, 1)
                    for i in range(3):
                        turned(pool, ("cvout", i))
                    store(O["prompt_conv"], cvo[0:3, :], cv_out)
                    store(O["sample_conv"], cvo[3:27, :], cv_out)
                    in_ps(pool, ("st", 1, 1))
                    pool.memset(xwt, 0.0).then_inc(xw_clear, 1)
                    pool.wait_ge(up_done, 16)
                    for h in range(2):
                        src = kvring[:, UNIT[("ST", h)] % 2].rearrange("p b a (c n) -> p b (a c) n", n=SN)
                        for b in range(GB):
                            store(O["sample_ssm"][h * GB + b].rearrange("(c p) n -> p c n", p=P), src[:, b],
                                  st_out)
                    for h in range(2):
                        turned(pool, ("sf", h))
                        store(O["prompt_ssm"][512 * h:512 * h + 512].rearrange("(c p) n -> p c n", p=P),
                              sfo[:, 512 * h:512 * h + 512].rearrange("p (c n) -> p c n", n=SN))
                    add_squares(2, T)
                    pool.wait_ge(stores, n_stores[0])
                    pool.wait_ge(st_out, 128)
                    meet(pool, 2)
                elif s[0] == "pair" and s[1:3] in (("out", 3), ("cao", 3)):
                    add_squares(3 if s[1] == "out" else 4, T)
            for g in range(3):
                off, n = TOKS[g]
                pool.wait_ge(fin_out, g + 1)
                store(O["y_prompt"][off:off + n] if g < 2 else O["y_sample"], yout[0:n, g % 2, :],
                      y0_out if g == 0 else stores)
            pool.wait_ge(y0_out, 16)
            pool.wait_ge(stores, n_stores[0])

        @block.tensor
        def _(pe):
            def transposes(key, pieces):
                bank_free(pe, key)
                for in_, col in pieces:
                    r, c = in_.shape[0], math.prod(in_.shape[1:])
                    last = pe.transpose(ps[0:c, bank(key), col:col + r], in_, ident[0:r, 0:r])
                last.then_inc(turn_ps, 1)

            def product_tile(key, rhs, k_tiles, chunks, slots, width, half, wait=None):
                t = TILE[key]
                if t >= 2:
                    pe.wait_ge(dense_out, t - 1)
                for c in range(chunks):
                    block_ready(pe, key[:2] + (c,))
                    for k in range(k_tiles):
                        if wait:
                            wait(c * k_tiles + k)
                        w = wring[:, slots[c], k * 256 + half * P:k * 256 + half * P + P]
                        last = pe.matmul(ps[:, t % 2, 0:width], w, rhs(c * k_tiles + k),
                                         start=(c + k == 0), stop=(c == chunks - 1 and k == k_tiles - 1))
                    if half == 1 and c < chunks - 1:
                        last.then_inc(chunk_used, 1)
                last.then_inc(dense_ps, 1)

            def pair(kind, n, chunks):
                slots = [BLOCK[(kind, n, c)] % SLOTS for c in range(chunks)]
                for half in range(2):
                    wait = None
                    if n == 0 and half == 0:
                        if kind in ("qk", "caq"):
                            base = 0 if kind == "qk" else 8
                            wait = lambda k, base=base: pe.wait_ge(hw_done, base + k + 1)
                        elif kind == "m":
                            wait = lambda k: pe.wait_ge(memw_done, k + 1)
                        elif kind == "out":
                            pe.wait_ge(z_normed, 8)
                            pe.wait_ge(p_out, H)
                            pe.wait_ge(heads_out, 2)
                        elif kind == "cao":
                            pe.wait_ge(p_out, H + CROSS)
                            pe.wait_ge(heads_out, 4)
                    if kind == "m":
                        rhs, width = (lambda k: memw[:, k, :]), NP_
                    elif kind == "out":
                        rhs, width = (lambda k: z[:, k, :] if k < DT else attT[:, k - DT, :]), T
                    elif kind == "cao":
                        rhs, width = (lambda k: attT[:, k, :]), T
                    else:
                        rhs, width = (lambda k: hw[:, k, :]), T
                    product_tile((kind, n, half), rhs, K_TILES[kind], chunks, slots, width, half, wait)

            def k_unit(u):
                kv_ready(pe, u)
                cross = u[0] == "MK"
                group = u[1] + (2 if cross else 0)
                src = kvring[:, UNIT[u] % 2]

                def turns(c):
                    for w in range(2):
                        transposes((u, c, w), [(src[:, 2 * w + b, t, c * P:(c + 1) * P], b * 256 + t * P)
                                               for b in range(2) for t in range(2)])

                turns(0)
                for c in range(4):
                    if c < 3:
                        turns(c + 1)
                    step = STEP[(u, c)]
                    turned(pe, (u, c, 0))
                    turned(pe, (u, c, 1))
                    if c == 0 and (cross or u[2] == 0) and group:
                        pe.wait_ge(scores_used, group if not cross else 2)
                    if c == 0 and cross:
                        pe.wait_ge(p_exp, H)
                        if u[1] == 0:
                            tile_done(pe, ("caq", 1, 1))
                    bk, lo = (4 + u[1], 0) if cross else (4 + u[2] // 2, 256 * (u[2] % 2))
                    for b in range(GB):
                        last = pe.matmul(ps[32 * b:32 * b + 32, bk, lo:lo + 256], qs[:, c, u[1] * GB + b, :],
                                         (xKT if cross else KT_)[:, step % 2, b, :], start=(c == 0), stop=(c == 3),
                                         tile_position=(0, 32 * b))
                    last.then_inc(kt_used, 1)

            def v_unit(u):
                kv_ready(pe, u)
                cross = u[0] == "MV"
                s = u[1] + (2 if cross else 0)
                first = cross or u[2] == 0
                if first and s:
                    pe.wait_ge(pv_out, s)
                if first:
                    turned(pe, ("probs", s, 0))
                    if not cross:
                        turned(pe, ("probs", s, 1))
                        turned(pe, ("probs", s, 2))
                src = kvring[:, UNIT[u] % 2]
                for t in range(2):
                    col = t if cross else 2 * u[2] + t
                    for b in range(GB):
                        last = pe.matmul(ps[32 * b:32 * b + 32, 7, :], (xPT if cross else PT)[:, col, 32 * b:32 * b + 32],
                                         src[:, b, t, :], start=(first and t == 0), stop=(cross and t == 1),
                                         tile_position=(0, 32 * b))
                last.then_inc(v_used, 1)

            def pv_end(s):
                if s < 2:
                    turned(pe, ("vtok", 2))
                    for b in range(GB):
                        last = pe.matmul(ps[32 * b:32 * b + 32, 7, :], PT[0:NS, 8, 32 * b:32 * b + 32],
                                         vtok[0:NS, 2, :], start=False, stop=True, tile_position=(0, 32 * b))
                    last.then_inc(pv_ps, 1)
                pe.wait_ge(pv_out, s + 1)
                o = xosb if s >= 2 else osb
                transposes(("ohead", s), [(o[:, c * P:(c + 1) * P], c * P) for c in range(4)])

            def prompt_attention(key, base, heads):
                cross = base > 0

                def scores(x):
                    if base + x >= 2:
                        pe.wait_ge(p_exp, base + x - 1)
                    for q in range(2):
                        lhsT = qz[:, 0, x, q * P:(q + 1) * P] if cross else qz[:, x % 2, x // 2, q * P:(q + 1) * P]
                        rhs = memkT[:, x, :] if cross else kT[:, x // 2, 0:NP_]
                        last = pe.matmul(ps[:, 4 + x % 2, q * 256:(q + 1) * 256], lhsT, rhs, start=True, stop=True)
                    last.then_inc(p_scores, 1)

                scores(0)
                scores(1)
                for x in range(heads):
                    pe.wait_ge(p_probs, base + x + 1)
                    transposes((key, x), [(PL[:, x % 2, q, m * P:(m + 1) * P], m * 256 + q * P)
                                          for q in range(2) for m in range(2)])
                    if x + 2 < heads:
                        scores(x + 2)
                    turned(pe, (key, x))
                    if x >= 2:
                        pe.wait_ge(p_out, base + x - 1)
                    for m in range(2):
                        if cross:
                            out, v = ps[:, x % 2, 0:NP_], memvtok[:, m, x * P:(x + 1) * P]
                        else:
                            out = ps[64 * (x % 2):64 * (x % 2) + 64, x // 2 % 2, 0:NP_]
                            v = vtok[:, m, x * DH:(x + 1) * DH]
                        last = pe.matmul(out, v, PTp[:, x % 2, m, :], start=(m == 0), stop=(m == 1),
                                         tile_position=(0, 0 if cross else 64 * (x % 2)))
                    last.then_inc(p_pv, 1)

            def ssd():
                pe.wait_ge(silu_done, 1)
                pe.wait_ge(cg_made, 1)
                for i in range(3):
                    transposes(("cvout", i), [(cg[:, 4 * i + j, :], j * P) for j in range(4)])
                pe.wait_ge(dt_done, 1)
                pe.matmul(ps[:, 4, 320:392], head_rows[:, :], psums[:, :, :].rearrange("h c b -> h (c b)"),
                          start=True, stop=True).then_inc(dec_ps, 1)
                for q in range(3):
                    off, n = TOKS[q]
                    lat, upt = (later, upto) if q < 2 else (later_s, upto_s)
                    dt_turn(q, off, n)
                    for h in range(2):
                        transposes_in(("xtok", q, h), [(xc[:, 4 * h + j, off:off + n], j * P) for j in range(4)], n)
                    transposes_in(("btok", q), [(xc[:, 8 + j, off:off + n], j * P) for j in range(2)], n)
                    turned(pe, ("dt", q))
                    pe.wait_ge(dec_exp, 1)
                    if q:
                        pe.wait_ge(sums_exp, q)
                    if q == 2:
                        pe.wait_ge(acb_exp, 4)
                    dtA = dtok[0:n, 16:32]
                    pe.matmul(ps[0:n, 4, 256:272], lat[0:n, 0:n], dtA, start=True, stop=True)
                    pe.matmul(ps[:, 4, 272:288], ones[0:n, :], dtA, start=True, stop=True)
                    pe.matmul(ps[0:n, 4, 288:304], upt[0:n, 0:n], dtA, start=True, stop=True).then_inc(sums_ps, 1)
                    for g in range(2):
                        last = pe.matmul(ps[0:n, 5, g * P:g * P + n], xc[:, 8 + g, off:off + n],
                                         xc[:, 10 + g, off:off + n], start=True, stop=True)
                    last.then_inc(g_ps, 1)
                    if q == 2:
                        ssd_sample()
                        break

                    def segments(hg):
                        k = 4 * q + hg
                        pe.wait_ge(rhs_made, k + 1)
                        if k >= 2:
                            pe.wait_ge(seg_exp, k - 1)
                        pe.matmul(ps[:, hg % 2, :], later[:, :], rhs4[:, hg % 2, :], start=True, stop=True)\
                            .then_inc(seg_ps, 1)
                        if q == 1:
                            if hg:
                                pe.wait_ge(acb_exp, hg)
                            else:
                                pe.wait_ge(gm_made, 2)
                            pe.matmul(ps[:, 5, :], ones[:, :], rhs4[:, hg % 2, :], start=True, stop=True)\
                                .then_inc(acb_ps, 1)

                    def outputs(hg):
                        pe.wait_ge(mix_made, 4 * q + hg + 1)
                        if q == 1:
                            pe.wait_ge(cs_made, hg + 1)
                            if hg == 0:
                                turned(pe, ("st", 0, 0))
                                turned(pe, ("st", 0, 1))
                        key = ("y", q, hg)
                        bank_free(pe, key)
                        for j in range(4):
                            h = 4 * hg + j
                            out = ps[64 * (j % 2):64 * (j % 2) + 64, bank(key), (j // 2) * P:(j // 2) * P + P]
                            last = pe.matmul(out, xtok[:, h * 64:h * 64 + 64], M4[:, hg % 2, j * P:(j + 1) * P],
                                             start=True, stop=(q == 0), tile_position=(0, 64 * (j % 2)))
                            if q == 1:
                                last = pe.matmul(out, st0[:, h * 64:h * 64 + 64], CS[:, hg % 2, j * P:(j + 1) * P],
                                                 start=False, stop=True, tile_position=(0, 64 * (j % 2)))
                        last.then_inc(turn_ps, 1)

                    segments(0)
                    for hg in range(4):
                        if hg < 3:
                            segments(hg + 1)
                        outputs(hg)
                    pe.wait_ge(xw_made, q + 1)
                    for g in range(2):
                        key = ("st", q, g)
                        bank_free(pe, key)
                        pe.matmul(ps[:, bank(key), :], btok[:, g * P:(g + 1) * P], xwt[:, g * 512:(g + 1) * 512],
                                  start=True, stop=True).then_inc(turn_ps, 1)
                pe.wait_ge(state_made, 1)
                for h in range(2):
                    transposes(("sf", h), [(st1[:, (4 * h + j) * P:(4 * h + j + 1) * P], j * P) for j in range(4)])

            def dt_turn(q, off, n):
                key = ("dt", q)
                bank_free(pe, key)
                for i in range(2):
                    last = pe.transpose(ps[0:n, bank(key), 16 * i:16 * i + 16], dts[:, i, off:off + n], ident[0:SH, 0:SH])
                last.then_inc(turn_ps, 1)

            def transposes_in(key, pieces, n):
                bank_free(pe, key)
                for in_, col in pieces:
                    last = pe.transpose(ps[0:n, bank(key), col:col + P], in_, ident[:, :])
                last.then_inc(turn_ps, 1)

            def ssd_sample():
                n = NS
                pe.wait_ge(rhs_made, 9)
                pe.wait_ge(seg_exp, 8)
                pe.matmul(ps[0:n, 0, :], later_s[:, :], rhs4[0:n, 0, :], start=True, stop=True).then_inc(seg_ps, 1)
                pe.wait_ge(cz_made, 1)
                pe.wait_ge(gm_made, 3)
                kv_ready(pe, ("ST", 0))
                kv_ready(pe, ("ST", 1))

                def state_turn(k):
                    bi, bh, g = k // 4, k // 2 % 2, k % 2
                    st = kvring[:, UNIT[("ST", bh)] % 2, bi].rearrange("p a (c n) -> p (a c) n", n=SN)
                    transposes(("ss", bi, bh, g), [(st[:, 4 * g + j, :], j * P) for j in range(4)])

                state_turn(0)
                state_turn(1)
                for k in range(16):
                    bi, bh, g = k // 4, k // 2 % 2, k % 2
                    if k + 2 < 16:
                        state_turn(k + 2)
                    turned(pe, ("ss", bi, bh, g))
                    r = 32 * (2 * bh + g)
                    pe.matmul(ps[r:r + 32, 5, :], cz[:, g, GB * bh + bi, :], ssT[k % 4], start=(bi == 0), stop=(bi == 3),
                              tile_position=(0, r)).then_inc(ssT_used, 1)
                pe.wait_ge(mix_made, 9)
                for g in range(2):
                    key = ("yd", g)
                    bank_free(pe, key)
                    for j in range(8):
                        h = 8 * g + j
                        last = pe.matmul(ps[0:n, bank(key), j * 64:(j + 1) * 64], M4[0:n, 0, h * n:(h + 1) * n],
                                         xtok[0:n, h * 64:h * 64 + 64], start=True, stop=True)
                    last.then_inc(turn_ps, 1)
                pe.wait_ge(xw_made, 3)
                pe.wait_ge(bbd_made, 1)
                for k in range(16):
                    c, bh = k // 2, k % 2
                    if k >= 2:
                        pe.wait_ge(up_done, k - 1)
                    else:
                        pe.wait_ge(seg_exp, 9)
                    pe.matmul(ps[:, k % 2, :], xwt[:, c * P:(c + 1) * P], bbd[:, c // 4, GB * bh:GB * bh + GB, :],
                              start=True, stop=True).then_inc(up_ps, 1)
                pe.wait_ge(ys_made, 1)
                key = "ys"
                bank_free(pe, key)
                for c in range(DT):
                    last = pe.transpose(ps[:, bank(key), c * n:(c + 1) * n], yo[:, c * P:(c + 1) * P], ident[0:n, 0:n])
                last.then_inc(turn_ps, 1)

            pe.wait_ge(ident_in, 16)
            pe.wait_ge(vec_in, 16 * 7)
            transposes("vec", [(vec_rows[:, :], 0)])
            pe.wait_ge(x_in, 32)
            for c in range(DT):
                transposes(("x", c), [(xin[0:n, g, c * P:(c + 1) * P], off) for g, (off, n) in enumerate(TOKS)])
            pe.wait_ge(tab_in, 16 * 6)
            pe.wait_ge(rbx_made, 1)
            for i, (a, n) in enumerate(((0, 512), (512, 512), (PAST, NS))):
                pe.matmul(ps[:, (4, 5, 0)[i], 0:n], rbx, oh_s[:, a:a + n], start=True, stop=True)
            pe.matmul(ps[0:H, 1, :], rb_tab[:, :], oh_p, start=True, stop=True).then_inc(tab_ps, 1)
            pe.wait_ge(mem_in, 16)
            for c in range(DT):
                transposes(("mem", c), [(memin[:, g, c * P:(c + 1) * P], g * P) for g in range(2)])
            pe.wait_ge(cv_in, 16)
            transposes("conv", [(cvin[:, c * P:(c + 1) * P], c * 24) for c in range(XT)])
            pe.wait_ge(tab_made, 3)

            for s in SEQ:
                if s[0] == "pair":
                    pair(*s[1:])
                elif s[0] == "ss":
                    k, n = s[1], NP_ if s[1] == 1 else T
                    pe.wait_ge(acc_done, 8 * k + 8)
                    pe.wait_ge(zeros_made, 5)
                    key = ("ss", k)
                    bank_free(pe, key)
                    pe.matmul(ps[:, bank(key), 0:n], ones[:, :], acc[:, k % 2, 0:n], start=True, stop=True)\
                        .then_inc(turn_ps, 1)
                elif s[0] == "dt":
                    t = TILE["dt"]
                    pe.wait_ge(dtw_in, 16)
                    pe.wait_ge(dense_out, t - 1)
                    for k in range(DT):
                        last = pe.matmul(ps[0:SH, t % 2, 0:T], wdt[:, k, :], hw[:, k, :], start=(k == 0), stop=(k == DT - 1))
                    last.then_inc(dense_ps, 1)
                elif s[0] == "unit":
                    if s[1] == "K" and s[2:] == (0, 0):
                        tile_done(pe, ("qk", 1, 1))
                    (k_unit if s[1] in ("K", "MK") else v_unit)(s[1:])
                elif s[0] in ("kvtok", "mtok"):
                    kv = s[0] == "kvtok"
                    if kv:
                        tile_done(pe, ("v", 1, 1))
                    else:
                        tile_done(pe, ("m", 3, 1))
                    for g in range(3 if kv else 2):
                        off, n = TOKS[g]
                        for name, src in ((("ktok", kT), ("vtok", vT)) if kv else (("mktok", memkT), ("mvtok", vT))):
                            transposes_in((name, g), [(src[:, c, off:off + n], c * P) for c in range(4)], n)
                elif s[0] == "own":
                    key = ("own", s[1])
                    bank_free(pe, key)
                    for b in range(GB):
                        for c in range(4):
                            last = pe.matmul(ps[32 * b:32 * b + 32, bank(key), 0:NS], qs[:, c, s[1] * GB + b, :],
                                             kT[:, c, NP_:T], start=(c == 0), stop=(c == 3), tile_position=(0, 32 * b))
                    last.then_inc(turn_ps, 1)
                elif s[0] == "probs":
                    k = s[1]
                    pe.wait_ge(row_exp, k + 1)
                    if k < 2:
                        for j in range(2):
                            transposes(("probs", k, j), [(logit[:, (4 * j + i) * P:(4 * j + i + 1) * P], i * P)
                                                         for i in range(4)])
                        transposes(("probs", k, 2), [(logit[:, PAST:PAST + NS], 0)])
                    else:
                        transposes(("probs", k, 0), [(logit_x[:, k % 2, i * P:(i + 1) * P], i * P) for i in range(2)])
                elif s[0] == "pvend":
                    pv_end(s[1])
                elif s[0] == "ssd":
                    meet(pe, 1)
                    ssd()
                    meet(pe, 2)
                elif s[0] == "prompt_self":
                    prompt_attention("prompt_self", 0, H)
                elif s[0] == "prompt_cross":
                    pe.wait_ge(scores_used, 4)
                    prompt_attention("prompt_cross", H, CROSS)

            first = N_BLOCKS % SLOTS
            before = [sum(1 for g in range(N_BLOCKS) if g % SLOTS == (first + j) % SLOTS) for j in range(SLOTS)]
            pe.wait_ge(hw_done, 24)
            with pe.Fori(0, 4) as i:
                for j in range(SLOTS):
                    s = (first + j) % SLOTS
                    pe.wait_ge(landed[s], i * 16 + 16 * (before[j] + 1))
                    for half in range(2):
                        t = UP0 + 2 * j + half
                        pe.wait_ge(dense_out, i * 8 + (t - 1))
                        for k in range(DT):
                            last = pe.matmul(ps[:, t % 2, 0:T], wring[:, s, k * 256 + half * P:k * 256 + half * P + P],
                                             hw[:, k, :], start=(k == 0), stop=(k == DT - 1))
                        last.then_inc(dense_ps, 1)
            pe.wait_ge(ff_done, FT)
            with pe.Fori(0, 4) as i:
                for half in range(2):
                    t = DOWN0 + half
                    pe.wait_ge(dense_out, i * 2 + (t - 1))
                    for j in range(SLOTS):
                        s = (first + j) % SLOTS
                        if half == 0:
                            pe.wait_ge(landed[s], i * 16 + 16 * (before[j] + 5))
                        for k in range(DT):
                            c = DT * j + k
                            last = pe.matmul(ps[:, t % 2, 0:T], wring[:, s, k * 256 + half * P:k * 256 + half * P + P],
                                             ff[:, c * T:(c + 1) * T], start=(c == 0), stop=(c == FT - 1))
                        if half == 1 and j < SLOTS - 1:
                            last.then_inc(chunk_used, 1)
                    last.then_inc(dense_ps, 1)
            pe.wait_ge(dense_out, DOWN0 + DT)
            for g in range(3):
                off, n = TOKS[g]
                for h in range(2):
                    transposes_in(("fin", g, h), [(h3[:, 4 * h + j, off:off + n], j * P) for j in range(4)], n)

        def turn_targets(key):
            kind = key if isinstance(key, str) else key[0]
            b = bank(key)
            if kind == "vec":
                return vec[:, :], ps[:, b, 0:VROWS]
            if kind == "x":
                return h3[:, key[1], :], ps[:, b, 0:T]
            if kind == "mem":
                return memw[:, key[1], :], ps[:, b, 0:NP_]
            if kind == "conv":
                return None, None
            if isinstance(kind, tuple):
                u, c, w = key
                buf = (xKT if u[0] == "MK" else KT_)[:, STEP[(u, c)] % 2, 2 * w:2 * w + 2, :]
                return buf, ps[:, b, :].rearrange("p (b t) -> p b t", b=2)
            if kind in ("ktok", "mktok"):
                n = TOKS[key[1]][1]
                return stage[0:n, key[1] % 2, :] if kind == "ktok" else mstage, ps[0:n, b, :]
            if kind in ("vtok", "mvtok"):
                n = TOKS[key[1]][1]
                return (vtok if kind == "vtok" else memvtok)[0:n, key[1], :], ps[0:n, b, :]
            if kind == "own":
                return own_raw[:, :], ps[:, b, 0:NS]
            if kind == "probs":
                s, j = key[1:]
                if s >= 2:
                    return xPT[:, :, :].rearrange("p c t -> p (c t)"), ps[:, b, 0:256]
                if j == 2:
                    return PT[0:NS, 8, :], ps[0:NS, b, 0:P]
                return PT[:, 4 * j:4 * j + 4, :].rearrange("p c t -> p (c t)"), ps[:, b, :]
            if kind == "ohead":
                return ohT[:, :], ps[:, b, :]
            if kind == "cvout":
                return cvo[:, key[1] * 512:(key[1] + 1) * 512], ps[0:27, b, :]
            if kind == "dt":
                n = TOKS[key[1]][1]
                return dtok[0:n, :], ps[0:n, b, 0:32]
            if kind == "xtok":
                n = TOKS[key[1]][1]
                return xtok[0:n, key[2] * 512:(key[2] + 1) * 512], ps[0:n, b, :]
            if kind == "btok":
                n = TOKS[key[1]][1]
                return btok[0:n, :], ps[0:n, b, 0:256]
            if kind == "y":
                return ybuf[:, key[2] % 2, :], ps[:, b, 0:256]
            if kind == "st":
                return (st0, st1)[key[1]][:, key[2] * 512:(key[2] + 1) * 512], ps[:, b, :]
            if kind == "yd":
                return ysb[:, key[1] * 512:(key[1] + 1) * 512], ps[0:NS, b, :]
            if kind == "ss" and len(key) == 4:
                return ssT[(4 * key[1] + 2 * key[2] + key[3]) % 4], ps[:, b, :]
            if kind == "ys":
                return ybuf[:, 0, :], ps[:, b, 0:256]
            if kind == "sf":
                return sfo[:, key[1] * 512:(key[1] + 1) * 512], ps[:, b, :]
            if kind in ("prompt_self", "prompt_cross"):
                return PTp[:, key[1] % 2, :, :].rearrange("p m q -> p (m q)"), ps[:, b, :]
            if kind == "fin":
                n = TOKS[key[1]][1]
                return ytok[0:n, key[1] % 2, key[2] * 512:(key[2] + 1) * 512], ps[0:n, b, :]
            raise KeyError(key)

        def target_free(e, key):
            kind = key if isinstance(key, str) else key[0]
            if isinstance(kind, tuple):
                step = STEP[(key[0], key[1])]
                if step >= 2:
                    e.wait_ge(kt_used, step - 1)
            elif kind == "ktok" and key[1] == 2:
                e.wait_ge(kst_out[0], 16)
            elif kind == "mktok":
                tile_done(e, "dt")
                if key[1]:
                    e.wait_ge(kst_out[3], 16)
            elif kind == "probs" and key[1] in (1, 3):
                e.wait_ge(pv_out, key[1])
            elif kind == "own" and key[1] == 1:
                e.wait_ge(scores_used, 1)
            elif kind == "ohead" and key[1]:
                e.wait_ge(heads_out, key[1])
            elif kind in ("dt", "xtok", "btok") and key[1]:
                in_ps(e, ("st", key[1] - 1, 1))
            elif kind == "y" and 4 * key[1] + key[2] >= 2:
                e.wait_ge(y_used, 4 * key[1] + key[2] - 1)
            elif kind == "st" and key[1] == 0:
                e.wait_ge(cv_out, 32)
            elif kind == "ss" and len(key) == 4:
                k = 4 * key[1] + 2 * key[2] + key[3]
                if k >= 4:
                    e.wait_ge(ssT_used, k - 3)
                elif k == 0 or k == 1:
                    in_ps(e, ("st", 1, 1))
                    e.wait_ge(mix_made, 8)
            elif kind == "ys":
                e.wait_ge(y_used, 8)
            elif kind in ("prompt_self", "prompt_cross"):
                x = key[1] + (H if kind == "prompt_cross" else 0)
                if x >= 2:
                    e.wait_ge(p_pv, x - 1)
            elif kind == "fin" and key[1] == 2:
                e.wait_ge(fin_out, 1)

        @block.scalar
        def _(act):
            n_step = [0]

            def step(ins):
                n_step[0] += 1
                ins.then_inc(act_step, 1)
                act.wait_ge(act_step, n_step[0])

            def leave(key):
                if TURN[key] % 2:
                    return
                in_ps(act, key)
                target_free(act, key)
                if key == "conv":
                    act.wait_ge(zeros_made, 5)
                    hist = ps[:, bank(key), 0:XT * 24].rearrange("p (c b r) -> p c b r", c=XT, b=NB)
                    for b in range(NB):
                        last = act.activation(xpad[:, :, XS + 7 * b:XS + 7 * b + 3], hist[:, :, b, :], ACT.Copy)
                    last.then_inc(turn_act, 1)
                    return
                if key[0] == "ss" and len(key) == 2:
                    n = NP_ if key[1] == 1 else T
                    if key[1]:
                        act.wait_ge(root_done, key[1])
                    act.activation(vv[:, 0:n], ps[:, bank(key), 0:n], ACT.Copy, scale=1.0 / D).then_inc(turn_act, 1)
                    return
                dst, src = turn_targets(key)
                act.activation(dst, src, ACT.Copy).then_inc(turn_act, 1)

            def square(k, c, src, n):
                m = 8 * k + c
                if m >= 2:
                    act.wait_ge(acc_done, m - 1)
                act.activation(sq[:, m % 2, 0:n], src, ACT.Square).then_inc(sq_done, 1)

            leave("vec")
            for c in range(DT):
                leave(("x", c))
                turned(act, ("x", c))
                square(0, c, h3[:, c, :], T)
            for c in range(DT):
                leave(("mem", c))
                turned(act, ("mem", c))
                square(1, c, memw[:, c, :], NP_)
            leave("conv")
            act.wait_ge(const_in, 16 * 12)
            act.activation(hcol[:, 3:4], hcol[:, 1:2], ACT.Exp).then_inc(alog_exp, 1)

            def row_exps(s):
                act.wait_ge(bounds_made, s + 1)
                if s < 2:
                    for k in range(5):
                        lo, hi = (256 * k, 256 * k + 256) if k < 4 else (PAST, PAST + NS)
                        last = act.activation(logit[:, lo:hi], logit[:, lo:hi], ACT.Exp, bias=sm(s, 14 + k, 15 + k),
                                              accum_out=sm(s, 19 + k, 20 + k))
                else:
                    act.activation(logit_x[:, s % 2, :], ps[:, 2 + s, 0:256], ACT.Exp, bias=sm(s, 14, 15),
                                   scale=P ** -0.5, accum_out=sm(s, 19, 20)).then_inc(scores_used, 1)
                    act.wait_ge(scores_used, s + 1)
                    last = act.activation(sm(s, 20, 21), sm(s, 19, 20), ACT.Copy)
                last.then_inc(row_exp, 1)

            def prompt_attention(key, base, heads):
                cross = base > 0

                def exps(x):
                    act.wait_ge(p_bound, base + x + 1)
                    for q in range(2):
                        src = ps[:, 4 + x % 2, q * 256:(q + 1) * 256] if cross else PL[:, x % 2, q, :]
                        last = act.activation(PL[:, x % 2, q, :], src, ACT.Exp, bias=mx[:, x % 2, 2 + q:3 + q],
                                              scale=P ** -0.5 if cross else 1.0,
                                              accum_out=mx[:, x % 2, 4 + q:5 + q])
                    last.then_inc(p_exp, 1)

                exps(0)
                for x in range(heads):
                    if x + 1 < heads:
                        exps(x + 1)
                    leave((key, x))

            def ssd():
                for c in range(XT):
                    act.wait_ge(conv_done, c + 1)
                act.activation(xc[:, :, :], xc[:, :, :], ACT.Silu)
                act.activation(z[:, :, :], z[:, :, :], ACT.Silu).then_inc(silu_done, 1)
                for i in range(3):
                    leave(("cvout", i))
                act.wait_ge(dec_ps, 1)
                cols = ps[:, 4, 320:392].rearrange("p (c b) -> p c b", b=9)
                act.activation(dec[:, :, 0:NB], cols[:, :, 0:NB], ACT.Exp)
                act.activation(dec[:, :, NB:NB + 1], cols[:, :, NB:NB + 1], ACT.Copy).then_inc(dec_exp, 1)
                for q in range(3):
                    off, n = TOKS[q]
                    leave(("dt", q))
                    leave(("xtok", q, 0)), leave(("xtok", q, 1)), leave(("btok", q))
                    act.wait_ge(sums_ps, q + 1)
                    if q:
                        act.wait_ge(xw_made, q)
                        if q == 2:
                            act.wait_ge(state_made, 1)
                    act.activation(ex[0:n, :], ps[0:n, 4, 256:304], ACT.Exp).then_inc(sums_exp, 1)
                    if q == 2:
                        act.wait_ge(seg_ps, 9)
                        act.wait_ge(mix_made, 8)
                        act.activation(E4[0:NS, 0, :], ps[0:NS, 0, :], ACT.Exp).then_inc(seg_exp, 1)
                        for k in range(16):
                            leave(("ss", k // 4, k // 2 % 2, k % 2))
                        leave(("yd", 0)), leave(("yd", 1)), leave("ys")
                        continue

                    def exps(hg):
                        k = 4 * q + hg
                        act.wait_ge(seg_ps, k + 1)
                        if k >= 2:
                            act.wait_ge(mix_made, k - 1)
                        act.activation(E4[:, hg % 2, :], ps[:, hg % 2, :], ACT.Exp).then_inc(seg_exp, 1)
                        if q == 1:
                            act.wait_ge(acb_ps, hg + 1)
                            if hg >= 2:
                                in_ps(act, ("y", 1, hg - 2))
                            act.activation(CS[:, hg % 2, :], ps[:, 5, :], ACT.Exp).then_inc(acb_exp, 1)

                    exps(0)
                    for hg in range(4):
                        if hg < 3:
                            exps(hg + 1)
                        leave(("y", q, hg))
                    leave(("st", q, 0)), leave(("st", q, 1))
                leave(("sf", 0)), leave(("sf", 1))
                for c in range(DT):
                    act.wait_ge(z_ready, 1)
                    square(2, c, z[:, c, :], T)

            for s in SEQ:
                if s[0] == "unit" and s[1] in ("K", "MK"):
                    for c in range(4):
                        leave((s[1:], c, 0)), leave((s[1:], c, 1))
                elif s[0] == "ss":
                    leave(s)
                    k, n = s[1], NP_ if s[1] == 1 else T
                    turned(act, s)
                    if k:
                        act.wait_ge(rstd_done, k)
                    act.activation(rstd[:, 0:n] if k != 1 else rmem[:, :], vv[:, 0:n], ACT.Sqrt, bias=eps_t[:, 0:1])\
                        .then_inc(root_done, 1)
                elif s[0] in ("kvtok", "mtok"):
                    for g in range(3 if s[0] == "kvtok" else 2):
                        for name in (("ktok", "vtok") if s[0] == "kvtok" else ("mktok", "mvtok")):
                            leave((name, g))
                elif s[0] == "own":
                    leave(s)
                    if s[1] == 0:
                        row_exps(0)
                elif s[0] == "dt":
                    row_exps(1)
                    act.wait_ge(dt_abs, 1)
                    act.activation(dts[:, 3, :], dts[:, 2, :], ACT.Exp, scale=-1.0).then_inc(dt_exp, 1)
                elif s[0] == "probs":
                    for j in range(3 if s[1] < 2 else 1):
                        leave(s + (j,))
                elif s[0] == "pvend":
                    leave(("ohead", s[1]))
                elif s[0] == "ssd":
                    meet(act, 1)
                    ssd()
                    meet(act, 2)
                elif s[0] in ("prompt_self", "prompt_cross"):
                    if s[0] == "prompt_cross":
                        row_exps(2)
                        row_exps(3)
                    prompt_attention(s[0], 0 if s[0] == "prompt_self" else H, H if s[0] == "prompt_self" else CROSS)
                elif s[0] == "pair" and s[1] in ("out", "cao"):
                    for h in range(2):
                        act.wait_ge(dense_out, TILE[s[1:3] + (h,)] + 1)
                        square(3 if s[1] == "out" else 4, 2 * s[2] + h, h3[:, 2 * s[2] + h, :], T)
            with act.Fori(0, FT) as i:
                act.wait_ge(dense_out, i + (UP0 + 1))
                act.activation(ff[:, ds(i * T, T)], ff[:, ds(i * T, T)], ACT.Square).then_inc(ff_done, 1)
            for g in range(3):
                n = TOKS[g][1]
                leave(("fin", g, 0)), leave(("fin", g, 1))
                turned(act, ("fin", g, 0)), turned(act, ("fin", g, 1))
                if g == 2:
                    act.wait_ge(y0_out, 16)
                step(act.activation(yout[0:n, g % 2, :], ytok[0:n, g % 2, :], ACT.Square,
                                    accum_out=mx[0:n, 0, g:g + 1]))
                act.activation(mx[0:n, 1, g:g + 1], mx[0:n, 0, g:g + 1], ACT.Sqrt, bias=eps_t[0:n, 0:1],
                               scale=1.0 / D).then_inc(fin_root, 1)

        @block.vector
        def _(dve):
            n_step = [0]

            def step(ins):
                n_step[0] += 1
                ins.then_inc(dve_step, 1)
                dve.wait_ge(dve_step, n_step[0])

            def leave(key):
                if TURN[key] % 2 == 0:
                    return
                in_ps(dve, key)
                target_free(dve, key)
                if key == "conv":
                    dve.wait_ge(zeros_made, 5)
                    hist = ps[:, bank(key), 0:XT * 24].rearrange("p (c b r) -> p c b r", c=XT, b=NB)
                    for b in range(NB):
                        last = dve.tensor_copy(xpad[:, :, XS + 7 * b:XS + 7 * b + 3], hist[:, :, b, :])
                    last.then_inc(turn_dve, 1)
                    return
                if key[0] == "ss" and len(key) == 2:
                    n = NP_ if key[1] == 1 else T
                    if key[1]:
                        dve.wait_ge(root_done, key[1])
                    dve.tensor_scalar(vv[:, 0:n], ps[:, bank(key), 0:n], 1.0 / D, None, ALU.mult).then_inc(turn_dve, 1)
                    return
                dst, src = turn_targets(key)
                dve.tensor_copy(dst, src).then_inc(turn_dve, 1)

            def scale_tile(dst, src, name, c, signal):
                dve.tensor_scalar(dst, src, vec[:, VEC[name] + c:VEC[name] + c + 1], None, ALU.mult).then_inc(signal, 1)

            def tile_out(kind, n, half):
                t, c = TILE[(kind, n, half)], 2 * n + half
                b = t % 2
                dve.wait_ge(dense_ps, t + 1)
                rs = rstd
                if kind == "qk" and c < 4:
                    sides = ((0, slice(0, 64)), (1, slice(64, 128)))
                    for side, r in sides:
                        dve.tensor_tensor(qz[r, side, c, :], ps[r, b, 0:NP_], rs[r, 0:NP_], ALU.mult)
                    for side, r in sides:
                        h = 2 * c + side
                        last = dve.tensor_tensor(
                            qs[r, c, :, h * NI:h * NI + NI], ps[r, b, NP_:T].rearrange("p (b i) -> p b i", b=NB),
                            rs[r, NP_:T].rearrange("p (b i) -> p b i", b=NB), ALU.mult)
                    last.then_inc(dense_out, 1)
                elif kind == "qk":
                    dve.tensor_tensor(kT[:, c - 4, :], ps[:, b, 0:T], rs[:, :], ALU.mult).then_inc(dense_out, 1)
                elif kind == "v":
                    dve.tensor_tensor(vT[:, c, :], ps[:, b, 0:T], rs[:, :], ALU.mult).then_inc(dense_out, 1)
                elif kind == "z":
                    dve.tensor_tensor(z[:, c, :], ps[:, b, 0:T], rs[:, :], ALU.mult).then_inc(dense_out, 1)
                elif kind == "m":
                    if c == 4:
                        turned(dve, ("vtok", 2))
                    dst = memkT[:, c, :] if c < 4 else vT[:, c - 4, 0:NP_]
                    dve.tensor_tensor(dst, ps[:, b, 0:NP_], rmem[:, :], ALU.mult).then_inc(dense_out, 1)
                elif kind == "x":
                    dve.tensor_tensor(xpad[:, c, CW - 1:XS], ps[:, b, 0:NP_], rs[:, 0:NP_], ALU.mult)
                    dve.tensor_tensor(xpad[:, c, XS:XPAD].rearrange("p (b r) -> p b r", b=NB)[:, :, CW - 1:],
                                      ps[:, b, NP_:T].rearrange("p (b i) -> p b i", b=NB),
                                      rs[:, NP_:T].rearrange("p (b i) -> p b i", b=NB), ALU.mult).then_inc(dense_out, 1)
                    dve.wait_ge(dense_out, t + 1)
                    conv(c)
                elif kind == "caq":
                    if c == 0:
                        dve.wait_ge(qs_clear, 1)
                    dve.tensor_tensor(qz[:, 0, c, :], ps[:, b, 0:NP_], rs[:, 0:NP_], ALU.mult)
                    dve.tensor_tensor(qs[:, c, :, c * NI:c * NI + NI],
                                      ps[:, b, NP_:T].rearrange("p (b i) -> p b i", b=NB),
                                      rs[:, NP_:T].rearrange("p (b i) -> p b i", b=NB), ALU.mult).then_inc(dense_out, 1)
                else:
                    dve.tensor_tensor(h3[:, c, :], h3[:, c, :], ps[:, b, 0:T], ALU.add).then_inc(dense_out, 1)
                    dve.wait_ge(dense_out, t + 1)
                    scale_tile(hw[:, c, :], h3[:, c, :], "norm_ca" if kind == "out" else "norm_mlp", c, hw_done)

            def conv(c):
                n = XPAD - CW + 1
                if c == 0:
                    for done in kst_out[:3]:
                        dve.wait_ge(done, 16)
                w = [vec[:, VEC["conv_w"] + k * XT + c:VEC["conv_w"] + k * XT + c + 1] for k in range(CW)]
                y = ctmp[:, 0:n]
                step(dve.tensor_scalar(y, xpad[:, c, 0:n], w[0], vec[:, VEC["conv_b"] + c:VEC["conv_b"] + c + 1],
                                       ALU.mult, ALU.add))
                for k in (1, 2):
                    step(dve.scalar_tensor_tensor(y, xpad[:, c, k:k + n], w[k], y, ALU.mult, ALU.add))
                dve.scalar_tensor_tensor(xc[:, c, 0:NP_], xpad[:, c, 3:3 + NP_], w[3], y[:, 0:NP_], ALU.mult, ALU.add)
                yb = ctmp[:, XS:XPAD].rearrange("p (b r) -> p b r", b=NB)[:, :, 0:NI]
                xb = xpad[:, c, XS:XPAD].rearrange("p (b r) -> p b r", b=NB)[:, :, CW - 1:]
                dve.scalar_tensor_tensor(xc[:, c, NP_:T].rearrange("p (b i) -> p b i", b=NB), xb, w[3], yb,
                                         ALU.mult, ALU.add).then_inc(conv_done, 1)

            def invert(k):
                dve.wait_ge(root_done, k + 1)
                a = rmem[:, :] if k == 1 else rstd[:, :]
                dve.reciprocal(a, a).then_inc(rstd_done, 1)
                dve.wait_ge(rstd_done, k + 1)

            def self_bounds(g):
                scale = DH ** -0.5
                dve.wait_ge(kt_used, 16 * (g + 1))
                turned(dve, ("own", g))
                if g:
                    in_ps(dve, ("probs", g - 1, 2))
                sc = ps[:, 4:6, :].rearrange("p a (b n) -> p (a b) n", b=2)
                dve.tensor_reduce(sm(g, 0, 4), sc, AX.X, ALU.add)
                dve.scalar_tensor_tensor(logit[:, 0:512], ps[:, 4, :], scale, biasS[:, 0:512], ALU.mult, ALU.add)
                dve.scalar_tensor_tensor(logit[:, 512:PAST], ps[:, 5, :], scale, biasS[:, 512:PAST], ALU.mult, ALU.add)\
                    .then_inc(scores_used, 1)
                step(dve.scalar_tensor_tensor(logit[:, PAST:], own_raw[:, :], scale, biasS[:, PAST:], ALU.mult, ALU.add))
                dve.tensor_tensor(logit[:, PAST:], logit[:, PAST:], mask_own[:, g * NS:(g + 1) * NS], ALU.add)
                step(dve.tensor_reduce(sm(g, 13, 14), sm(g, 0, 4), AX.X, ALU.min))
                step(dve.tensor_scalar(sm(g, 4, 8), sm(g, 0, 4), sm(g, 13, 14), None, ALU.is_equal))
                step(dve.tensor_tensor(sm(g, 4, 8), sm(g, 4, 8), place[:, :], ALU.mult))
                step(dve.tensor_reduce(sm(g, 13, 14), sm(g, 4, 8), AX.X, ALU.max))
                step(dve.tensor_scalar(sm(g, 4, 8), sm(g, 4, 8), sm(g, 13, 14), NEG, ALU.is_equal, ALU.mult))
                dve.tensor_reduce(sm(g, 8, 12), logit[:, 0:PAST].rearrange("p (b n) -> p b n", b=4), AX.X, ALU.max)
                step(dve.tensor_reduce(sm(g, 12, 13), logit[:, PAST:], AX.X, ALU.max))
                step(dve.tensor_tensor(sm(g, 8, 12), sm(g, 8, 12), sm(g, 4, 8), ALU.add))
                step(dve.tensor_reduce(sm(g, 13, 14), sm(g, 8, 13), AX.X, ALU.max))
                dve.tensor_scalar(sm(g, 14, 18), sm(g, 4, 8), sm(g, 13, 14), None, ALU.subtract)
                dve.tensor_scalar(sm(g, 18, 19), sm(g, 13, 14), -1.0, None, ALU.mult).then_inc(bounds_made, 1)
                dve.wait_ge(scores_used, g + 1)

            def cross_bounds(g):
                s = 2 + g
                dve.wait_ge(kt_used, 32 + 4 * (g + 1))
                step(dve.tensor_reduce(sm(s, 13, 14), ps[:, 4 + g, 0:256], AX.X, ALU.max))
                dve.tensor_scalar(sm(s, 14, 15), sm(s, 13, 14), -(P ** -0.5), None, ALU.mult).then_inc(bounds_made, 1)

            def take_result(s):
                dve.wait_ge(row_exp, s + 1)
                step(dve.tensor_reduce(sm(s, 8, 9), sm(s, 19, 24 if s < 2 else 20), AX.X, ALU.add))
                step(dve.reciprocal(sm(s, 9, 10), sm(s, 8, 9)))
                if s < 2:
                    dve.wait_ge(pv_ps, s + 1)
                else:
                    dve.wait_ge(v_used, 8 + s - 2 + 1)
                dve.tensor_scalar((osb if s < 2 else xosb), ps[:, 7, :], sm(s, 9, 10), None, ALU.mult).then_inc(pv_out, 1)

            def dt_rates():
                t = TILE["dt"]
                dve.wait_ge(dense_ps, t + 1)
                d = [dts[:, i, :] for i in range(6)]
                dve.tensor_tensor(d[0], ps[0:SH, t % 2, 0:T], rstd[0:SH, :], ALU.mult).then_inc(dense_out, 1)
                dve.wait_ge(dense_out, t + 1)
                dve.wait_ge(const_in, 16 * 12)
                step(dve.tensor_scalar(d[1], d[0], hcol[:, 0:1], None, ALU.add))
                dve.scalar_tensor_tensor(d[2], d[1], -1.0, d[1], ALU.mult, ALU.max).then_inc(dt_abs, 1)
                dve.wait_ge(dt_exp, 1)
                step(dve.tensor_scalar(d[4], d[3], 2.0, None, ALU.add))
                step(dve.reciprocal(d[5], d[4]))
                step(dve.tensor_tensor(d[4], d[3], d[5], ALU.mult))
                step(dve.tensor_tensor(d[5], d[4], d[4], ALU.mult))
                step(dve.tensor_scalar(d[3], d[5], 1.0 / 15, None, ALU.mult))
                for k in (13, 11, 9, 7, 5, 3):
                    step(dve.scalar_tensor_tensor(d[3], d[3], 1.0 / k, d[5], ALU.add, ALU.mult))
                step(dve.scalar_tensor_tensor(d[3], d[3], 1.0, d[4], ALU.add, ALU.mult))
                step(dve.tensor_scalar(d[1], d[1], 0.0, None, ALU.max))
                step(dve.scalar_tensor_tensor(d[0], d[3], 2.0, d[1], ALU.mult, ALU.add))
                dve.wait_ge(alog_exp, 1)
                step(dve.tensor_scalar(d[1], d[0], hcol[:, 3:4], -1.0, ALU.mult, ALU.mult))
                dve.tensor_reduce(sums[:, 0:NB], dts[:, 1, NP_:T].rearrange("p (b i) -> p b i", b=NB), AX.X, ALU.add)
                step(dve.tensor_copy(sums[:, NB:NB + 1], hcol[:, 2:3]))
                dve.tensor_tensor(psums[:, :, :], spread(sums[:, :], [SH, DT, NB + 1], 1),
                                  spread(pair_of[:, :], [SH, DT, NB + 1], 2), ALU.mult).then_inc(dt_done, 1)

            def heads(ap, n_heads, width):
                return ap.rearrange("p (h w) -> p h w", h=n_heads)

            def spread(col, shape, axis):
                return col.unsqueeze(axis).broadcast_to(shape)

            def ssd():
                for i in range(3):
                    leave(("cvout", i))
                dve.wait_ge(silu_done, 1)
                for q in range(3):
                    off, n = TOKS[q]
                    upt = (upto, upto_s)[q == 2]
                    if q == 2:
                        state()
                        dve.wait_ge(seg_ps, 8)
                        dve.wait_ge(acb_ps, 4)
                    leave(("dt", q))
                    turned(dve, ("dt", q))

                    def rhs(hg):
                        if 4 * q + hg >= 2:
                            dve.wait_ge(seg_ps, 4 * q + hg - 1)
                        if q == 1 and hg >= 2:
                            dve.wait_ge(acb_ps, hg - 1)
                        dve.tensor_tensor(heads(rhs4[:, hg % 2, :], 4, P), spread(upto[:, :], [P, 4, P], 1),
                                          spread(dtok[:, 16 + 4 * hg:20 + 4 * hg], [P, 4, P], 2), ALU.mult)\
                            .then_inc(rhs_made, 1)

                    if q < 2:
                        rhs(0)
                        rhs(1)
                    else:
                        dve.tensor_tensor(heads(rhs4[0:n, 0, :], SH, n), spread(upto_s[:, :], [n, SH, n], 1),
                                          spread(dtok[0:n, 16:32], [n, SH, n], 2), ALU.mult).then_inc(rhs_made, 1)
                    leave(("xtok", q, 0)), leave(("xtok", q, 1)), leave(("btok", q))
                    turned(dve, ("xtok", q, 0)), turned(dve, ("xtok", q, 1)), turned(dve, ("btok", q))
                    xh, wh = heads(xtok[0:n, :], SH, 64), heads(xwt[0:n, :], SH, 64)
                    step(dve.tensor_tensor(xh, xh, spread(dtok[0:n, 0:16], [n, SH, 64], 2), ALU.mult))
                    dve.wait_ge(sums_exp, q + 1)
                    if q == 2:
                        dve.wait_ge(xw_clear, 1)
                    dve.tensor_tensor(wh, xh, spread(ex[0:n, 0:16], [n, SH, 64], 2), ALU.mult).then_inc(xw_made, 1)
                    dve.wait_ge(g_ps, q + 1)
                    dve.tensor_tensor(heads(Gm[0:n, :], 2, P)[:, :, 0:n], heads(ps[0:n, 5, 0:256], 2, P)[:, :, 0:n],
                                      spread(upt[0:n, 0:n], [n, 2, n], 1), ALU.mult).then_inc(gm_made, 1)
                    dve.wait_ge(gm_made, q + 1)
                    if q == 2:
                        ssd_sample()
                        break

                    def mix(hg):
                        k = 4 * q + hg
                        dve.wait_ge(seg_exp, k + 1)
                        if k >= 2:
                            in_ps(dve, ("y",) + divmod(k - 2, 4))
                        dve.tensor_tensor(heads(M4[:, hg % 2, :], 4, P), heads(E4[:, hg % 2, :], 4, P),
                                          spread(Gm[:, (hg // 2) * P:(hg // 2) * P + P], [P, 4, P], 1), ALU.mult)\
                            .then_inc(mix_made, 1)
                        if q == 1:
                            dve.wait_ge(acb_exp, hg + 1)
                            c4 = heads(CS[:, hg % 2, :], 4, P)
                            dve.tensor_tensor(c4, c4, spread(xc[:, 10 + hg // 2, off:off + n], [P, 4, P], 1), ALU.mult)\
                                .then_inc(cs_made, 1)

                    def gate(hg):
                        turned(dve, ("y", q, hg))
                        if q == 0 and hg == 0:
                            dve.wait_ge(dec_exp, 1)
                        for j in range(2):
                            c = 2 * hg + j
                            y = ybuf[:, hg % 2, j * P:(j + 1) * P]
                            last = dve.scalar_tensor_tensor(y, xc[:, c, off:off + n], dec[:, c, NB:NB + 1], y,
                                                            ALU.mult, ALU.add)
                        step(last)
                        zz = z[:, 2 * hg:2 * hg + 2, off:off + n]
                        dve.tensor_tensor(zz, zz, heads(ybuf[:, hg % 2, :], 2, P), ALU.mult).then_inc(y_used, 1)

                    mix(0)
                    for hg in range(4):
                        if hg + 2 < 4:
                            rhs(hg + 2)
                        if hg < 3:
                            mix(hg + 1)
                        leave(("y", q, hg))
                        gate(hg)
                    leave(("st", q, 0)), leave(("st", q, 1))
                leave(("sf", 0)), leave(("sf", 1))

            def state():
                turned(dve, ("st", 1, 0)), turned(dve, ("st", 1, 1))
                in_ps(dve, ("st", 1, 1))
                s0 = heads(st0, SH, 64)
                step(dve.tensor_tensor(s0, s0, spread(ex[:, 16:32], [P, SH, 64], 2), ALU.mult))
                dve.tensor_tensor(st1, st0, st1, ALU.add).then_inc(state_made, 1)
                dve.wait_ge(state_made, 1)

            def ssd_sample():
                n = NS
                dve.wait_ge(cz_made, 1)
                for g in range(2):
                    last = dve.tensor_tensor(bbd[0:n, g], spread(btok[0:n, g * P:(g + 1) * P], [n, NB, P], 1),
                                             spread(batch_of[:, :], [n, NB, P], 2), ALU.mult)
                last.then_inc(bbd_made, 1)
                dve.wait_ge(seg_exp, 9)
                for g in range(2):
                    last = dve.tensor_tensor(heads(M4[0:n, 0, g * 256:(g + 1) * 256], 8, n),
                                             heads(E4[0:n, 0, g * 256:(g + 1) * 256], 8, n),
                                             spread(Gm[0:n, g * P:g * P + n], [n, 8, n], 1), ALU.mult)
                last.then_inc(mix_made, 1)
                for k in range(16):
                    leave(("ss", k // 4, k // 2 % 2, k % 2))
                leave(("yd", 0)), leave(("yd", 1))
                turned(dve, ("yd", 0)), turned(dve, ("yd", 1))
                dve.wait_ge(ssT_used, 16)
                for g in range(2):
                    step(dve.tensor_copy(yo[:, g * 512:(g + 1) * 512], ps[32 * g:32 * g + 32, 5, :]))
                    y = yo[:, g * 512:(g + 1) * 512]
                    step(dve.tensor_tensor(y, ps[64 + 32 * g:96 + 32 * g, 5, :], y, ALU.add))
                y3 = heads(yo, SH, 64)
                step(dve.tensor_tensor(y3, y3, spread(ex[0:n, 32:48], [n, SH, 64], 2), ALU.mult))
                dve.tensor_tensor(yo, yo, ysb, ALU.add).then_inc(ys_made, 1)
                for k in range(16):
                    c, bh = k // 2, k % 2
                    dve.wait_ge(up_ps, k + 1)
                    st = kvring[:, UNIT[("ST", bh)] % 2].rearrange("p b a (c n) -> p b (a c) n", n=SN)
                    for b in range(GB):
                        last = dve.scalar_tensor_tensor(st[:, b, c, :], st[:, b, c, :],
                                                        dec[:, c, GB * bh + b:GB * bh + b + 1],
                                                        ps[:, k % 2, b * P:(b + 1) * P], ALU.mult, ALU.add)
                    last.then_inc(up_done, 1)
                leave("ys")
                turned(dve, "ys")
                for c in range(DT):
                    y = ybuf[:, 0, c * n:(c + 1) * n]
                    last = dve.scalar_tensor_tensor(y, xc[:, c, NP_:T], dec[:, c, NB:NB + 1], y, ALU.mult, ALU.add)
                step(last)
                dve.tensor_tensor(z[:, :, NP_:T], z[:, :, NP_:T], heads(ybuf[:, 0, :], DT, n), ALU.mult)\
                    .then_inc(z_ready, 1)

            def prompt_attention(key, base, heads_):
                cross = base > 0

                def bound(x):
                    dve.wait_ge(p_scores, base + x + 1)
                    sc = ps[:, 4 + x % 2, :].rearrange("p (q k) -> p q k", q=2)
                    m = mx[:, x % 2, :]
                    if x >= 2:
                        in_ps(dve, (key, x - 2))
                    if cross:
                        step(dve.tensor_reduce(m[:, 0:2], sc, AX.X, ALU.max))
                        dve.tensor_scalar(m[:, 2:4], m[:, 0:2], -(P ** -0.5), None, ALU.mult).then_inc(p_bound, 1)
                    else:
                        step(dve.scalar_tensor_tensor(PL[:, x % 2], sc, DH ** -0.5, biasP[:, :, x, ::-1], ALU.mult, ALU.add))
                        step(dve.tensor_reduce(m[:, 0:2], PL[:, x % 2], AX.X, ALU.max))
                        dve.tensor_scalar(m[:, 2:4], m[:, 0:2], -1.0, None, ALU.mult).then_inc(p_bound, 1)

                def norm(x):
                    dve.wait_ge(p_exp, base + x + 1)
                    m = mx[:, x % 2, :]
                    step(dve.reciprocal(m[:, 6:8], m[:, 4:6]))
                    dve.tensor_tensor(PL[:, x % 2], PL[:, x % 2], spread(m[:, 6:8], [P, 2, 256], 2), ALU.mult)\
                        .then_inc(p_probs, 1)

                def out(x):
                    dve.wait_ge(p_pv, base + x + 1)
                    if cross:
                        dve.tensor_copy(attT[:, x, 0:NP_], ps[:, x % 2, 0:NP_]).then_inc(p_out, 1)
                    else:
                        r = slice(64 * (x % 2), 64 * (x % 2) + 64)
                        dve.tensor_copy(attT[r, x // 2, 0:NP_], ps[r, x // 2 % 2, 0:NP_]).then_inc(p_out, 1)

                if not cross:
                    dve.wait_ge(bias_in, 32)
                bound(0)
                for x in range(heads_):
                    if x + 1 < heads_:
                        bound(x + 1)
                    norm(x)
                    leave((key, x))
                    if x:
                        out(x - 1)
                out(heads_ - 1)

            dve.wait_ge(tab_in, 16 * 6)
            dve.tensor_tensor(rbx.rearrange("p (b h i) -> p b h i", b=GB, h=H),
                              rb4[:, :].unsqueeze(1).unsqueeze(3).broadcast_to([P, GB, H, NI]),
                              step_of[:, :].unsqueeze(1).unsqueeze(1).broadcast_to([P, GB, H, NI]), ALU.mult)\
                .then_inc(rbx_made, 1)
            leave("vec")
            turned(dve, "vec")
            for c in range(DT):
                leave(("x", c))
                turned(dve, ("x", c))
                scale_tile(hw[:, c, :], h3[:, c, :], "norm_mix", c, hw_done)
            dve.wait_ge(tab_ps, 1)
            dve.tensor_copy(biasS[:, 0:PAST].rearrange("p (a n) -> p a n", a=2), ps[:, 4:6, :]).then_inc(tab_made, 1)
            dve.tensor_copy(biasS[:, PAST:], ps[:, 0, 0:NS]).then_inc(tab_made, 1)
            dve.tensor_tensor(rb_row, ps[0:H, 1, :], mask_p, ALU.add).then_inc(tab_made, 1)
            dve.wait_ge(tab_made, 3)
            for c in range(DT):
                leave(("mem", c))
                turned(dve, ("mem", c))
                dve.wait_ge(sq_done, 8 + c + 1)
                scale_tile(memw[:, c, :], memw[:, c, :], "norm_mem", c, memw_done)
            leave("conv")
            dve.wait_ge(const_in, 16 * 12)
            dve.wait_ge(zeros_made, 5)
            turned(dve, "conv")

            pending = []
            for i, s in enumerate(SEQ):
                if s[0] == "pair":
                    if s[1] in ("qk", "caq") and SEQ[i + 1][0] == "ss":
                        pending = [s]
                        continue
                    tile_out(*s[1:3], 0), tile_out(*s[1:3], 1)
                elif s[0] == "ss":
                    leave(s)
                    invert(s[1])
                    for p in pending:
                        tile_out(*p[1:3], 0), tile_out(*p[1:3], 1)
                    pending = []
                    if s[1] == 2:
                        for c in range(DT):
                            last = dve.scalar_tensor_tensor(z[:, c, :], z[:, c, :],
                                                            vec[:, VEC["ssd_norm"] + c:VEC["ssd_norm"] + c + 1],
                                                            rstd[:, :], ALU.mult, ALU.mult)
                            last.then_inc(z_normed, 1)
                elif s[0] == "unit" and s[1] in ("K", "MK"):
                    for c in range(4):
                        leave((s[1:], c, 0)), leave((s[1:], c, 1))
                    if s[1] == "MK":
                        cross_bounds(s[2])
                elif s[0] in ("kvtok", "mtok"):
                    for g in range(3 if s[0] == "kvtok" else 2):
                        for name in (("ktok", "vtok") if s[0] == "kvtok" else ("mktok", "mvtok")):
                            leave((name, g))
                elif s[0] == "own":
                    leave(s)
                    self_bounds(s[1])
                elif s[0] == "dt":
                    dt_rates()
                elif s[0] == "probs":
                    for j in range(3 if s[1] < 2 else 1):
                        leave(s + (j,))
                elif s[0] == "pvend":
                    take_result(s[1])
                    leave(("ohead", s[1]))
                elif s[0] == "ssd":
                    meet(dve, 1)
                    ssd()
                    meet(dve, 2)
                elif s[0] in ("prompt_self", "prompt_cross"):
                    prompt_attention(s[0], 0 if s[0] == "prompt_self" else H, H if s[0] == "prompt_self" else CROSS)
            with dve.Fori(0, FT // 2) as i:
                for b in range(2):
                    dve.wait_ge(dense_ps, i * 2 + (UP0 + b + 1))
                    dve.scalar_tensor_tensor(ff[:, ds(i * (2 * T) + b * T, T)], ps[:, (UP0 + b) % 2, 0:T], 0.0, rstd[:, :],
                                             ALU.max, ALU.mult).then_inc(dense_out, 1)
            with dve.Fori(0, DT // 2) as i:
                for b in range(2):
                    dve.wait_ge(dense_ps, i * 2 + (DOWN0 + b + 1))
                    h = hT[:, ds(i * (2 * T) + b * T, T)]
                    dve.tensor_tensor(h, h, ps[:, (DOWN0 + b) % 2, 0:T], ALU.add).then_inc(dense_out, 1)
            dve.wait_ge(fnorm_in, 16)
            for g in range(3):
                n = TOKS[g][1]
                leave(("fin", g, 0)), leave(("fin", g, 1))
                dve.wait_ge(fin_root, g + 1)
                step(dve.reciprocal(mx[0:n, 1, 4 + g:5 + g], mx[0:n, 1, g:g + 1]))
                dve.scalar_tensor_tensor(yout[0:n, g % 2, :], ytok[0:n, g % 2, :], mx[0:n, 1, 4 + g:5 + g],
                                         fnorm[0:n, :], ALU.mult, ALU.mult).then_inc(fin_out, 1)


_FLAT = {"x_prompt": (NP_, D), "x_sample": (NS, D), "cache_k": (-1, PAGE, 512), "cache_v": (-1, PAGE, 512),
         "cache_mem_k": (NB, MEM, 512), "cache_mem_v": (NB, MEM, 512), "state_conv": (NB * 3, XT * P),
         "state_ssm": (NB, SH * SP_, SN), "page_table": (NB, NPAGE), "mem_prompt": (MEM, D), "norm_mix": (D,),
         "w_in": (D, -1), "conv_w": (-1,), "conv_b": (-1,), "dt_bias": (SH,), "a_log": (SH,), "d_skip": (SH,),
         "ssd_norm": (D,), "rel_bias": (BUCKETS, H), "w_out": (-1, D), "norm_ca": (D,), "norm_mem": (D,),
         "w_ca_q": (D, 512), "w_ca_kv": (D, 1024), "w_ca_o": (512, D), "norm_mlp": (D,), "w_up": (D, -1),
         "w_down": (-1, D), "norm_final": (D,)}
_OUTS = {"y_prompt": ((1, NP_, D), (NP_, D)), "y_sample": ((NB, NI, D), (NS, D)),
         "prompt_k": ((1, 1, NP_, H, DH), (NP_, 512)), "prompt_v": ((1, 1, NP_, H, DH), (NP_, 512)),
         "prompt_mem_k": ((1, 1, MEM, CROSS, P), (MEM, 512)), "prompt_mem_v": ((1, 1, MEM, CROSS, P), (MEM, 512)),
         "prompt_conv": ((1, 1, 3, XT * P), (3, XT * P)), "prompt_ssm": ((1, 1, SH, SP_, SN), (SH * SP_, SN)),
         "sample_k": ((1, NB, NI, H, DH), (NS, 512)), "sample_v": ((1, NB, NI, H, DH), (NS, 512)),
         "sample_conv": ((1, NB, 3, XT * P), (NB * 3, XT * P)),
         "sample_ssm": ((1, NB, SH, SP_, SN), (NB, SH * SP_, SN))}


def kernel(**inputs):
    import concourse.bacc as bacc
    from concourse.bass_utils import run_bass_kernel_spmd as run

    nc = bacc.Bacc("TRN2", target_bir_lowering=False, num_devices=1)
    arrays = {n: np.ascontiguousarray(inputs[n]).reshape(shape) for n, shape in _FLAT.items()}
    arrays.update(constants())
    ins = {n: nc.dram_tensor("in_" + n, a.shape, mybir.dt.from_np(a.dtype), kind="ExternalInput").ap()
           for n, a in arrays.items()}
    outs = {n: nc.dram_tensor("out_" + n, flat, F32, kind="ExternalOutput").ap() for n, (_, flat) in _OUTS.items()}
    scratch = nc.dram_tensor("bias_rows", (H, 512), F32, kind="Internal").ap()
    build(nc, ins, outs, scratch)
    r = run(nc, [{"in_" + n: a for n, a in arrays.items()}], core_ids=[0])
    return tuple(r.results[0]["out_" + n].reshape(shape) for n, (shape, _) in _OUTS.items())
```

```python
import math
from contextlib import ExitStack

import numpy as np

import concourse.bass as bass
from concourse import mybir

F32 = mybir.dt.float32
I32 = mybir.dt.int32
ALU = mybir.AluOpType
ACT = mybir.ActivationFunctionType
AX = mybir.AxisListType
ds = bass.ds

P = 128
D = 1024
DT = D // P
NP_ = 256
NB, NI = 8, 4
NS = NB * NI
T = NP_ + NS
H, DH = 8, 64
PAIRS = H // 2
SH, SP_, SN = 16, 64, 128
CW = 4
XT = 12
CROSS = 4
MEM = 256
FT = 32
PAST = 1024
PAGE = 128
NPAGE = PAST // PAGE
BUCKETS, MAXD = 32, 128
EPS = 1e-5
NEG = -1e30
SLOTS = 4
G = 2
GB = NB // G
XPAD = CW - 1 + NP_ + NB * (CW - 1 + NI)
XS = CW - 1 + NP_
IN_Z, IN_X, IN_DT, IN_Q, IN_K, IN_V = 0, 1024, 2560, 2576, 3088, 3600
TOKS = [(0, 128), (128, 128), (256, 32)]
TURN_BANKS = [2, 3, 6]

VEC, at = {}, 0
for _name, _rows in (("norm_mix", 8), ("norm_ca", 8), ("norm_mem", 8), ("norm_mlp", 8), ("ssd_norm", 8),
                     ("conv_b", 12), ("conv_w", 48)):
    VEC[_name] = at
    at += _rows
VROWS = at


def bucket(n):
    half = BUCKETS // 2
    if n < half:
        return n
    return min(BUCKETS - 1, half + int(math.log(n / half) / math.log(MAXD / half) * (BUCKETS - half)))


def constants():
    f = np.float32
    k, j = np.arange(P)[:, None], np.arange(P)[None, :]
    c = {"ident": np.eye(P, dtype=f), "later": (k > j).astype(f), "upto": (k <= j).astype(f)}
    ks, js = np.arange(NS)[:, None], np.arange(NS)[None, :]
    same = ks // NI == js // NI
    c["later_s"] = (same & (ks > js)).astype(f)
    c["upto_s"] = (same & (ks <= js)).astype(f)
    c["batch_of"] = (ks // NI == np.arange(NB)[None, :]).astype(f)
    oh = np.zeros((NI, BUCKETS, PAST + NS), f)
    for i in range(NI):
        for key in range(PAST):
            oh[i, bucket(PAST + i - key), key] = 1
        for tok in range(NS):
            if i >= tok % NI:
                oh[i, bucket(i - tok % NI), PAST + tok] = 1
    c["onehot_s"] = oh.reshape(P, PAST + NS)
    c["step_of"] = (np.arange(P)[:, None] // BUCKETS == np.arange(NI)[None, :]).astype(f)
    oh = np.zeros((BUCKETS, 512), f)
    m = np.zeros((H, 512), f)
    for r in range(512):
        if r >= 255:
            oh[bucket(r - 255), r] = 1
        else:
            m[:, r] = NEG
    c["onehot_p"], c["mask_p"] = oh, m
    row = np.arange(P)
    b4, i = row // 32, row % NI
    own = np.full((P, G, NS), NEG, f)
    for g in range(G):
        for tok in range(NS):
            own[(g * GB + b4 == tok // NI) & (tok % NI <= i), g, tok] = 0
    c["mask_own"] = own.reshape(P, G * NS)
    c["place"] = np.tile(np.arange(1, 5, dtype=f)[None], (P, 1))
    h = np.arange(SH)[:, None]
    c["head_rows"] = (h % 2 == np.arange(P)[None, :] // 64).astype(f)
    c["pair_of"] = (h // 2 == np.arange(DT)[None, :]).astype(f)
    return c


def make_plan():
    seq = []

    def pair(kind, n, chunks):
        seq.append(("pair", kind, n, chunks))

    def unit(*a):
        seq.append(("unit",) + a)

    def item(*a):
        seq.append(a)

    pair("qk", 0, 1)
    item("ss", 0)
    item("early")
    pair("qk", 1, 1)
    unit("K", 0, 0)
    pair("qk", 2, 1)
    unit("K", 0, 1)
    pair("qk", 3, 1)
    unit("K", 0, 2)
    pair("v", 0, 1)
    unit("K", 0, 3)
    item("own", 0)
    pair("v", 1, 1)
    unit("K", 1, 0)
    item("kvtok")
    item("ss", 1)
    pair("m", 0, 1)
    unit("K", 1, 1)
    item("probs", 0)
    pair("m", 1, 1)
    unit("K", 1, 2)
    pair("m", 2, 1)
    unit("K", 1, 3)
    item("own", 1)
    pair("m", 3, 1)
    item("mtok")
    item("heads_in", "self")
    pair("x", 0, 1)
    unit("V", 0, 0)
    item("head", "self", 0)
    pair("x", 1, 1)
    unit("V", 0, 1)
    item("head", "self", 1)
    pair("x", 2, 1)
    unit("V", 0, 2)
    item("head", "self", 2)
    pair("x", 3, 1)
    unit("V", 0, 3)
    item("pvend", 0)
    item("probs", 1)
    item("head", "self", 3)
    pair("x", 4, 1)
    unit("V", 1, 0)
    item("head", "self", 4)
    pair("x", 5, 1)
    item("dt")
    unit("V", 1, 1)
    pair("z", 0, 1)
    item("head", "self", 5)
    pair("z", 1, 1)
    unit("V", 1, 2)
    item("silu_x")
    item("head", "self", 6)
    pair("z", 2, 1)
    pair("z", 3, 1)
    unit("V", 1, 3)
    item("pvend", 1)
    item("head", "self", 7)
    item("heads_end", "self")
    item("ssd")
    item("ss", 2)
    for n in range(4):
        pair("out", n, 2)
    pair("caq", 0, 1)
    item("ss", 3)
    pair("caq", 1, 1)
    item("meet")
    item("heads_in", "cross")
    unit("MK", 0)
    item("head", "cross", 0)
    unit("MK", 1)
    item("probs", 2)
    item("head", "cross", 1)
    unit("MV", 0)
    item("head", "cross", 2)
    item("pvend", 2)
    item("probs", 3)
    item("head", "cross", 3)
    unit("MV", 1)
    item("heads_end", "cross")
    item("pvend", 3)
    for n in range(4):
        pair("cao", n, 1)
    item("ss", 4)
    return seq


SEQ = make_plan()
BLOCK, TILE, UNIT, TURN = {}, {}, {}, {}
USED = {}
for s in SEQ:
    if s[0] == "pair":
        for c in range(s[3]):
            if c < s[3] - 1:
                USED[s[1:3] + (c,)] = len(USED)
            BLOCK[s[1:3] + (c,)] = len(BLOCK)
        for h in range(2):
            TILE[s[1:3] + (h,)] = len(TILE)
    elif s[0] == "dt":
        TILE["dt"] = len(TILE)
    elif s[0] == "unit" and s[1] in ("K", "V"):
        UNIT[s[1:]] = len(UNIT)
    elif s[0] == "ssd":
        for h in range(2):
            UNIT[("ST", h)] = len(UNIT)
    elif s[0] == "unit":
        UNIT[s[1:]] = len(UNIT)
N_BLOCKS, N_TILES, N_USED = len(BLOCK), len(TILE), len(USED)


N_HEADS = {"self": H, "cross": CROSS}
HEAD0 = {"self": 0, "cross": H}


def turn(key):
    TURN[key] = len(TURN)


def plan_turns():
    turn("vec")
    for c in range(DT):
        turn(("x", c))
    for s in SEQ:
        if s[0] == "unit" and s[1] in ("K", "MK"):
            for c in range(4):
                turn((s[1:], c, 0)), turn((s[1:], c, 1))
        elif s[0] == "ss":
            turn(("ss", s[1]))
        elif s[0] == "early":
            for c in range(DT):
                turn(("mem", c))
            turn("conv")
        elif s[0] == "kvtok":
            for g in range(3):
                turn(("ktok", g)), turn(("vtok", g))
        elif s[0] == "mtok":
            for g in range(2):
                turn(("mktok", g)), turn(("mvtok", g))
        elif s[0] == "own":
            turn(("own", s[1]))
        elif s[0] == "probs":
            turn(("probs", s[1], 0))
            if s[1] < 2:
                turn(("probs", s[1], 1)), turn(("probs", s[1], 2))
        elif s[0] == "pvend":
            turn(("ohead", s[1]))
        elif s[0] == "ssd":
            for i in range(3):
                turn(("cvout", i))
            for q in range(3):
                turn(("dt", q))
                turn(("xtok", q, 0)), turn(("xtok", q, 1)), turn(("btok", q))
                if q < 2:
                    for hg in range(4):
                        turn(("y", q, hg))
                    turn(("st", q, 0)), turn(("st", q, 1))
                else:
                    for bi in range(GB):
                        for bh in range(G):
                            for g in range(2):
                                turn(("ss", bi, bh, g))
                    turn(("yd", 0)), turn(("yd", 1))
                    turn("ys")
            turn(("sf", 0)), turn(("sf", 1))
        elif s[0] == "head":
            if s[2]:
                turn(("pv", s[1], s[2] - 1))
            turn(("pt", s[1], s[2]))
        elif s[0] == "heads_end":
            turn(("pv", s[1], N_HEADS[s[1]] - 1))
    for g in range(3):
        for h in range(2):
            turn(("fin", g, h))


plan_turns()
STEP = {}
for s in SEQ:
    if s[0] == "unit" and s[1] in ("K", "MK"):
        for c in range(4):
            STEP[(s[1:], c)] = len(STEP)
UP0, DOWN0 = N_TILES, N_TILES + FT
BLOCKS, UNITS = list(BLOCK), list(UNIT)
KV_DMAS = [8 if u[0] in ("K", "V") else GB for u in UNITS]
V_ORDER = {u: i for i, u in enumerate([u for u in UNITS if u[0] in ("V", "MV")])}
K_TILES = {"qk": 8, "v": 8, "z": 8, "x": 8, "m": 8, "out": 6, "caq": 8, "cao": 4}


def build(nc, I, O, scratch):
    ctx = ExitStack()
    with ctx:
        def sb(name, shape, dt=F32):
            return ctx.enter_context(nc.sbuf_tensor(name, shape, dt))

        def sem(name):
            return ctx.enter_context(nc.semaphore(name))

        ps = ctx.enter_context(nc.psum_tensor("ps", [P, 8, 512], F32))

        ident = sb("ident", [P, P])
        later, upto, ones = sb("later", [P, P]), sb("upto", [P, P]), sb("ones", [P, P])
        later_s, upto_s = sb("later_s", [NS, NS]), sb("upto_s", [NS, NS])
        batch_of, step_of = sb("batch_of", [NS, NB]), sb("step_of", [P, NI])
        place, mask_own = sb("place", [P, 4]), sb("mask_own", [P, G * NS])
        head_rows, pair_of = sb("head_rows", [SH, P]), sb("pair_of", [SH, DT])
        vec_rows, vec = sb("vec_rows", [VROWS, P]), sb("vec", [P, VROWS])
        hcol = sb("hcol", [SH, 4])
        pages = sb("pages", [1, NB * NPAGE], I32)
        rb4 = sb("rb4", [P, H])
        small = sb("small", [P, 96])
        eps_t = sb("eps_t", [P, 1])

        wring = sb("wring", [P, SLOTS, 2048])
        wdt = sb("wdt", [P, DT, SH])
        big = sb("big", [P, 2 * 4096 + DT * T])
        kvring = big[:, 0:8192].rearrange("p (s b c n) -> p s b c n", s=2, b=GB, c=2)
        z = big[:, 8192:8192 + DT * T].rearrange("p (c t) -> p c t", c=DT)
        ff = big[:, 0:FT * T]

        hT, hw = sb("hT", [P, DT * T]), sb("hw", [P, DT, T])
        h3 = hT[:, :].rearrange("p (c t) -> p c t", c=DT)
        xc = sb("xc", [P, XT, T])
        qz = sb("qz", [P, 2, PAIRS, NP_])
        kT = sb("kT", [P, PAIRS, T])
        vtok = sb("vtok", [P, 3, 512])
        attT = sb("attT", [P, 4, T])
        mkv = sb("mkv", [P, 2048])
        memkT = mkv[:, 0:1024].rearrange("p (c t) -> p c t", c=4)
        memvtok = mkv[:, 1024:2048].rearrange("p (c t) -> p c t", c=2)
        qs = sb("qs", [P, 4, NB, 32])
        sq, acc, rstd = sb("sq", [P, 2, T]), sb("acc", [P, 2, T]), sb("rstd", [P, T])
        rmem = sb("rmem", [P, NP_])
        vv = sb("vv", [P, T])
        T_FREE = 13200
        tmp = sb("tmp", [P, T_FREE])

        at = [0]

        def part(n):
            a = tmp[:, at[0]:at[0] + n]
            at[0] += n
            assert at[0] <= T_FREE, at[0]
            return a

        xpad = part(XT * XPAD).rearrange("p (c t) -> p c t", c=XT)
        ssd_at = at[0]
        memw = part(DT * NP_).rearrange("p (c t) -> p c t", c=DT)
        KT_ = part(2 * 1024).rearrange("p (s b t) -> p s b t", s=2, b=GB)
        vT = part(PAIRS * T).rearrange("p (c t) -> p c t", c=PAIRS)
        logit = part(PAST + NS)
        biasS = part(PAST + NS)
        PT = part(9 * P).rearrange("p (c t) -> p c t", c=9)
        osb = part(512)
        ctmp = part(XPAD)
        stage = xc[:, :, :].rearrange("p c t -> p (c t)")[:, 0:1024].rearrange("p (s t) -> p s t", s=2)
        mstage = big[:, 8192:8192 + 1024].rearrange("p (s t) -> p s t", s=2)
        xin = xc[:, :, :].rearrange("p c t -> p (c t)")[:, 0:3072].rearrange("p (g n) -> p g n", g=3)
        memin = big[:, 8192:8192 + 2048].rearrange("p (g n) -> p g n", g=2)
        cvin = mkv[0:NB * 3, 0:1536]
        at[0] = ssd_at
        xtok, xwt = part(1024), part(1024)
        btok = part(256)
        rhs4 = part(1024).rearrange("p (s t) -> p s t", s=2)
        E4 = part(1024).rearrange("p (s t) -> p s t", s=2)
        M4 = part(1024).rearrange("p (s t) -> p s t", s=2)
        CS = part(1024).rearrange("p (s t) -> p s t", s=2)
        ybuf = part(2 * 256).rearrange("p (s t) -> p s t", s=2)
        st01 = part(2048)
        st0, st1 = st01[:, 0:1024], st01[:, 1024:2048]
        Gm = part(256)
        ohT = sb("ohT", [P, 512])
        ebuf = ohT[:, :]
        bbd = tmp[:, 0:2048].rearrange("p (g b n) -> p g b n", g=2, b=NB)
        cz = tmp[:, 2048:2560].rearrange("p (g b n) -> p g b n", g=2, b=NB)
        dts = [acc[0:SH, i, :] for i in range(2)] + [logit[0:SH, i * T:(i + 1) * T] for i in range(3)] + [biasS[0:SH, 0:T]]
        zpart = tmp[:, 2560:2560 + T]
        sums = sb("sums", [SH, NB + 1])
        psums = sb("psums", [SH, DT, NB + 1])
        dec = sb("dec", [P, DT, NB + 1])
        dtok = sb("dtok", [P, 32])
        ex = sb("ex", [P, 48])
        at[0] = ssd_at
        PL = part(2 * 512).rearrange("p (s q k) -> p s q k", s=2, q=2)
        PTp = part(2 * 512).rearrange("p (s m q) -> p s m q", s=2, m=2)
        biasP = part(2 * 512).rearrange("p (s q k) -> p s q k", s=2, q=2)
        mx = sb("mx", [P, 2, 8])
        at[0] = ssd_at + 2048
        logit_x = part(512).rearrange("p (g t) -> p g t", g=2)
        ytok = tmp[:, 0:2048].rearrange("p (s t) -> p s t", s=2)
        yout = tmp[:, 2048:4096].rearrange("p (s t) -> p s t", s=2)
        xKT = part(2 * 1024).rearrange("p (s b t) -> p s b t", s=2, b=GB)
        xPT = part(2 * P).rearrange("p (c t) -> p c t", c=2)
        xosb = part(512)
        fnorm = part(1024)
        rb_tab = sb("rb_tab", [BUCKETS, H])

        oh_s = big[:, 0:PAST + NS]
        oh_p = wring[0:BUCKETS, 3, 0:512]
        mask_p = wring[0:H, 3, 512:1024]
        rb_row = wring[0:H, 3, 1024:1536]
        rbx = wring[:, 3, 1536:1664]

        cg = ebuf[:, 0:XT * 27].rearrange("p (c r) -> p c r", c=XT)
        cvo = st01[0:27, 0:XT * P]
        ysb, yo = CS[0:NS, :, :].rearrange("p s t -> p (s t)"), st01[0:NS, 0:1024]
        ssT = [rhs4[:, 1, :], E4[:, 1, :], M4[:, 1, :], ebuf]
        sfo = M4[:, :, :].rearrange("p s t -> p (s t)")
        own_raw = sb("own_raw", [P, NS])

        def sm(s, a, b):
            return small[:, 24 * s + a:24 * s + b]

        x_in, ident_in, vec_in, const_in = sem("x_in"), sem("ident_in"), sem("vec_in"), sem("const_in")
        mem_in, cv_in, tab_in, pages_in = sem("mem_in"), sem("cv_in"), sem("tab_in"), sem("pages_in")
        dtw_in, fnorm_in = sem("dtw_in"), sem("fnorm_in")
        bias_in = [sem(f"bias_in{i}") for i in range(2)]
        landed = [sem(f"landed{i}") for i in range(SLOTS)]
        kv_in = [sem(f"kv_in{i}") for i in range(2)]
        dense_ps, dense_out = sem("dense_ps"), sem("dense_out")
        chunk_used = sem("chunk_used")
        turn_ps, turn_act, turn_dve = sem("turn_ps"), sem("turn_act"), sem("turn_dve")
        sq_done, acc_done, root_done, rstd_done = sem("sq_done"), sem("acc_done"), sem("root_done"), sem("rstd_done")
        hw_done, memw_done, zeros_made, qs_clear = sem("hw_done"), sem("memw_done"), sem("zeros_made"), sem("qs_clear")
        rbx_made, tab_ps, tab_made, rb_out = sem("rbx_made"), sem("tab_ps"), sem("tab_made"), sem("rb_out")
        conv_done, silu_done = sem("conv_done"), sem("silu_done")
        kt_used, scores_used = sem("kt_used"), sem("scores_used")
        bounds_made, row_exp = sem("bounds_made"), sem("row_exp")
        v_used, pv_ps, pv_out, heads_out = sem("v_used"), sem("pv_ps"), sem("pv_out"), sem("heads_out")
        dve_step, act_step, pool_step = sem("dve_step"), sem("act_step"), sem("pool_step")
        phase, stores, cv_out, st_out, y0_out = sem("phase"), sem("stores"), sem("cv_out"), sem("st_out"), sem("y0_out")
        kst_out = [sem(f"kst_out{i}") for i in range(5)]
        dt_abs, dt_exp, dt_done, alog_exp = sem("dt_abs"), sem("dt_exp"), sem("dt_done"), sem("alog_exp")
        cg_made, dec_ps, dec_exp = sem("cg_made"), sem("dec_ps"), sem("dec_exp")
        sums_ps, sums_exp, g_ps, gm_made, xw_made = sem("sums_ps"), sem("sums_exp"), sem("g_ps"), sem("gm_made"), sem("xw_made")
        rhs_made, seg_ps, seg_exp, mix_made = sem("rhs_made"), sem("seg_ps"), sem("seg_exp"), sem("mix_made")
        acb_ps, acb_exp, cs_made = sem("acb_ps"), sem("acb_exp"), sem("cs_made")
        y_used, state_made, xw_clear, cz_made = sem("y_used"), sem("state_made"), sem("xw_clear"), sem("cz_made")
        bbd_made, yoff_ps, ys_made, up_ps, up_done = sem("bbd_made"), sem("yoff_ps"), sem("ys_made"), sem("up_ps"), sem("up_done")
        z_ready, z_scaled, ssT_used = sem("z_ready"), sem("z_scaled"), sem("ssT_used")
        p_scores, p_bound, p_exp, p_probs = sem("p_scores"), sem("p_bound"), sem("p_exp"), sem("p_probs")
        z_silu = sem("z_silu")
        ff_done, fin_root, fin_out = sem("ff_done"), sem("fin_root"), sem("fin_out")

        def bank(key):
            return TURN_BANKS[TURN[key] % len(TURN_BANKS)]

        def turned(e, key):
            u = TURN[key]
            e.wait_ge(turn_dve if u % 2 else turn_act, u // 2 + 1)

        def bank_free(e, key):
            u = TURN[key] - len(TURN_BANKS)
            if u >= 0:
                e.wait_ge(turn_dve if u % 2 else turn_act, u // 2 + 1)

        def in_ps(e, key):
            e.wait_ge(turn_ps, TURN[key] + 1)

        def kv_ready(e, unit):
            n = UNIT[unit]
            e.wait_ge(kv_in[n % 2], sum(KV_DMAS[m] * 16 for m in range(n % 2, n + 1, 2)))

        def block_ready(e, key):
            g = BLOCK[key]
            e.wait_ge(landed[g % SLOTS], 16 * (g // SLOTS + 1))

        def tile_done(e, key):
            e.wait_ge(dense_out, TILE[key] + 1)

        def meet(e, n):
            e.drain().then_inc(phase, 1)
            e.wait_ge(phase, 4 * n)

        w_in, w_kv = I["w_in"], I["w_ca_kv"]

        def block_source(kind, n, c):
            if kind == "out":
                c = 1 - c
            w, col = {"qk": (w_in, IN_Q), "v": (w_in, IN_V), "z": (w_in, IN_Z), "x": (w_in, IN_X),
                      "m": (w_kv, 0), "out": (I["w_out"], 0), "caq": (I["w_ca_q"], 0),
                      "cao": (I["w_ca_o"], 0)}[kind]
            k = K_TILES[kind]
            return w[c * k * P:(c + 1) * k * P, col + 256 * n:col + 256 * (n + 1)].rearrange("(k p) n -> p k n", p=P)

        block = ctx.enter_context(nc.Block())

        @block.sync
        def _(sp):
            def load_block(key):
                g = BLOCK[key]
                if g >= SLOTS:
                    old = BLOCKS[g - SLOTS]
                    if old in USED:
                        sp.wait_ge(chunk_used, USED[old] + 1)
                    else:
                        sp.wait_ge(dense_ps, TILE[old[:2] + (1,)] + 1)
                k = K_TILES[key[0]]
                sp.dma_start(wring[:, g % SLOTS, 0:k * 256].rearrange("p (k n) -> p k n", k=k),
                             block_source(*key)).then_inc(landed[g % SLOTS], 16)

            def slot_free(n):
                if n < 2:
                    return
                old = UNITS[n - 2]
                if old[0] in ("K", "MK"):
                    sp.wait_ge(turn_ps, TURN[(old, 3, 1)] + 1)
                elif old[0] in ("V", "MV"):
                    sp.wait_ge(v_used, V_ORDER[old] + 1)
                else:
                    sp.wait_ge(st_out, 128)

            def load_unit(u):
                n = UNIT[u]
                slot_free(n)
                dst = kvring[:, n % 2]
                if u[0] in ("K", "V"):
                    cache = I["cache_k"] if u[0] == "K" else I["cache_v"]
                    first = (u[1] * 4 + u[2]) * 8
                    with sp.Fori(0, 8) as i:
                        page = sp.value_load(pages[0:1, ds(i + first, 1)], min_val=0, max_val=cache.shape[0] - 1)
                        sp.dma_start(big[:, ds(i * 512 + (n % 2) * 4096, 512)],
                                     cache[ds(page, 1)].rearrange("o p n -> p (o n)")).then_inc(kv_in[n % 2], 16)
                elif u[0] in ("MK", "MV"):
                    cache = I["cache_mem_k"] if u[0] == "MK" else I["cache_mem_v"]
                    for b in range(GB):
                        sp.dma_start(dst[:, b], cache[u[1] * GB + b].rearrange("(c p) n -> p c n", p=P))\
                            .then_inc(kv_in[n % 2], 16)
                else:
                    for b in range(GB):
                        sp.dma_start(dst[:, b].rearrange("p a (c n) -> p (a c) n", n=SN),
                                     I["state_ssm"][u[1] * GB + b].rearrange("(c p) n -> p c n", p=P))\
                            .then_inc(kv_in[n % 2], 16)

            sp.dma_start(xin[:, 0:2, :], I["x_prompt"].rearrange("(g p) n -> p g n", p=P)).then_inc(x_in, 16)
            sp.dma_start(xin[0:NS, 2, :], I["x_sample"]).then_inc(x_in, 16)
            sp.dma_start(ident[:, :], I["ident"]).then_inc(ident_in, 16)
            for name in ("norm_mix", "norm_ca", "norm_mem", "norm_mlp", "ssd_norm", "conv_b", "conv_w"):
                rows = I[name].rearrange("(r n) -> r n", n=P)
                sp.dma_start(vec_rows[VEC[name]:VEC[name] + rows.shape[0], :], rows).then_inc(vec_in, 16)
            load_block(BLOCKS[0])
            sp.dma_start(rb4[:, :], bass.AP(I["rel_bias"].tensor, 0, [[0, NI], [H, BUCKETS], [1, H]])).then_inc(tab_in, 16)
            sp.dma_start(rb_tab[:, :], I["rel_bias"]).then_inc(tab_in, 16)
            sp.dma_start(step_of[:, :], I["step_of"]).then_inc(tab_in, 16)
            sp.dma_start(oh_s, I["onehot_s"]).then_inc(tab_in, 16)
            sp.dma_start(oh_p, I["onehot_p"]).then_inc(tab_in, 16)
            sp.dma_start(mask_p, I["mask_p"]).then_inc(tab_in, 16)
            sp.dma_start(memin, I["mem_prompt"].rearrange("(g p) n -> p g n", p=P)).then_inc(mem_in, 16)
            sp.dma_start(cvin, I["state_conv"]).then_inc(cv_in, 16)
            load_block(BLOCKS[1])
            load_block(BLOCKS[2])
            sp.dma_start(pages[0:1, :].rearrange("o (k b w) -> o k b w", k=8, b=GB)[:, 0:4],
                         I["page_table"][0:GB].rearrange("b (k w) -> k b w", w=2).unsqueeze(0)).then_inc(pages_in, 16)
            sp.dma_start(pages[0:1, :].rearrange("o (k b w) -> o k b w", k=8, b=GB)[:, 4:8],
                         I["page_table"][GB:NB].rearrange("b (k w) -> k b w", w=2).unsqueeze(0)).then_inc(pages_in, 16)
            for dst, name in ((later, "later"), (upto, "upto"), (later_s, "later_s"), (upto_s, "upto_s"),
                              (batch_of, "batch_of"), (place, "place"), (mask_own, "mask_own"),
                              (head_rows, "head_rows"), (pair_of, "pair_of")):
                sp.dma_start(dst[:, :], I[name]).then_inc(const_in, 16)
            for i, name in enumerate(("dt_bias", "a_log", "d_skip")):
                sp.dma_start(hcol[:, i:i + 1], I[name].rearrange("(h o) -> h o", o=1)).then_inc(const_in, 16)
            sp.dma_start(wdt[:, :, :], w_in[:, IN_DT:IN_DT + SH].rearrange("(k p) n -> p k n", p=P)).then_inc(dtw_in, 16)
            sp.wait_ge(tab_made, 3)
            sp.dma_start(scratch, rb_row).then_inc(rb_out, 16)
            sp.wait_ge(pages_in, 32)
            sp.wait_ge(rb_out, 16)
            done = 3
            for s in SEQ:
                if s[0] == "pair":
                    for c in range(s[3]):
                        if BLOCK[s[1:3] + (c,)] >= done:
                            load_block(s[1:3] + (c,))
                elif s[0] == "unit":
                    load_unit(s[1:])
                elif s[0] == "ssd":
                    load_unit(("ST", 0))
                    load_unit(("ST", 1))
            up, down = I["w_up"], I["w_down"]
            first = N_BLOCKS % SLOTS

            def load_up(i, j):
                s = (first + j) % SLOTS
                sp.dma_start(wring[:, s, :].rearrange("p (k n) -> p k n", k=DT),
                             up[:, ds(i * 1024 + 256 * j, 256)].rearrange("(k p) n -> p k n", p=P)).then_inc(landed[s], 16)

            def load_down(i, j):
                s = (first + j) % SLOTS
                sp.dma_start(wring[:, s, :].rearrange("p (k n) -> p k n", k=DT),
                             down[1024 * j:1024 * (j + 1), ds(i * 256, 256)].rearrange("(k p) n -> p k n", p=P))\
                    .then_inc(landed[s], 16)

            for j in range(SLOTS):
                old = BLOCKS[N_BLOCKS - SLOTS + j]
                sp.wait_ge(dense_ps, TILE[old[:2] + (1,)] + 1)
                load_up(0, j)
            with sp.Fori(1, 4) as i:
                for j in range(SLOTS):
                    sp.wait_ge(dense_ps, i * 8 + (UP0 - 8 + 2 * j + 2))
                    load_up(i, j)
            for j in range(SLOTS):
                sp.wait_ge(dense_ps, UP0 + 24 + 2 * j + 2)
                load_down(0, j)
            sp.dma_start(fnorm, I["norm_final"].rearrange("(o n) -> o n", o=1).broadcast_to([P, D])).then_inc(fnorm_in, 16)
            with sp.Fori(1, 4) as i:
                for j in range(SLOTS):
                    if j < SLOTS - 1:
                        sp.wait_ge(chunk_used, i * 3 + (N_USED - 3 + j + 1))
                    else:
                        sp.wait_ge(dense_ps, i * 2 + DOWN0)
                    load_down(i, j)

        @block.gpsimd
        def _(pool):
            n_step = [0]

            def step(ins):
                n_step[0] += 1
                ins.then_inc(pool_step, 1)
                pool.wait_ge(pool_step, n_step[0])

            n_stores = [0]

            def store(dst, src, signal=stores):
                if signal is stores:
                    n_stores[0] += 16
                pool.dma_start(dst, src).then_inc(signal, 16)

            def add_squares(k, n):
                for c in range(DT):
                    m = 8 * k + c
                    pool.wait_ge(sq_done, m + 1)
                    a = acc[:, k % 2, 0:n]
                    if c == 0:
                        if k >= 2:
                            in_ps(pool, ("ss", k - 2))
                        pool.tensor_copy(a, sq[:, m % 2, 0:n]).then_inc(acc_done, 1)
                    else:
                        pool.wait_ge(acc_done, m)
                        pool.tensor_tensor(a, a, sq[:, m % 2, 0:n], ALU.add).then_inc(acc_done, 1)

            pool.memset(ones[:, :], 1.0).then_inc(zeros_made, 1)
            pool.memset(eps_t[:, :], EPS).then_inc(zeros_made, 1)
            pool.memset(xpad[:, :, 0:CW - 1], 0.0).then_inc(zeros_made, 1)
            pool.memset(qz[:, :, :, :], 0.0).then_inc(zeros_made, 1)
            pool.memset(qs[:, :, :, :], 0.0).then_inc(zeros_made, 1)
            add_squares(0, T)

            def load_bias(x):
                for q in range(2):
                    pool.dma_start(biasP[:, x % 2, q], bass.AP(scratch.tensor, x * 512 + q * P, [[1, P], [1, 256]]))\
                        .then_inc(bias_in[x % 2], 16)

            for s in SEQ:
                if s[0] == "early":
                    add_squares(1, NP_)
                elif s == ("heads_in", "self"):
                    in_ps(pool, ("mvtok", 1))
                    pool.wait_ge(rb_out, 16)
                    load_bias(0), load_bias(1)
                elif s[0:2] == ("head", "self") and s[2] + 2 < H:
                    pool.wait_ge(p_bound, s[2] + 1)
                    load_bias(s[2] + 2)
                elif s[0] == "kvtok" or s[0] == "mtok":
                    outs = ((("ktok", "vtok"), ("prompt_k", "prompt_v"), vtok) if s[0] == "kvtok" else
                            (("mktok", "mvtok"), ("prompt_mem_k", "prompt_mem_v"), memvtok))
                    for g in range(3 if s[0] == "kvtok" else 2):
                        off, n = TOKS[g]
                        kd, vd = (O[x][off:off + n] if g < 2 else O["sample" + x[6:]] for x in outs[1])
                        turned(pool, (outs[0][0], g))
                        store(kd, (stage if s[0] == "kvtok" else mstage)[0:n, g % 2],
                              kst_out[g if s[0] == "kvtok" else 3 + g])
                        turned(pool, (outs[0][1], g))
                        store(vd, outs[2][0:n, g, :])
                elif s[0] == "own" and s[1] == 1:
                    turned(pool, ("own", 1))
                    pool.memset(qs[:, :, :, :], 0.0).then_inc(qs_clear, 1)
                elif s[0] == "pvend":
                    k = s[1]
                    turned(pool, ("ohead", k))
                    lo = NP_ + 16 * (k % 2)
                    for h in range(H if k < 2 else CROSS):
                        r = slice(64 * (h % 2), 64 * (h % 2) + 64) if k < 2 else slice(0, P)
                        c = h // 2 if k < 2 else h
                        src = ohT[r, c * P:(c + 1) * P].rearrange("p (b h i) -> p b h i", b=GB, h=8)[:, :, h, :]
                        dst = attT[r, c, lo:lo + 16].rearrange("p (b i) -> p b i", b=GB)
                        copy = pool.tensor_copy(dst, src)
                        if h < (H if k < 2 else CROSS) - 1:
                            step(copy)
                    copy.then_inc(heads_out, 1)
                    pool.wait_ge(heads_out, k + 1)
                elif s[0] == "ssd":
                    pool.wait_ge(stores, n_stores[0])
                    for done in kst_out:
                        pool.wait_ge(done, 16)
                    meet(pool, 1)
                    pool.tensor_copy(cg[:, :, 0:3], xpad[:, :, NP_:NP_ + 3])
                    pool.tensor_copy(cg[:, :, 3:27].rearrange("p c (b r) -> p c b r", b=NB)[:, 0:6],
                                     xpad[:, 0:6, XS:XPAD].rearrange("p c (b r) -> p c b r", b=NB)[:, :, :, NI:NI + 3])
                    pool.tensor_copy(cg[:, :, 3:27].rearrange("p c (b r) -> p c b r", b=NB)[:, 6:12],
                                     xpad[:, 6:12, XS:XPAD].rearrange("p c (b r) -> p c b r", b=NB)[:, :, :, NI:NI + 3])\
                        .then_inc(cg_made, 1)
                    pool.wait_ge(cg_made, 1)
                    step(pool.memset(tmp[:, 0:2560], 0.0))
                    pool.wait_ge(silu_done, 1)
                    for g in range(2):
                        for b in range(NB):
                            last = pool.tensor_copy(cz[:, g, b, NI * b:NI * b + NI],
                                                    xc[:, 10 + g, NP_ + NI * b:NP_ + NI * b + NI])
                    last.then_inc(cz_made, 1)
                    for i in range(3):
                        turned(pool, ("cvout", i))
                    store(O["prompt_conv"], cvo[0:3, :], cv_out)
                    store(O["sample_conv"], cvo[3:27, :], cv_out)
                    in_ps(pool, ("st", 1, 1))
                    pool.memset(xwt, 0.0).then_inc(xw_clear, 1)
                    add_squares(2, T)
                    pool.wait_ge(up_done, 16)
                    for h in range(2):
                        src = kvring[:, UNIT[("ST", h)] % 2].rearrange("p b a (c n) -> p b (a c) n", n=SN)
                        for b in range(GB):
                            store(O["sample_ssm"][h * GB + b].rearrange("(c p) n -> p c n", p=P), src[:, b],
                                  st_out)
                    for h in range(2):
                        turned(pool, ("sf", h))
                        store(O["prompt_ssm"][512 * h:512 * h + 512].rearrange("(c p) n -> p c n", p=P),
                              sfo[:, 512 * h:512 * h + 512].rearrange("p (c n) -> p c n", n=SN))
                elif s[0] == "meet":
                    pool.wait_ge(stores, n_stores[0])
                    pool.wait_ge(st_out, 128)
                    meet(pool, 2)
                elif s[0] == "pair" and s[1:3] in (("out", 3), ("cao", 3)):
                    add_squares(3 if s[1] == "out" else 4, T)
            for g in range(3):
                off, n = TOKS[g]
                pool.wait_ge(fin_out, g + 1)
                store(O["y_prompt"][off:off + n] if g < 2 else O["y_sample"], yout[0:n, g % 2, :],
                      y0_out if g == 0 else stores)
            pool.wait_ge(y0_out, 16)
            pool.wait_ge(stores, n_stores[0])

        @block.tensor
        def _(pe):
            def transposes(key, pieces):
                bank_free(pe, key)
                for in_, col in pieces:
                    r, c = in_.shape[0], math.prod(in_.shape[1:])
                    last = pe.transpose(ps[0:c, bank(key), col:col + r], in_, ident[0:r, 0:r])
                last.then_inc(turn_ps, 1)

            def product_tile(key, rhs, k_tiles, chunks, slots, width, half, wait=None):
                t = TILE[key]
                if t >= 2:
                    pe.wait_ge(dense_out, t - 1)
                for c in range(chunks):
                    block_ready(pe, key[:2] + (c,))
                    for k in range(k_tiles):
                        if wait:
                            wait(c * k_tiles + k)
                        w = wring[:, slots[c], k * 256 + half * P:k * 256 + half * P + P]
                        last = pe.matmul(ps[:, t % 2, 0:width], w, rhs(c * k_tiles + k),
                                         start=(c + k == 0), stop=(c == chunks - 1 and k == k_tiles - 1))
                    if half == 1 and c < chunks - 1:
                        last.then_inc(chunk_used, 1)
                last.then_inc(dense_ps, 1)

            def out_tile(n, half, slots):
                t = TILE[("out", n, half)]
                if n + half == 0:
                    for x in range(H):
                        turned(pe, ("pv", "self", x))
                    pe.wait_ge(heads_out, 2)
                pe.wait_ge(dense_out, t - 1)
                for i, k in enumerate((8, 9, 10, 11, 6, 7, 0, 1, 2, 3, 4, 5)):
                    if i in (0, 6):
                        block_ready(pe, ("out", n, i // 6))
                    if n + half == 0 and k < DT:
                        pe.wait_ge(z_scaled, k + 1)
                    w = wring[:, slots[i // 6], k % 6 * 256 + half * P:k % 6 * 256 + half * P + P]
                    if k >= DT:
                        last = pe.matmul(ps[:, 4 + t % 2, 0:T], w, attT[:, k - DT, :], start=(k == 8), stop=(k == 11))
                    else:
                        last = pe.matmul(ps[:, t % 2, 0:T], w, z[:, k, :], start=(k == 6), stop=(k == 5))
                    if half == 1 and i == 5:
                        last.then_inc(chunk_used, 1)
                last.then_inc(dense_ps, 1)

            def pair(kind, n, chunks):
                slots = [BLOCK[(kind, n, c)] % SLOTS for c in range(chunks)]
                for half in range(2):
                    if kind == "out":
                        out_tile(n, half, slots)
                        continue
                    wait = None
                    if n == 0 and half == 0:
                        if kind in ("qk", "caq"):
                            base = 0 if kind == "qk" else 8
                            wait = lambda k, base=base: pe.wait_ge(hw_done, base + k + 1)
                        elif kind == "m":
                            wait = lambda k: pe.wait_ge(memw_done, k + 1)
                        elif kind == "cao":
                            for x in range(CROSS):
                                turned(pe, ("pv", "cross", x))
                            pe.wait_ge(scores_used, 4)
                            pe.wait_ge(heads_out, 4)
                    if kind == "m":
                        rhs, width = (lambda k: memw[:, k, :]), NP_
                    elif kind == "cao":
                        rhs, width = (lambda k: attT[:, k, :]), T
                    else:
                        rhs, width = (lambda k: hw[:, k, :]), T
                    product_tile((kind, n, half), rhs, K_TILES[kind], chunks, slots, width, half, wait)

            def k_unit(u):
                kv_ready(pe, u)
                cross = u[0] == "MK"
                group = u[1] + (2 if cross else 0)
                src = kvring[:, UNIT[u] % 2]

                def turns(c):
                    for w in range(2):
                        transposes((u, c, w), [(src[:, 2 * w + b, t, c * P:(c + 1) * P], b * 256 + t * P)
                                               for b in range(2) for t in range(2)])

                turns(0)
                for c in range(4):
                    if c < 3:
                        turns(c + 1)
                    step = STEP[(u, c)]
                    turned(pe, (u, c, 0))
                    turned(pe, (u, c, 1))
                    if c == 0 and not cross and u[1:] == (1, 0):
                        pe.wait_ge(scores_used, 1)
                    if c == 0 and u == ("K", 0, 0):
                        tile_done(pe, ("qk", 1, 1))
                    if c == 0 and u == ("MK", 0):
                        tile_done(pe, ("caq", 1, 1))
                    bk, lo = (u[1], 0) if cross else (4 + u[2] // 2, 256 * (u[2] % 2))
                    for b in range(GB):
                        last = pe.matmul(ps[32 * b:32 * b + 32, bk, lo:lo + 256], qs[:, c, u[1] * GB + b, :],
                                         (xKT if cross else KT_)[:, step % 2, b, :], start=(c == 0), stop=(c == 3),
                                         tile_position=(0, 32 * b))
                    last.then_inc(kt_used, 1)

            def v_unit(u):
                kv_ready(pe, u)
                cross = u[0] == "MV"
                s = u[1] + (2 if cross else 0)
                first = cross or u[2] == 0
                if first and s:
                    pe.wait_ge(pv_out, s)
                if first:
                    turned(pe, ("probs", s, 0))
                    if not cross:
                        turned(pe, ("probs", s, 1))
                        turned(pe, ("probs", s, 2))
                src = kvring[:, UNIT[u] % 2]
                for t in range(2):
                    col = t if cross else 2 * u[2] + t
                    for b in range(GB):
                        last = pe.matmul(ps[32 * b:32 * b + 32, 7, :], (xPT if cross else PT)[:, col, 32 * b:32 * b + 32],
                                         src[:, b, t, :], start=(first and t == 0), stop=(cross and t == 1),
                                         tile_position=(0, 32 * b))
                last.then_inc(v_used, 1)

            def pv_end(s):
                if s < 2:
                    turned(pe, ("vtok", 2))
                    for b in range(GB):
                        last = pe.matmul(ps[32 * b:32 * b + 32, 7, :], PT[0:NS, 8, 32 * b:32 * b + 32],
                                         vtok[0:NS, 2, :], start=False, stop=True, tile_position=(0, 32 * b))
                    last.then_inc(pv_ps, 1)
                pe.wait_ge(pv_out, s + 1)
                o = xosb if s >= 2 else osb
                transposes(("ohead", s), [(o[:, c * P:(c + 1) * P], c * P) for c in range(4)])

            def head_scores(kind, x):
                cross, k = kind == "cross", HEAD0[kind] + x
                if k >= 2:
                    pe.wait_ge(p_exp, k - 1)
                for q in range(2):
                    lhsT = qz[:, 0, x, q * P:(q + 1) * P] if cross else qz[:, x % 2, x // 2, q * P:(q + 1) * P]
                    rhs = memkT[:, x, :] if cross else kT[:, x // 2, 0:NP_]
                    last = pe.matmul(ps[:, 4 + x % 2, q * 256:(q + 1) * 256], lhsT, rhs, start=True, stop=True)
                last.then_inc(p_scores, 1)

            def head_values(kind, x):
                cross, key = kind == "cross", ("pv", kind, x)
                turned(pe, ("pt", kind, x))
                bank_free(pe, key)
                for m in range(2):
                    r, v = (0, memvtok[:, m, x * P:(x + 1) * P]) if cross else \
                        (64 * (x % 2), vtok[:, m, x * DH:(x + 1) * DH])
                    last = pe.matmul(ps[r:r + v.shape[1], bank(key), 0:NP_], v, PTp[:, x % 2, m, :],
                                     start=(m == 0), stop=(m == 1), tile_position=(0, r))
                last.then_inc(turn_ps, 1)

            def head(kind, x):
                if x:
                    head_values(kind, x - 1)
                pe.wait_ge(p_probs, HEAD0[kind] + x + 1)
                transposes(("pt", kind, x), [(PL[:, x % 2, q, m * P:(m + 1) * P], m * 256 + q * P)
                                             for q in range(2) for m in range(2)])
                if x + 2 < N_HEADS[kind]:
                    head_scores(kind, x + 2)

            def ssd():
                pe.wait_ge(silu_done, 1)
                pe.wait_ge(cg_made, 1)
                for i in range(3):
                    transposes(("cvout", i), [(cg[:, 4 * i + j, :], j * P) for j in range(4)])
                pe.wait_ge(dt_done, 1)
                pe.matmul(ps[:, 4, 320:392], head_rows[:, :], psums[:, :, :].rearrange("h c b -> h (c b)"),
                          start=True, stop=True).then_inc(dec_ps, 1)
                for q in range(3):
                    off, n = TOKS[q]
                    lat, upt = (later, upto) if q < 2 else (later_s, upto_s)
                    dt_turn(q, off, n)
                    for h in range(2):
                        transposes_in(("xtok", q, h), [(xc[:, 4 * h + j, off:off + n], j * P) for j in range(4)], n)
                    transposes_in(("btok", q), [(xc[:, 8 + j, off:off + n], j * P) for j in range(2)], n)
                    turned(pe, ("dt", q))
                    pe.wait_ge(dec_exp, 1)
                    if q:
                        pe.wait_ge(sums_exp, q)
                    if q == 2:
                        pe.wait_ge(acb_exp, 4)
                    dtA = dtok[0:n, 16:32]
                    pe.matmul(ps[0:n, 4, 256:272], lat[0:n, 0:n], dtA, start=True, stop=True)
                    pe.matmul(ps[:, 4, 272:288], ones[0:n, :], dtA, start=True, stop=True)
                    pe.matmul(ps[0:n, 4, 288:304], upt[0:n, 0:n], dtA, start=True, stop=True).then_inc(sums_ps, 1)
                    for g in range(2):
                        last = pe.matmul(ps[0:n, 5, g * P:g * P + n], xc[:, 8 + g, off:off + n],
                                         xc[:, 10 + g, off:off + n], start=True, stop=True)
                    last.then_inc(g_ps, 1)
                    if q == 2:
                        ssd_sample()
                        break

                    def segments(hg):
                        k = 4 * q + hg
                        pe.wait_ge(rhs_made, k + 1)
                        if k >= 2:
                            pe.wait_ge(seg_exp, k - 1)
                        pe.matmul(ps[:, hg % 2, :], later[:, :], rhs4[:, hg % 2, :], start=True, stop=True)\
                            .then_inc(seg_ps, 1)
                        if q == 1:
                            if hg:
                                pe.wait_ge(acb_exp, hg)
                            else:
                                pe.wait_ge(gm_made, 2)
                            pe.matmul(ps[:, 5, :], ones[:, :], rhs4[:, hg % 2, :], start=True, stop=True)\
                                .then_inc(acb_ps, 1)

                    def outputs(hg):
                        pe.wait_ge(mix_made, 4 * q + hg + 1)
                        if q == 1:
                            pe.wait_ge(cs_made, hg + 1)
                            if hg == 0:
                                turned(pe, ("st", 0, 0))
                                turned(pe, ("st", 0, 1))
                        key = ("y", q, hg)
                        bank_free(pe, key)
                        for j in range(4):
                            h = 4 * hg + j
                            out = ps[64 * (j % 2):64 * (j % 2) + 64, bank(key), (j // 2) * P:(j // 2) * P + P]
                            last = pe.matmul(out, xtok[:, h * 64:h * 64 + 64], M4[:, hg % 2, j * P:(j + 1) * P],
                                             start=True, stop=(q == 0), tile_position=(0, 64 * (j % 2)))
                            if q == 1:
                                last = pe.matmul(out, st0[:, h * 64:h * 64 + 64], CS[:, hg % 2, j * P:(j + 1) * P],
                                                 start=False, stop=True, tile_position=(0, 64 * (j % 2)))
                        last.then_inc(turn_ps, 1)

                    segments(0)
                    for hg in range(4):
                        if hg < 3:
                            segments(hg + 1)
                        outputs(hg)
                    pe.wait_ge(xw_made, q + 1)
                    for g in range(2):
                        key = ("st", q, g)
                        bank_free(pe, key)
                        pe.matmul(ps[:, bank(key), :], btok[:, g * P:(g + 1) * P], xwt[:, g * 512:(g + 1) * 512],
                                  start=True, stop=True).then_inc(turn_ps, 1)
                pe.wait_ge(state_made, 1)
                for h in range(2):
                    transposes(("sf", h), [(st1[:, (4 * h + j) * P:(4 * h + j + 1) * P], j * P) for j in range(4)])

            def dt_turn(q, off, n):
                key = ("dt", q)
                bank_free(pe, key)
                for i in range(2):
                    last = pe.transpose(ps[0:n, bank(key), 16 * i:16 * i + 16], dts[i][:, off:off + n], ident[0:SH, 0:SH])
                last.then_inc(turn_ps, 1)

            def transposes_in(key, pieces, n):
                bank_free(pe, key)
                for in_, col in pieces:
                    last = pe.transpose(ps[0:n, bank(key), col:col + P], in_, ident[:, :])
                last.then_inc(turn_ps, 1)

            def ssd_sample():
                n = NS
                pe.wait_ge(rhs_made, 9)
                pe.wait_ge(seg_exp, 8)
                pe.matmul(ps[0:n, 0, :], later_s[:, :], rhs4[0:n, 0, :], start=True, stop=True).then_inc(seg_ps, 1)
                pe.wait_ge(cz_made, 1)
                pe.wait_ge(gm_made, 3)
                kv_ready(pe, ("ST", 0))
                kv_ready(pe, ("ST", 1))

                def state_turn(k):
                    bi, bh, g = k // 4, k // 2 % 2, k % 2
                    st = kvring[:, UNIT[("ST", bh)] % 2, bi].rearrange("p a (c n) -> p (a c) n", n=SN)
                    transposes(("ss", bi, bh, g), [(st[:, 4 * g + j, :], j * P) for j in range(4)])

                state_turn(0)
                state_turn(1)
                for k in range(16):
                    bi, bh, g = k // 4, k // 2 % 2, k % 2
                    if k + 2 < 16:
                        state_turn(k + 2)
                    turned(pe, ("ss", bi, bh, g))
                    r = 32 * (2 * bh + g)
                    pe.matmul(ps[r:r + 32, 5, :], cz[:, g, GB * bh + bi, :], ssT[k % 4], start=(bi == 0), stop=(bi == 3),
                              tile_position=(0, r)).then_inc(ssT_used, 1)
                pe.wait_ge(mix_made, 9)
                for g in range(2):
                    key = ("yd", g)
                    bank_free(pe, key)
                    for j in range(8):
                        h = 8 * g + j
                        last = pe.matmul(ps[0:n, bank(key), j * 64:(j + 1) * 64], M4[0:n, 0, h * n:(h + 1) * n],
                                         xtok[0:n, h * 64:h * 64 + 64], start=True, stop=True)
                    last.then_inc(turn_ps, 1)
                pe.wait_ge(xw_made, 3)
                pe.wait_ge(bbd_made, 1)
                def update(k):
                    c, bh = k // 2, k % 2
                    if k >= 2:
                        pe.wait_ge(up_done, k - 1)
                    else:
                        pe.wait_ge(seg_exp, 9)
                    pe.matmul(ps[:, k % 2, :], xwt[:, c * P:(c + 1) * P], bbd[:, c // 4, GB * bh:GB * bh + GB, :],
                              start=True, stop=True).then_inc(up_ps, 1)

                update(0)
                update(1)
                pe.wait_ge(ys_made, 1)
                key = "ys"
                bank_free(pe, key)
                for c in range(DT):
                    last = pe.transpose(ps[:, bank(key), c * n:(c + 1) * n], yo[:, c * P:(c + 1) * P], ident[0:n, 0:n])
                last.then_inc(turn_ps, 1)
                for k in range(2, 16):
                    update(k)

            pe.wait_ge(ident_in, 16)
            pe.wait_ge(vec_in, 16 * 7)
            transposes("vec", [(vec_rows[:, :], 0)])
            pe.wait_ge(x_in, 32)
            for c in range(DT):
                transposes(("x", c), [(xin[0:n, g, c * P:(c + 1) * P], off) for g, (off, n) in enumerate(TOKS)])
            pe.wait_ge(tab_in, 16 * 6)
            pe.wait_ge(rbx_made, 1)
            for i, (a, n) in enumerate(((0, 512), (512, 512), (PAST, NS))):
                pe.matmul(ps[:, (4, 5, 0)[i], 0:n], rbx, oh_s[:, a:a + n], start=True, stop=True)
            pe.matmul(ps[0:H, 1, :], rb_tab[:, :], oh_p, start=True, stop=True).then_inc(tab_ps, 1)
            pe.wait_ge(tab_made, 3)

            for s in SEQ:
                if s[0] == "pair":
                    pair(*s[1:])
                elif s[0] == "early":
                    pe.wait_ge(mem_in, 16)
                    for c in range(DT):
                        transposes(("mem", c), [(memin[:, g, c * P:(c + 1) * P], g * P) for g in range(2)])
                    pe.wait_ge(cv_in, 16)
                    transposes("conv", [(cvin[:, c * P:(c + 1) * P], c * 24) for c in range(XT)])
                elif s[0] == "heads_in":
                    if s[1] == "self":
                        pe.wait_ge(scores_used, 2)
                    else:
                        tile_done(pe, ("caq", 1, 1))
                    head_scores(s[1], 0), head_scores(s[1], 1)
                elif s[0] == "head":
                    head(*s[1:])
                elif s[0] == "heads_end":
                    head_values(s[1], N_HEADS[s[1]] - 1)
                elif s[0] == "meet":
                    meet(pe, 2)
                elif s[0] == "ss":
                    k, n = s[1], NP_ if s[1] == 1 else T
                    pe.wait_ge(acc_done, 8 * k + 8)
                    pe.wait_ge(zeros_made, 5)
                    key = ("ss", k)
                    bank_free(pe, key)
                    pe.matmul(ps[:, bank(key), 0:n], ones[:, :], acc[:, k % 2, 0:n], start=True, stop=True)\
                        .then_inc(turn_ps, 1)
                elif s[0] == "dt":
                    t = TILE["dt"]
                    pe.wait_ge(dtw_in, 16)
                    pe.wait_ge(dense_out, t - 1)
                    for k in range(DT):
                        last = pe.matmul(ps[0:SH, t % 2, 0:T], wdt[:, k, :], hw[:, k, :], start=(k == 0), stop=(k == DT - 1))
                    last.then_inc(dense_ps, 1)
                elif s[0] == "unit":
                    (k_unit if s[1] in ("K", "MK") else v_unit)(s[1:])
                elif s[0] in ("kvtok", "mtok"):
                    kv = s[0] == "kvtok"
                    if kv:
                        tile_done(pe, ("v", 1, 1))
                    else:
                        tile_done(pe, ("m", 3, 1))
                    for g in range(3 if kv else 2):
                        off, n = TOKS[g]
                        for name, src in ((("ktok", kT), ("vtok", vT)) if kv else (("mktok", memkT), ("mvtok", vT))):
                            transposes_in((name, g), [(src[:, c, off:off + n], c * P) for c in range(4)], n)
                elif s[0] == "own":
                    key = ("own", s[1])
                    bank_free(pe, key)
                    for b in range(GB):
                        for c in range(4):
                            last = pe.matmul(ps[32 * b:32 * b + 32, bank(key), 0:NS], qs[:, c, s[1] * GB + b, :],
                                             kT[:, c, NP_:T], start=(c == 0), stop=(c == 3), tile_position=(0, 32 * b))
                    last.then_inc(turn_ps, 1)
                elif s[0] == "probs":
                    k = s[1]
                    pe.wait_ge(row_exp, k + 1)
                    if k < 2:
                        for j in range(2):
                            transposes(("probs", k, j), [(logit[:, (4 * j + i) * P:(4 * j + i + 1) * P], i * P)
                                                         for i in range(4)])
                        transposes(("probs", k, 2), [(logit[:, PAST:PAST + NS], 0)])
                    else:
                        transposes(("probs", k, 0), [(logit_x[:, k % 2, i * P:(i + 1) * P], i * P) for i in range(2)])
                elif s[0] == "pvend":
                    pv_end(s[1])
                elif s[0] == "ssd":
                    meet(pe, 1)
                    ssd()

            first = N_BLOCKS % SLOTS
            before = [sum(1 for g in range(N_BLOCKS) if g % SLOTS == (first + j) % SLOTS) for j in range(SLOTS)]
            pe.wait_ge(hw_done, 24)
            with pe.Fori(0, 4) as i:
                for j in range(SLOTS):
                    s = (first + j) % SLOTS
                    pe.wait_ge(landed[s], i * 16 + 16 * (before[j] + 1))
                    for half in range(2):
                        t = UP0 + 2 * j + half
                        pe.wait_ge(dense_out, i * 8 + (t - 1))
                        for k in range(DT):
                            last = pe.matmul(ps[:, t % 2, 0:T], wring[:, s, k * 256 + half * P:k * 256 + half * P + P],
                                             hw[:, k, :], start=(k == 0), stop=(k == DT - 1))
                        last.then_inc(dense_ps, 1)
            pe.wait_ge(ff_done, FT)
            with pe.Fori(0, 4) as i:
                for half in range(2):
                    t = DOWN0 + half
                    pe.wait_ge(dense_out, i * 2 + (t - 1))
                    for j in range(SLOTS):
                        s = (first + j) % SLOTS
                        if half == 0:
                            pe.wait_ge(landed[s], i * 16 + 16 * (before[j] + 5))
                        for k in range(DT):
                            c = DT * j + k
                            last = pe.matmul(ps[:, t % 2, 0:T], wring[:, s, k * 256 + half * P:k * 256 + half * P + P],
                                             ff[:, c * T:(c + 1) * T], start=(c == 0), stop=(c == FT - 1))
                        if half == 1 and j < SLOTS - 1:
                            last.then_inc(chunk_used, 1)
                    last.then_inc(dense_ps, 1)
            pe.wait_ge(dense_out, DOWN0 + DT)
            for g in range(3):
                off, n = TOKS[g]
                for h in range(2):
                    transposes_in(("fin", g, h), [(h3[:, 4 * h + j, off:off + n], j * P) for j in range(4)], n)

        def turn_targets(key):
            kind = key if isinstance(key, str) else key[0]
            b = bank(key)
            if kind == "vec":
                return vec[:, :], ps[:, b, 0:VROWS]
            if kind == "x":
                return h3[:, key[1], :], ps[:, b, 0:T]
            if kind == "mem":
                return memw[:, key[1], :], ps[:, b, 0:NP_]
            if kind == "conv":
                return None, None
            if isinstance(kind, tuple):
                u, c, w = key
                buf = (xKT if u[0] == "MK" else KT_)[:, STEP[(u, c)] % 2, 2 * w:2 * w + 2, :]
                return buf, ps[:, b, :].rearrange("p (b t) -> p b t", b=2)
            if kind in ("ktok", "mktok"):
                n = TOKS[key[1]][1]
                return (stage if kind == "ktok" else mstage)[0:n, key[1] % 2, :], ps[0:n, b, :]
            if kind in ("vtok", "mvtok"):
                n = TOKS[key[1]][1]
                return (vtok if kind == "vtok" else memvtok)[0:n, key[1], :], ps[0:n, b, :]
            if kind == "own":
                return own_raw[:, :], ps[:, b, 0:NS]
            if kind == "probs":
                s, j = key[1:]
                if s >= 2:
                    return xPT[:, :, :].rearrange("p c t -> p (c t)"), ps[:, b, 0:256]
                if j == 2:
                    return PT[0:NS, 8, :], ps[0:NS, b, 0:P]
                return PT[:, 4 * j:4 * j + 4, :].rearrange("p c t -> p (c t)"), ps[:, b, :]
            if kind == "ohead":
                return ohT[:, :], ps[:, b, :]
            if kind == "cvout":
                return cvo[:, key[1] * 512:(key[1] + 1) * 512], ps[0:27, b, :]
            if kind == "dt":
                n = TOKS[key[1]][1]
                return dtok[0:n, :], ps[0:n, b, 0:32]
            if kind == "xtok":
                n = TOKS[key[1]][1]
                return xtok[0:n, key[2] * 512:(key[2] + 1) * 512], ps[0:n, b, :]
            if kind == "btok":
                n = TOKS[key[1]][1]
                return btok[0:n, :], ps[0:n, b, 0:256]
            if kind == "y":
                return ybuf[:, key[2] % 2, :], ps[:, b, 0:256]
            if kind == "st":
                return (st0, st1)[key[1]][:, key[2] * 512:(key[2] + 1) * 512], ps[:, b, :]
            if kind == "yd":
                return ysb[:, key[1] * 512:(key[1] + 1) * 512], ps[0:NS, b, :]
            if kind == "ss" and len(key) == 4:
                return ssT[(4 * key[1] + 2 * key[2] + key[3]) % 4], ps[:, b, :]
            if kind == "ys":
                return ybuf[:, 0, :], ps[:, b, 0:256]
            if kind == "sf":
                return sfo[:, key[1] * 512:(key[1] + 1) * 512], ps[:, b, :]
            if kind == "pt":
                return PTp[:, key[2] % 2, :, :].rearrange("p m q -> p (m q)"), ps[:, b, :]
            if kind == "pv":
                x = key[2]
                if key[1] == "cross":
                    return attT[:, x, 0:NP_], ps[:, b, 0:NP_]
                r = slice(64 * (x % 2), 64 * (x % 2) + 64)
                return attT[r, x // 2, 0:NP_], ps[r, b, 0:NP_]
            if kind == "fin":
                n = TOKS[key[1]][1]
                return ytok[0:n, key[1] % 2, key[2] * 512:(key[2] + 1) * 512], ps[0:n, b, :]
            raise KeyError(key)

        def target_free(e, key):
            kind = key if isinstance(key, str) else key[0]
            if isinstance(kind, tuple):
                step = STEP[(key[0], key[1])]
                if step >= 2:
                    e.wait_ge(kt_used, step - 1)
            elif kind == "ktok" and key[1] == 2:
                e.wait_ge(kst_out[0], 16)
            elif kind == "probs" and key[1] in (1, 3):
                e.wait_ge(pv_out, key[1])
            elif kind == "own" and key[1] == 1:
                e.wait_ge(scores_used, 1)
            elif kind == "ohead" and key[1]:
                e.wait_ge(heads_out, key[1])
            elif kind in ("dt", "xtok", "btok") and key[1]:
                in_ps(e, ("st", key[1] - 1, 1))
            elif kind == "y" and 4 * key[1] + key[2] >= 2:
                e.wait_ge(y_used, 4 * key[1] + key[2] - 1)
            elif kind == "st" and key[1] == 0:
                e.wait_ge(cv_out, 32)
            elif kind == "ss" and len(key) == 4:
                k = 4 * key[1] + 2 * key[2] + key[3]
                if k >= 4:
                    e.wait_ge(ssT_used, k - 3)
                elif k == 0 or k == 1:
                    in_ps(e, ("st", 1, 1))
                    e.wait_ge(mix_made, 8)
            elif kind == "ys":
                e.wait_ge(y_used, 8)
            elif kind == "pt" and key[2] >= 2:
                in_ps(e, ("pv", key[1], key[2] - 2))
            elif kind == "fin" and key[1] == 2:
                e.wait_ge(fin_out, 1)

        @block.scalar
        def _(act):
            n_step = [0]

            def step(ins):
                n_step[0] += 1
                ins.then_inc(act_step, 1)
                act.wait_ge(act_step, n_step[0])

            def leave(key):
                if TURN[key] % 2:
                    return
                in_ps(act, key)
                target_free(act, key)
                if key == "conv":
                    act.wait_ge(zeros_made, 5)
                    hist = ps[:, bank(key), 0:XT * 24].rearrange("p (c b r) -> p c b r", c=XT, b=NB)
                    for b in range(NB):
                        last = act.activation(xpad[:, :, XS + 7 * b:XS + 7 * b + 3], hist[:, :, b, :], ACT.Copy)
                    last.then_inc(turn_act, 1)
                    return
                if key[0] == "ss" and len(key) == 2:
                    n = NP_ if key[1] == 1 else T
                    if key[1]:
                        act.wait_ge(root_done, key[1])
                    act.activation(vv[:, 0:n], ps[:, bank(key), 0:n], ACT.Copy, scale=1.0 / D).then_inc(turn_act, 1)
                    return
                dst, src = turn_targets(key)
                act.activation(dst, src, ACT.Copy).then_inc(turn_act, 1)

            def square(k, c, src, n):
                m = 8 * k + c
                if m >= 2:
                    act.wait_ge(acc_done, m - 1)
                act.activation(sq[:, m % 2, 0:n], src, ACT.Square).then_inc(sq_done, 1)

            leave("vec")
            for c in range(DT):
                leave(("x", c))
                turned(act, ("x", c))
                square(0, c, h3[:, c, :], T)
            def row_exps(s):
                act.wait_ge(bounds_made, s + 1)
                if s < 2:
                    for k in range(5):
                        lo, hi = (256 * k, 256 * k + 256) if k < 4 else (PAST, PAST + NS)
                        last = act.activation(logit[:, lo:hi], logit[:, lo:hi], ACT.Exp, bias=sm(s, 14 + k, 15 + k),
                                              accum_out=sm(s, 19 + k, 20 + k))
                else:
                    act.activation(logit_x[:, s % 2, :], ps[:, s - 2, 0:256], ACT.Exp, bias=sm(s, 14, 15),
                                   scale=P ** -0.5, accum_out=sm(s, 19, 20)).then_inc(scores_used, 1)
                    act.wait_ge(scores_used, s + 1)
                    last = act.activation(sm(s, 20, 21), sm(s, 19, 20), ACT.Copy)
                last.then_inc(row_exp, 1)

            def head_exps(kind, x):
                cross = kind == "cross"
                act.wait_ge(p_bound, HEAD0[kind] + x + 1)
                for q in range(2):
                    src = ps[:, 4 + x % 2, q * 256:(q + 1) * 256] if cross else PL[:, x % 2, q, :]
                    last = act.activation(PL[:, x % 2, q, :], src, ACT.Exp, bias=mx[:, x % 2, 2 + q:3 + q],
                                          scale=P ** -0.5 if cross else 1.0,
                                          accum_out=mx[:, x % 2, 4 + q:5 + q])
                last.then_inc(p_exp, 1)

            def ssd():
                act.activation(z[:, :, :], z[:, :, :], ACT.Silu).then_inc(z_silu, 1)
                for i in range(3):
                    leave(("cvout", i))
                act.wait_ge(dec_ps, 1)
                cols = ps[:, 4, 320:392].rearrange("p (c b) -> p c b", b=9)
                act.activation(dec[:, :, 0:NB], cols[:, :, 0:NB], ACT.Exp)
                act.activation(dec[:, :, NB:NB + 1], cols[:, :, NB:NB + 1], ACT.Copy).then_inc(dec_exp, 1)
                for q in range(3):
                    off, n = TOKS[q]
                    leave(("dt", q))
                    leave(("xtok", q, 0)), leave(("xtok", q, 1)), leave(("btok", q))
                    act.wait_ge(sums_ps, q + 1)
                    if q:
                        act.wait_ge(xw_made, q)
                        if q == 2:
                            act.wait_ge(state_made, 1)
                    act.activation(ex[0:n, :], ps[0:n, 4, 256:304], ACT.Exp).then_inc(sums_exp, 1)
                    if q == 2:
                        act.wait_ge(seg_ps, 9)
                        act.wait_ge(mix_made, 8)
                        act.activation(E4[0:NS, 0, :], ps[0:NS, 0, :], ACT.Exp).then_inc(seg_exp, 1)
                        for k in range(16):
                            leave(("ss", k // 4, k // 2 % 2, k % 2))
                        leave(("yd", 0)), leave(("yd", 1)), leave("ys")
                        continue

                    def exps(hg):
                        k = 4 * q + hg
                        act.wait_ge(seg_ps, k + 1)
                        if k >= 2:
                            act.wait_ge(mix_made, k - 1)
                        act.activation(E4[:, hg % 2, :], ps[:, hg % 2, :], ACT.Exp).then_inc(seg_exp, 1)
                        if q == 1:
                            act.wait_ge(acb_ps, hg + 1)
                            if hg >= 2:
                                in_ps(act, ("y", 1, hg - 2))
                            act.activation(CS[:, hg % 2, :], ps[:, 5, :], ACT.Exp).then_inc(acb_exp, 1)

                    exps(0)
                    for hg in range(4):
                        if hg < 3:
                            exps(hg + 1)
                        leave(("y", q, hg))
                    leave(("st", q, 0)), leave(("st", q, 1))
                act.wait_ge(z_ready, 1)
                for c in range(DT):
                    square(2, c, z[:, c, :], T)
                leave(("sf", 0)), leave(("sf", 1))

            for s in SEQ:
                if s[0] == "unit" and s[1] in ("K", "MK"):
                    for c in range(4):
                        leave((s[1:], c, 0)), leave((s[1:], c, 1))
                elif s[0] == "ss":
                    leave(s)
                    k, n = s[1], NP_ if s[1] == 1 else T
                    turned(act, s)
                    if k:
                        act.wait_ge(rstd_done, k)
                    act.activation(rstd[:, 0:n] if k != 1 else rmem[:, :], vv[:, 0:n], ACT.Sqrt, bias=eps_t[:, 0:1])\
                        .then_inc(root_done, 1)
                elif s[0] in ("kvtok", "mtok"):
                    for g in range(3 if s[0] == "kvtok" else 2):
                        for name in (("ktok", "vtok") if s[0] == "kvtok" else ("mktok", "mvtok")):
                            leave((name, g))
                elif s[0] == "early":
                    for c in range(DT):
                        leave(("mem", c))
                        turned(act, ("mem", c))
                        square(1, c, memw[:, c, :], NP_)
                    leave("conv")
                    act.wait_ge(const_in, 16 * 12)
                    act.activation(hcol[:, 3:4], hcol[:, 1:2], ACT.Exp).then_inc(alog_exp, 1)
                elif s[0] == "own":
                    leave(s)
                    row_exps(s[1])
                elif s[0] == "heads_in":
                    head_exps(s[1], 0), head_exps(s[1], 1)
                elif s[0] == "head":
                    kind, x = s[1:]
                    if x:
                        leave(("pv", kind, x - 1))
                    leave(("pt", kind, x))
                    if x + 2 < N_HEADS[kind]:
                        head_exps(kind, x + 2)
                elif s[0] == "heads_end":
                    leave(("pv", s[1], N_HEADS[s[1]] - 1))
                elif s[0] == "meet":
                    meet(act, 2)
                elif s[0] == "silu_x":
                    for c in range(XT):
                        act.wait_ge(conv_done, c + 1)
                    act.activation(xc[:, :, :], xc[:, :, :], ACT.Silu).then_inc(silu_done, 1)
                elif s[0] == "dt":
                    act.wait_ge(dt_abs, 1)
                    act.activation(dts[3], dts[2], ACT.Exp, scale=-1.0).then_inc(dt_exp, 1)
                elif s[0] == "probs":
                    if s[1] >= 2:
                        row_exps(s[1])
                    for j in range(3 if s[1] < 2 else 1):
                        leave(s + (j,))
                elif s[0] == "pvend":
                    leave(("ohead", s[1]))
                elif s[0] == "ssd":
                    meet(act, 1)
                    ssd()
                elif s[0] == "pair" and s[1] in ("out", "cao"):
                    for h in range(2):
                        act.wait_ge(dense_out, TILE[s[1:3] + (h,)] + 1)
                        square(3 if s[1] == "out" else 4, 2 * s[2] + h, h3[:, 2 * s[2] + h, :], T)
            with act.Fori(0, FT) as i:
                act.wait_ge(dense_out, i + (UP0 + 1))
                act.activation(ff[:, ds(i * T, T)], ff[:, ds(i * T, T)], ACT.Square).then_inc(ff_done, 1)
            for g in range(3):
                n = TOKS[g][1]
                leave(("fin", g, 0)), leave(("fin", g, 1))
                turned(act, ("fin", g, 0)), turned(act, ("fin", g, 1))
                if g == 2:
                    act.wait_ge(y0_out, 16)
                step(act.activation(yout[0:n, g % 2, :], ytok[0:n, g % 2, :], ACT.Square,
                                    accum_out=mx[0:n, 0, g:g + 1]))
                act.activation(mx[0:n, 1, g:g + 1], mx[0:n, 0, g:g + 1], ACT.Sqrt, bias=eps_t[0:n, 0:1],
                               scale=1.0 / D).then_inc(fin_root, 1)

        @block.vector
        def _(dve):
            n_step = [0]

            def step(ins):
                n_step[0] += 1
                ins.then_inc(dve_step, 1)
                dve.wait_ge(dve_step, n_step[0])

            def leave(key):
                if TURN[key] % 2 == 0:
                    return
                in_ps(dve, key)
                target_free(dve, key)
                if key == "conv":
                    dve.wait_ge(zeros_made, 5)
                    hist = ps[:, bank(key), 0:XT * 24].rearrange("p (c b r) -> p c b r", c=XT, b=NB)
                    for b in range(NB):
                        last = dve.tensor_copy(xpad[:, :, XS + 7 * b:XS + 7 * b + 3], hist[:, :, b, :])
                    last.then_inc(turn_dve, 1)
                    return
                if key[0] == "ss" and len(key) == 2:
                    n = NP_ if key[1] == 1 else T
                    if key[1]:
                        dve.wait_ge(root_done, key[1])
                    dve.tensor_scalar(vv[:, 0:n], ps[:, bank(key), 0:n], 1.0 / D, None, ALU.mult).then_inc(turn_dve, 1)
                    return
                dst, src = turn_targets(key)
                dve.tensor_copy(dst, src).then_inc(turn_dve, 1)

            def scale_tile(dst, src, name, c, signal):
                dve.tensor_scalar(dst, src, vec[:, VEC[name] + c:VEC[name] + c + 1], None, ALU.mult).then_inc(signal, 1)

            def tile_out(kind, n, half):
                t, c = TILE[(kind, n, half)], 2 * n + half
                b = t % 2
                dve.wait_ge(dense_ps, t + 1)
                rs = rstd
                if kind == "qk" and c < 4:
                    sides = ((0, slice(0, 64)), (1, slice(64, 128)))
                    for side, r in sides:
                        dve.tensor_tensor(qz[r, side, c, :], ps[r, b, 0:NP_], rs[r, 0:NP_], ALU.mult)
                    for side, r in sides:
                        h = 2 * c + side
                        last = dve.tensor_tensor(
                            qs[r, c, :, h * NI:h * NI + NI], ps[r, b, NP_:T].rearrange("p (b i) -> p b i", b=NB),
                            rs[r, NP_:T].rearrange("p (b i) -> p b i", b=NB), ALU.mult)
                    last.then_inc(dense_out, 1)
                elif kind == "qk":
                    dve.tensor_tensor(kT[:, c - 4, :], ps[:, b, 0:T], rs[:, :], ALU.mult).then_inc(dense_out, 1)
                elif kind == "v":
                    dve.tensor_tensor(vT[:, c, :], ps[:, b, 0:T], rs[:, :], ALU.mult).then_inc(dense_out, 1)
                elif kind == "z":
                    if c == 0:
                        for done in kst_out[3:]:
                            dve.wait_ge(done, 16)
                    dve.tensor_tensor(z[:, c, :], ps[:, b, 0:T], rs[:, :], ALU.mult).then_inc(dense_out, 1)
                elif kind == "m":
                    if c == 4:
                        turned(dve, ("vtok", 2))
                    dst = memkT[:, c, :] if c < 4 else vT[:, c - 4, 0:NP_]
                    dve.tensor_tensor(dst, ps[:, b, 0:NP_], rmem[:, :], ALU.mult).then_inc(dense_out, 1)
                elif kind == "x":
                    dve.tensor_tensor(xpad[:, c, CW - 1:XS], ps[:, b, 0:NP_], rs[:, 0:NP_], ALU.mult)
                    dve.tensor_tensor(xpad[:, c, XS:XPAD].rearrange("p (b r) -> p b r", b=NB)[:, :, CW - 1:],
                                      ps[:, b, NP_:T].rearrange("p (b i) -> p b i", b=NB),
                                      rs[:, NP_:T].rearrange("p (b i) -> p b i", b=NB), ALU.mult).then_inc(dense_out, 1)
                    dve.wait_ge(dense_out, t + 1)
                    conv(c)
                elif kind == "caq":
                    if c == 0:
                        dve.wait_ge(qs_clear, 1)
                    dve.tensor_tensor(qz[:, 0, c, :], ps[:, b, 0:NP_], rs[:, 0:NP_], ALU.mult)
                    dve.tensor_tensor(qs[:, c, :, c * NI:c * NI + NI],
                                      ps[:, b, NP_:T].rearrange("p (b i) -> p b i", b=NB),
                                      rs[:, NP_:T].rearrange("p (b i) -> p b i", b=NB), ALU.mult).then_inc(dense_out, 1)
                else:
                    if kind == "out":
                        step(dve.tensor_tensor(zpart, ps[:, b, 0:T], rs[:, :], ALU.mult))
                        step(dve.tensor_tensor(h3[:, c, :], h3[:, c, :], zpart, ALU.add))
                        b += 4
                    dve.tensor_tensor(h3[:, c, :], h3[:, c, :], ps[:, b, 0:T], ALU.add).then_inc(dense_out, 1)
                    dve.wait_ge(dense_out, t + 1)
                    scale_tile(hw[:, c, :], h3[:, c, :], "norm_ca" if kind == "out" else "norm_mlp", c, hw_done)

            def conv(c):
                n = XPAD - CW + 1
                if c == 0:
                    for done in kst_out[:3]:
                        dve.wait_ge(done, 16)
                w = [vec[:, VEC["conv_w"] + k * XT + c:VEC["conv_w"] + k * XT + c + 1] for k in range(CW)]
                y = ctmp[:, 0:n]
                step(dve.tensor_scalar(y, xpad[:, c, 0:n], w[0], vec[:, VEC["conv_b"] + c:VEC["conv_b"] + c + 1],
                                       ALU.mult, ALU.add))
                for k in (1, 2):
                    step(dve.scalar_tensor_tensor(y, xpad[:, c, k:k + n], w[k], y, ALU.mult, ALU.add))
                dve.scalar_tensor_tensor(xc[:, c, 0:NP_], xpad[:, c, 3:3 + NP_], w[3], y[:, 0:NP_], ALU.mult, ALU.add)
                yb = ctmp[:, XS:XPAD].rearrange("p (b r) -> p b r", b=NB)[:, :, 0:NI]
                xb = xpad[:, c, XS:XPAD].rearrange("p (b r) -> p b r", b=NB)[:, :, CW - 1:]
                dve.scalar_tensor_tensor(xc[:, c, NP_:T].rearrange("p (b i) -> p b i", b=NB), xb, w[3], yb,
                                         ALU.mult, ALU.add).then_inc(conv_done, 1)

            def invert(k):
                dve.wait_ge(root_done, k + 1)
                a = rmem[:, :] if k == 1 else rstd[:, :]
                dve.reciprocal(a, a).then_inc(rstd_done, 1)
                dve.wait_ge(rstd_done, k + 1)

            def self_bounds(g):
                scale = DH ** -0.5
                dve.wait_ge(kt_used, 16 * (g + 1))
                turned(dve, ("own", g))
                if g:
                    in_ps(dve, ("probs", g - 1, 2))
                sc = ps[:, 4:6, :].rearrange("p a (b n) -> p (a b) n", b=2)
                dve.tensor_reduce(sm(g, 0, 4), sc, AX.X, ALU.add)
                dve.scalar_tensor_tensor(logit[:, 0:512], ps[:, 4, :], scale, biasS[:, 0:512], ALU.mult, ALU.add)
                dve.scalar_tensor_tensor(logit[:, 512:PAST], ps[:, 5, :], scale, biasS[:, 512:PAST], ALU.mult, ALU.add)\
                    .then_inc(scores_used, 1)
                step(dve.scalar_tensor_tensor(logit[:, PAST:], own_raw[:, :], scale, biasS[:, PAST:], ALU.mult, ALU.add))
                dve.tensor_tensor(logit[:, PAST:], logit[:, PAST:], mask_own[:, g * NS:(g + 1) * NS], ALU.add)
                step(dve.tensor_reduce(sm(g, 13, 14), sm(g, 0, 4), AX.X, ALU.min))
                step(dve.tensor_scalar(sm(g, 4, 8), sm(g, 0, 4), sm(g, 13, 14), None, ALU.is_equal))
                step(dve.tensor_tensor(sm(g, 4, 8), sm(g, 4, 8), place[:, :], ALU.mult))
                step(dve.tensor_reduce(sm(g, 13, 14), sm(g, 4, 8), AX.X, ALU.max))
                step(dve.tensor_scalar(sm(g, 4, 8), sm(g, 4, 8), sm(g, 13, 14), NEG, ALU.is_equal, ALU.mult))
                dve.tensor_reduce(sm(g, 8, 12), logit[:, 0:PAST].rearrange("p (b n) -> p b n", b=4), AX.X, ALU.max)
                step(dve.tensor_reduce(sm(g, 12, 13), logit[:, PAST:], AX.X, ALU.max))
                step(dve.tensor_tensor(sm(g, 8, 12), sm(g, 8, 12), sm(g, 4, 8), ALU.add))
                step(dve.tensor_reduce(sm(g, 13, 14), sm(g, 8, 13), AX.X, ALU.max))
                dve.tensor_scalar(sm(g, 14, 18), sm(g, 4, 8), sm(g, 13, 14), None, ALU.subtract)
                dve.tensor_scalar(sm(g, 18, 19), sm(g, 13, 14), -1.0, None, ALU.mult).then_inc(bounds_made, 1)
                dve.wait_ge(scores_used, g + 1)

            def cross_bounds(g):
                s = 2 + g
                dve.wait_ge(kt_used, 32 + 4 * (g + 1))
                step(dve.tensor_reduce(sm(s, 13, 14), ps[:, g, 0:256], AX.X, ALU.max))
                dve.tensor_scalar(sm(s, 14, 15), sm(s, 13, 14), -(P ** -0.5), None, ALU.mult).then_inc(bounds_made, 1)

            def take_result(s):
                dve.wait_ge(row_exp, s + 1)
                step(dve.tensor_reduce(sm(s, 8, 9), sm(s, 19, 24 if s < 2 else 20), AX.X, ALU.add))
                step(dve.reciprocal(sm(s, 9, 10), sm(s, 8, 9)))
                if s < 2:
                    dve.wait_ge(pv_ps, s + 1)
                else:
                    dve.wait_ge(v_used, 8 + s - 2 + 1)
                dve.tensor_scalar((osb if s < 2 else xosb), ps[:, 7, :], sm(s, 9, 10), None, ALU.mult).then_inc(pv_out, 1)

            def dt_rates():
                t = TILE["dt"]
                dve.wait_ge(dense_ps, t + 1)
                in_ps(dve, ("probs", 1, 2))
                d = dts
                dve.tensor_tensor(d[0], ps[0:SH, t % 2, 0:T], rstd[0:SH, :], ALU.mult).then_inc(dense_out, 1)
                dve.wait_ge(dense_out, t + 1)
                dve.wait_ge(const_in, 16 * 12)
                step(dve.tensor_scalar(d[1], d[0], hcol[:, 0:1], None, ALU.add))
                dve.scalar_tensor_tensor(d[2], d[1], -1.0, d[1], ALU.mult, ALU.max).then_inc(dt_abs, 1)
                dve.wait_ge(dt_exp, 1)
                step(dve.tensor_scalar(d[4], d[3], 2.0, None, ALU.add))
                step(dve.reciprocal(d[5], d[4]))
                step(dve.tensor_tensor(d[4], d[3], d[5], ALU.mult))
                step(dve.tensor_tensor(d[5], d[4], d[4], ALU.mult))
                step(dve.tensor_scalar(d[3], d[5], 1.0 / 15, None, ALU.mult))
                for k in (13, 11, 9, 7, 5, 3):
                    step(dve.scalar_tensor_tensor(d[3], d[3], 1.0 / k, d[5], ALU.add, ALU.mult))
                step(dve.scalar_tensor_tensor(d[3], d[3], 1.0, d[4], ALU.add, ALU.mult))
                step(dve.tensor_scalar(d[1], d[1], 0.0, None, ALU.max))
                step(dve.scalar_tensor_tensor(d[0], d[3], 2.0, d[1], ALU.mult, ALU.add))
                dve.wait_ge(alog_exp, 1)
                step(dve.tensor_scalar(d[1], d[0], hcol[:, 3:4], -1.0, ALU.mult, ALU.mult))
                dve.tensor_reduce(sums[:, 0:NB], d[1][:, NP_:T].rearrange("p (b i) -> p b i", b=NB), AX.X, ALU.add)
                step(dve.tensor_copy(sums[:, NB:NB + 1], hcol[:, 2:3]))
                dve.tensor_tensor(psums[:, :, :], spread(sums[:, :], [SH, DT, NB + 1], 1),
                                  spread(pair_of[:, :], [SH, DT, NB + 1], 2), ALU.mult).then_inc(dt_done, 1)

            def heads(ap, n_heads, width):
                return ap.rearrange("p (h w) -> p h w", h=n_heads)

            def spread(col, shape, axis):
                return col.unsqueeze(axis).broadcast_to(shape)

            def ssd():
                for i in range(3):
                    leave(("cvout", i))
                dve.wait_ge(silu_done, 1)
                for q in range(3):
                    off, n = TOKS[q]
                    upt = (upto, upto_s)[q == 2]
                    if q == 2:
                        state()
                        dve.wait_ge(seg_ps, 8)
                        dve.wait_ge(acb_ps, 4)
                    leave(("dt", q))
                    turned(dve, ("dt", q))

                    def rhs(hg):
                        if 4 * q + hg >= 2:
                            dve.wait_ge(seg_ps, 4 * q + hg - 1)
                        if q == 1 and hg >= 2:
                            dve.wait_ge(acb_ps, hg - 1)
                        dve.tensor_tensor(heads(rhs4[:, hg % 2, :], 4, P), spread(upto[:, :], [P, 4, P], 1),
                                          spread(dtok[:, 16 + 4 * hg:20 + 4 * hg], [P, 4, P], 2), ALU.mult)\
                            .then_inc(rhs_made, 1)

                    if q < 2:
                        rhs(0)
                        rhs(1)
                    else:
                        dve.tensor_tensor(heads(rhs4[0:n, 0, :], SH, n), spread(upto_s[:, :], [n, SH, n], 1),
                                          spread(dtok[0:n, 16:32], [n, SH, n], 2), ALU.mult).then_inc(rhs_made, 1)
                    leave(("xtok", q, 0)), leave(("xtok", q, 1)), leave(("btok", q))
                    turned(dve, ("xtok", q, 0)), turned(dve, ("xtok", q, 1)), turned(dve, ("btok", q))
                    xh, wh = heads(xtok[0:n, :], SH, 64), heads(xwt[0:n, :], SH, 64)
                    step(dve.tensor_tensor(xh, xh, spread(dtok[0:n, 0:16], [n, SH, 64], 2), ALU.mult))
                    dve.wait_ge(sums_exp, q + 1)
                    if q == 2:
                        dve.wait_ge(xw_clear, 1)
                    dve.tensor_tensor(wh, xh, spread(ex[0:n, 0:16], [n, SH, 64], 2), ALU.mult).then_inc(xw_made, 1)
                    dve.wait_ge(g_ps, q + 1)
                    dve.tensor_tensor(heads(Gm[0:n, :], 2, P)[:, :, 0:n], heads(ps[0:n, 5, 0:256], 2, P)[:, :, 0:n],
                                      spread(upt[0:n, 0:n], [n, 2, n], 1), ALU.mult).then_inc(gm_made, 1)
                    dve.wait_ge(gm_made, q + 1)
                    if q == 2:
                        ssd_sample()
                        break

                    def mix(hg):
                        k = 4 * q + hg
                        dve.wait_ge(seg_exp, k + 1)
                        if k >= 2:
                            in_ps(dve, ("y",) + divmod(k - 2, 4))
                        dve.tensor_tensor(heads(M4[:, hg % 2, :], 4, P), heads(E4[:, hg % 2, :], 4, P),
                                          spread(Gm[:, (hg // 2) * P:(hg // 2) * P + P], [P, 4, P], 1), ALU.mult)\
                            .then_inc(mix_made, 1)
                        if q == 1:
                            dve.wait_ge(acb_exp, hg + 1)
                            c4 = heads(CS[:, hg % 2, :], 4, P)
                            dve.tensor_tensor(c4, c4, spread(xc[:, 10 + hg // 2, off:off + n], [P, 4, P], 1), ALU.mult)\
                                .then_inc(cs_made, 1)

                    def gate(hg):
                        turned(dve, ("y", q, hg))
                        if q == 0 and hg == 0:
                            dve.wait_ge(dec_exp, 1)
                            dve.wait_ge(z_silu, 1)
                        for j in range(2):
                            c = 2 * hg + j
                            y = ybuf[:, hg % 2, j * P:(j + 1) * P]
                            last = dve.scalar_tensor_tensor(y, xc[:, c, off:off + n], dec[:, c, NB:NB + 1], y,
                                                            ALU.mult, ALU.add)
                        step(last)
                        zz = z[:, 2 * hg:2 * hg + 2, off:off + n]
                        dve.tensor_tensor(zz, zz, heads(ybuf[:, hg % 2, :], 2, P), ALU.mult).then_inc(y_used, 1)

                    mix(0)
                    for hg in range(4):
                        if hg + 2 < 4:
                            rhs(hg + 2)
                        if hg < 3:
                            mix(hg + 1)
                        leave(("y", q, hg))
                        gate(hg)
                    leave(("st", q, 0)), leave(("st", q, 1))
                leave(("sf", 0)), leave(("sf", 1))

            def state():
                turned(dve, ("st", 1, 0)), turned(dve, ("st", 1, 1))
                in_ps(dve, ("st", 1, 1))
                s0 = heads(st0, SH, 64)
                step(dve.tensor_tensor(s0, s0, spread(ex[:, 16:32], [P, SH, 64], 2), ALU.mult))
                dve.tensor_tensor(st1, st0, st1, ALU.add).then_inc(state_made, 1)
                dve.wait_ge(state_made, 1)

            def ssd_sample():
                n = NS
                dve.wait_ge(cz_made, 1)
                for g in range(2):
                    last = dve.tensor_tensor(bbd[0:n, g], spread(btok[0:n, g * P:(g + 1) * P], [n, NB, P], 1),
                                             spread(batch_of[:, :], [n, NB, P], 2), ALU.mult)
                last.then_inc(bbd_made, 1)
                dve.wait_ge(seg_exp, 9)
                for g in range(2):
                    last = dve.tensor_tensor(heads(M4[0:n, 0, g * 256:(g + 1) * 256], 8, n),
                                             heads(E4[0:n, 0, g * 256:(g + 1) * 256], 8, n),
                                             spread(Gm[0:n, g * P:g * P + n], [n, 8, n], 1), ALU.mult)
                last.then_inc(mix_made, 1)
                for k in range(16):
                    leave(("ss", k // 4, k // 2 % 2, k % 2))
                leave(("yd", 0)), leave(("yd", 1))
                turned(dve, ("yd", 0)), turned(dve, ("yd", 1))
                dve.wait_ge(ssT_used, 16)
                for g in range(2):
                    step(dve.tensor_copy(yo[:, g * 512:(g + 1) * 512], ps[32 * g:32 * g + 32, 5, :]))
                    y = yo[:, g * 512:(g + 1) * 512]
                    step(dve.tensor_tensor(y, ps[64 + 32 * g:96 + 32 * g, 5, :], y, ALU.add))
                y3 = heads(yo, SH, 64)
                step(dve.tensor_tensor(y3, y3, spread(ex[0:n, 32:48], [n, SH, 64], 2), ALU.mult))
                dve.tensor_tensor(yo, yo, ysb, ALU.add).then_inc(ys_made, 1)
                leave("ys")
                turned(dve, "ys")
                for c in range(DT):
                    y = ybuf[:, 0, c * n:(c + 1) * n]
                    last = dve.scalar_tensor_tensor(y, xc[:, c, NP_:T], dec[:, c, NB:NB + 1], y, ALU.mult, ALU.add)
                step(last)
                dve.tensor_tensor(z[:, :, NP_:T], z[:, :, NP_:T], heads(ybuf[:, 0, :], DT, n), ALU.mult)\
                    .then_inc(z_ready, 1)
                for k in range(16):
                    c, bh = k // 2, k % 2
                    dve.wait_ge(up_ps, k + 1)
                    st = kvring[:, UNIT[("ST", bh)] % 2].rearrange("p b a (c n) -> p b (a c) n", n=SN)
                    for b in range(GB):
                        last = dve.scalar_tensor_tensor(st[:, b, c, :], st[:, b, c, :],
                                                        dec[:, c, GB * bh + b:GB * bh + b + 1],
                                                        ps[:, k % 2, b * P:(b + 1) * P], ALU.mult, ALU.add)
                    last.then_inc(up_done, 1)
                for c in range(DT):
                    dve.wait_ge(sq_done, 16 + c + 1)
                    scale_tile(z[:, c, :], z[:, c, :], "ssd_norm", c, z_scaled)

            def head_bound(kind, x):
                cross = kind == "cross"
                dve.wait_ge(p_scores, HEAD0[kind] + x + 1)
                sc = ps[:, 4 + x % 2, :].rearrange("p (q k) -> p q k", q=2)
                m = mx[:, x % 2, :]
                if x >= 2:
                    in_ps(dve, ("pt", kind, x - 2))
                if cross:
                    step(dve.tensor_reduce(m[:, 0:2], sc, AX.X, ALU.max))
                    dve.tensor_scalar(m[:, 2:4], m[:, 0:2], -(P ** -0.5), None, ALU.mult).then_inc(p_bound, 1)
                else:
                    dve.wait_ge(bias_in[x % 2], 32 * (x // 2 + 1))
                    step(dve.scalar_tensor_tensor(PL[:, x % 2], sc, DH ** -0.5, biasP[:, x % 2, :, ::-1],
                                                  ALU.mult, ALU.add))
                    step(dve.tensor_reduce(m[:, 0:2], PL[:, x % 2], AX.X, ALU.max))
                    dve.tensor_scalar(m[:, 2:4], m[:, 0:2], -1.0, None, ALU.mult).then_inc(p_bound, 1)

            def head_norm(kind, x):
                dve.wait_ge(p_exp, HEAD0[kind] + x + 1)
                m = mx[:, x % 2, :]
                step(dve.reciprocal(m[:, 6:8], m[:, 4:6]))
                dve.tensor_tensor(PL[:, x % 2], PL[:, x % 2], spread(m[:, 6:8], [P, 2, 256], 2), ALU.mult)\
                    .then_inc(p_probs, 1)

            dve.wait_ge(tab_in, 16 * 6)
            dve.tensor_tensor(rbx.rearrange("p (b h i) -> p b h i", b=GB, h=H),
                              rb4[:, :].unsqueeze(1).unsqueeze(3).broadcast_to([P, GB, H, NI]),
                              step_of[:, :].unsqueeze(1).unsqueeze(1).broadcast_to([P, GB, H, NI]), ALU.mult)\
                .then_inc(rbx_made, 1)
            leave("vec")
            turned(dve, "vec")
            for c in range(DT):
                leave(("x", c))
                turned(dve, ("x", c))
                scale_tile(hw[:, c, :], h3[:, c, :], "norm_mix", c, hw_done)
            dve.wait_ge(tab_ps, 1)
            dve.tensor_copy(biasS[:, 0:PAST].rearrange("p (a n) -> p a n", a=2), ps[:, 4:6, :]).then_inc(tab_made, 1)
            dve.tensor_copy(biasS[:, PAST:], ps[:, 0, 0:NS]).then_inc(tab_made, 1)
            dve.tensor_tensor(rb_row, ps[0:H, 1, :], mask_p, ALU.add).then_inc(tab_made, 1)
            dve.wait_ge(tab_made, 3)
            pending = []
            for i, s in enumerate(SEQ):
                if s[0] == "pair":
                    if s[1] in ("qk", "caq") and SEQ[i + 1][0] == "ss":
                        pending = [s]
                        continue
                    tile_out(*s[1:3], 0), tile_out(*s[1:3], 1)
                elif s[0] == "ss":
                    leave(s)
                    invert(s[1])
                    for p in pending:
                        tile_out(*p[1:3], 0), tile_out(*p[1:3], 1)
                    pending = []
                elif s[0] == "unit" and s[1] in ("K", "MK"):
                    for c in range(4):
                        leave((s[1:], c, 0)), leave((s[1:], c, 1))
                    if s[1] == "MK":
                        cross_bounds(s[2])
                elif s[0] in ("kvtok", "mtok"):
                    for g in range(3 if s[0] == "kvtok" else 2):
                        for name in (("ktok", "vtok") if s[0] == "kvtok" else ("mktok", "mvtok")):
                            leave((name, g))
                elif s[0] == "early":
                    for c in range(DT):
                        leave(("mem", c))
                        turned(dve, ("mem", c))
                        dve.wait_ge(sq_done, 8 + c + 1)
                        scale_tile(memw[:, c, :], memw[:, c, :], "norm_mem", c, memw_done)
                    leave("conv")
                    dve.wait_ge(const_in, 16 * 12)
                    dve.wait_ge(zeros_made, 5)
                    turned(dve, "conv")
                elif s[0] == "heads_in":
                    if s[1] == "self":
                        in_ps(dve, ("mvtok", 1))
                    head_bound(s[1], 0), head_bound(s[1], 1)
                    head_norm(s[1], 0)
                elif s[0] == "head":
                    kind, x = s[1:]
                    if x:
                        leave(("pv", kind, x - 1))
                    leave(("pt", kind, x))
                    if x + 1 < N_HEADS[kind]:
                        head_norm(kind, x + 1)
                    if x + 2 < N_HEADS[kind]:
                        head_bound(kind, x + 2)
                elif s[0] == "heads_end":
                    leave(("pv", s[1], N_HEADS[s[1]] - 1))
                elif s[0] == "meet":
                    meet(dve, 2)
                elif s[0] == "own":
                    leave(s)
                    self_bounds(s[1])
                elif s[0] == "dt":
                    dt_rates()
                elif s[0] == "probs":
                    for j in range(3 if s[1] < 2 else 1):
                        leave(s + (j,))
                elif s[0] == "pvend":
                    take_result(s[1])
                    leave(("ohead", s[1]))
                elif s[0] == "ssd":
                    meet(dve, 1)
                    ssd()
            with dve.Fori(0, FT // 2) as i:
                for b in range(2):
                    dve.wait_ge(dense_ps, i * 2 + (UP0 + b + 1))
                    dve.scalar_tensor_tensor(ff[:, ds(i * (2 * T) + b * T, T)], ps[:, (UP0 + b) % 2, 0:T], 0.0, rstd[:, :],
                                             ALU.max, ALU.mult).then_inc(dense_out, 1)
            with dve.Fori(0, DT // 2) as i:
                for b in range(2):
                    dve.wait_ge(dense_ps, i * 2 + (DOWN0 + b + 1))
                    h = hT[:, ds(i * (2 * T) + b * T, T)]
                    dve.tensor_tensor(h, h, ps[:, (DOWN0 + b) % 2, 0:T], ALU.add).then_inc(dense_out, 1)
            dve.wait_ge(fnorm_in, 16)
            for g in range(3):
                n = TOKS[g][1]
                leave(("fin", g, 0)), leave(("fin", g, 1))
                dve.wait_ge(fin_root, g + 1)
                step(dve.reciprocal(mx[0:n, 1, 4 + g:5 + g], mx[0:n, 1, g:g + 1]))
                dve.scalar_tensor_tensor(yout[0:n, g % 2, :], ytok[0:n, g % 2, :], mx[0:n, 1, 4 + g:5 + g],
                                         fnorm[0:n, :], ALU.mult, ALU.mult).then_inc(fin_out, 1)


_FLAT = {"x_prompt": (NP_, D), "x_sample": (NS, D), "cache_k": (-1, PAGE, 512), "cache_v": (-1, PAGE, 512),
         "cache_mem_k": (NB, MEM, 512), "cache_mem_v": (NB, MEM, 512), "state_conv": (NB * 3, XT * P),
         "state_ssm": (NB, SH * SP_, SN), "page_table": (NB, NPAGE), "mem_prompt": (MEM, D), "norm_mix": (D,),
         "w_in": (D, -1), "conv_w": (-1,), "conv_b": (-1,), "dt_bias": (SH,), "a_log": (SH,), "d_skip": (SH,),
         "ssd_norm": (D,), "rel_bias": (BUCKETS, H), "w_out": (-1, D), "norm_ca": (D,), "norm_mem": (D,),
         "w_ca_q": (D, 512), "w_ca_kv": (D, 1024), "w_ca_o": (512, D), "norm_mlp": (D,), "w_up": (D, -1),
         "w_down": (-1, D), "norm_final": (D,)}
_OUTS = {"y_prompt": ((1, NP_, D), (NP_, D)), "y_sample": ((NB, NI, D), (NS, D)),
         "prompt_k": ((1, 1, NP_, H, DH), (NP_, 512)), "prompt_v": ((1, 1, NP_, H, DH), (NP_, 512)),
         "prompt_mem_k": ((1, 1, MEM, CROSS, P), (MEM, 512)), "prompt_mem_v": ((1, 1, MEM, CROSS, P), (MEM, 512)),
         "prompt_conv": ((1, 1, 3, XT * P), (3, XT * P)), "prompt_ssm": ((1, 1, SH, SP_, SN), (SH * SP_, SN)),
         "sample_k": ((1, NB, NI, H, DH), (NS, 512)), "sample_v": ((1, NB, NI, H, DH), (NS, 512)),
         "sample_conv": ((1, NB, 3, XT * P), (NB * 3, XT * P)),
         "sample_ssm": ((1, NB, SH, SP_, SN), (NB, SH * SP_, SN))}


def kernel(**inputs):
    import concourse.bacc as bacc
    from concourse.bass_utils import run_bass_kernel_spmd as run

    nc = bacc.Bacc("TRN2", target_bir_lowering=False, num_devices=1)
    arrays = {n: np.ascontiguousarray(inputs[n]).reshape(shape) for n, shape in _FLAT.items()}
    arrays.update(constants())
    ins = {n: nc.dram_tensor("in_" + n, a.shape, mybir.dt.from_np(a.dtype), kind="ExternalInput").ap()
           for n, a in arrays.items()}
    outs = {n: nc.dram_tensor("out_" + n, flat, F32, kind="ExternalOutput").ap() for n, (_, flat) in _OUTS.items()}
    scratch = nc.dram_tensor("bias_rows", (H, 512), F32, kind="Internal").ap()
    build(nc, ins, outs, scratch)
    r = run(nc, [{"in_" + n: a for n, a in arrays.items()}], core_ids=[0])
    return tuple(r.results[0]["out_" + n].reshape(shape) for n, (shape, _) in _OUTS.items())
```
